# Optimizing a Trainium2 kernel written in Bass

```python
import jax, jax.numpy as jnp
from jax import lax
import numpy as np

D_MODEL = 1024
BATCH = 1
SEQ = 512
DEPTH = 1

N_HEADS = 8
HEAD_DIM = 64
ATTN_WIDTH = N_HEADS * HEAD_DIM
KV_RANK = 128
IDX_HEADS = 8
IDX_DIM = 64
TOPK_MAX = 256
Q_BLOCK = 128
CHUNK = 128
GMLP_GROUPS = 4
GMLP_GROUP_DIM = 128
GMLP_WIDTH = GMLP_GROUPS * GMLP_GROUP_DIM
NUM_BUCKETS = 32
MAX_DISTANCE = 128
N_GROUPS = 4
EXPERTS_PER_GROUP = 8
N_EXPERTS = N_GROUPS * EXPERTS_PER_GROUP
TOP_K_INNER = 2
D_FF_EXPERT = 256
EPS = 1e-6
IN_SIZES = (ATTN_WIDTH, KV_RANK, IDX_HEADS * IDX_DIM, IDX_DIM, IDX_HEADS, GMLP_WIDTH, GMLP_WIDTH, D_MODEL, D_MODEL)
IN_COLS = ATTN_WIDTH + KV_RANK + IDX_HEADS * IDX_DIM + IDX_DIM + IDX_HEADS + 2 * GMLP_WIDTH + 2 * D_MODEL


def rms_norm(x, g):
    xf = x.astype(jnp.float32)
    y = xf * lax.rsqrt(jnp.mean(xf * xf, axis=-1, keepdims=True) + EPS)
    return y.astype(x.dtype) * g

def layer_norm(x, g, b):
    xf = x.astype(jnp.float32)
    mu = jnp.mean(xf, axis=-1, keepdims=True)
    var = jnp.mean(jnp.square(xf - mu), axis=-1, keepdims=True)
    return ((xf - mu) * lax.rsqrt(var + EPS)).astype(x.dtype) * g + b

def t5_bucket(n):
    max_exact = NUM_BUCKETS // 2
    nf = jnp.maximum(n, 1).astype(jnp.float32)
    large = max_exact + (jnp.log(nf / max_exact) / np.float32(np.log(MAX_DISTANCE / max_exact)) * (NUM_BUCKETS - max_exact)).astype(jnp.int32)
    large = jnp.minimum(large, NUM_BUCKETS - 1)
    return jnp.where(n < max_exact, n, large)

def sparse_attention(q_lat, q_idx, w_idx, c_kv, k_idx, rel_bias):
    B, T = c_kv.shape[:2]
    nb = T // Q_BLOCK
    topk = min(TOPK_MAX, T // 4)
    scale = HEAD_DIM ** -0.5
    s_pos = jnp.arange(T, dtype=jnp.int32)

    def to_blocks(a):
        return jnp.moveaxis(a.reshape((B, nb, Q_BLOCK) + a.shape[2:]), 1, 0)

    def block(args):
        blk, ql, qi, wi = args
        t_pos = blk * Q_BLOCK + jnp.arange(Q_BLOCK, dtype=jnp.int32)
        rel = jax.nn.relu(jnp.einsum('bqhd,bsd->bqhs', qi, k_idx))
        index = jnp.einsum('bqhs,bqh->bqs', rel, wi)
        causal = s_pos[None, :] <= t_pos[:, None]
        index = jnp.where(causal[None], index, -jnp.inf)
        _, sel = lax.top_k(index, topk)
        c_sel = jax.vmap(lambda c, i: c[i])(c_kv, sel)
        dist = t_pos[None, :, None] - sel
        valid = dist >= 0
        bias = rel_bias[t5_bucket(jnp.maximum(dist, 0))]
        scores = jnp.einsum('bqhr,bqkr->bqhk', ql, c_sel).astype(jnp.float32) * scale
        scores = scores + jnp.transpose(bias, (0, 1, 3, 2)).astype(jnp.float32)
        scores = jnp.where(valid[:, :, None, :], scores, -jnp.inf)
        p = jax.nn.softmax(scores, axis=-1).astype(c_sel.dtype)
        return jnp.einsum('bqhk,bqkr->bqhr', p, c_sel)

    out = lax.map(block, (jnp.arange(nb, dtype=jnp.int32), to_blocks(q_lat), to_blocks(q_idx), to_blocks(w_idx)))
    return jnp.moveaxis(out, 0, 1).reshape(B, T, N_HEADS, KV_RANK)

def chunked_gmlp(u, v, ln_g, ln_b, w_s, b_s):
    B, T = u.shape[:2]
    u = jax.nn.gelu(u)
    v = layer_norm(jax.nn.gelu(v), ln_g, ln_b)
    vc = v.reshape(B, T // CHUNK, CHUNK, GMLP_GROUPS, GMLP_GROUP_DIM)
    mask = jnp.tril(jnp.ones((CHUNK, CHUNK), dtype=bool))
    ws = jnp.where(mask[None], w_s, 0.0)
    s = jnp.einsum('gij,bcjge->bcige', ws, vc) + jnp.transpose(b_s)[None, None, :, :, None]
    return u * s.reshape(B, T, GMLP_WIDTH)

def hier_moe(h, rg_w, rg_b, re_w, re_b, w_gate, w_up, w_down):
    N = h.shape[0]
    gp = jax.nn.softmax((h @ rg_w + rg_b).astype(jnp.float32), axis=-1)
    g_w, g_idx = lax.top_k(gp, 1)
    el = (h @ re_w + re_b).reshape(N, N_GROUPS, EXPERTS_PER_GROUP)
    el = jnp.take_along_axis(el, g_idx[:, :, None], axis=1)[:, 0]
    ep = jax.nn.softmax(el.astype(jnp.float32), axis=-1)
    e_w, e_idx = lax.top_k(ep, TOP_K_INNER)
    e_w = g_w * e_w / jnp.sum(e_w, axis=-1, keepdims=True)
    eid = g_idx * EXPERTS_PER_GROUP + e_idx
    comb = jnp.sum(jax.nn.one_hot(eid, N_EXPERTS, dtype=jnp.float32) * e_w[..., None], axis=1).astype(h.dtype)
    y = jnp.zeros_like(h)
    for e in range(N_EXPERTS):
        he = jax.nn.silu(h @ w_gate[e]) * (h @ w_up[e])
        y = y + comb[:, e:e + 1] * (he @ w_down[e])
    return y

def first_inputs(seed: int = 0) -> dict:
    key = jax.random.key(seed)
    ks = jax.random.split(key, 24)

    def nrm(k, shape, s):
        return jax.random.normal(k, shape, jnp.float32) * s

    return {
        "x": nrm(ks[0], (BATCH, SEQ, D_MODEL), 1.0),
        "w_in": nrm(ks[1], (DEPTH, D_MODEL, IN_COLS), D_MODEL ** -0.5),
        "kv_norm_g": 1.0 + nrm(ks[2], (DEPTH, KV_RANK), 0.01),
        "w_uk": nrm(ks[3], (DEPTH, KV_RANK, N_HEADS, HEAD_DIM), KV_RANK ** -0.5),
        "w_uv": nrm(ks[4], (DEPTH, KV_RANK, N_HEADS, HEAD_DIM), KV_RANK ** -0.5),
        "rel_bias": nrm(ks[5], (NUM_BUCKETS, N_HEADS), 0.5),
        "ln_v_g": 1.0 + nrm(ks[6], (DEPTH, GMLP_WIDTH), 0.01),
        "ln_v_b": nrm(ks[7], (DEPTH, GMLP_WIDTH), 0.01),
        "w_spatial": nrm(ks[8], (DEPTH, GMLP_GROUPS, CHUNK, CHUNK), CHUNK ** -0.5),
        "b_spatial": 1.0 + nrm(ks[9], (DEPTH, GMLP_GROUPS, CHUNK), 0.01),
        "w_proj_a": nrm(ks[10], (DEPTH, ATTN_WIDTH, D_MODEL), ATTN_WIDTH ** -0.5),
        "w_proj_b": nrm(ks[11], (DEPTH, GMLP_WIDTH, D_MODEL), GMLP_WIDTH ** -0.5),
        "w_out": nrm(ks[12], (DEPTH, D_MODEL, D_MODEL), D_MODEL ** -0.5),
        "norm1_g": 1.0 + nrm(ks[13], (DEPTH, D_MODEL), 0.01),
        "norm2_g": 1.0 + nrm(ks[14], (DEPTH, D_MODEL), 0.01),
        "router_group_w": nrm(ks[15], (DEPTH, D_MODEL, N_GROUPS), D_MODEL ** -0.5),
        "router_group_b": nrm(ks[16], (DEPTH, N_GROUPS), 0.01),
        "router_expert_w": nrm(ks[17], (DEPTH, D_MODEL, N_EXPERTS), D_MODEL ** -0.5),
        "router_expert_b": nrm(ks[18], (DEPTH, N_EXPERTS), 0.01),
        "w_gate": nrm(ks[19], (DEPTH, N_EXPERTS, D_MODEL, D_FF_EXPERT), D_MODEL ** -0.5),
        "w_up": nrm(ks[20], (DEPTH, N_EXPERTS, D_MODEL, D_FF_EXPERT), D_MODEL ** -0.5),
        "w_down": nrm(ks[21], (DEPTH, N_EXPERTS, D_FF_EXPERT, D_MODEL), D_FF_EXPERT ** -0.5),
        "final_norm_g": 1.0 + nrm(ks[22], (D_MODEL,), 0.01),
    }

def first_block(x, w_in, kv_norm_g, w_uk, w_uv, rel_bias, ln_v_g, ln_v_b, w_spatial, b_spatial, w_proj_a, w_proj_b, w_out, norm1_g, norm2_g, router_group_w, router_group_b, router_expert_w, router_expert_b, w_gate, w_up, w_down, final_norm_g):
    B, T, D = x.shape
    splits = [int(c) for c in np.cumsum(IN_SIZES)[:-1]]
    idx_scale = (IDX_HEADS ** -0.5) * (IDX_DIM ** -0.5)
    for l in range(DEPTH):
        h = rms_norm(x, norm1_g[l])
        proj = h @ w_in[l]
        q, ckv, qi, ki, wi, u, v, ga, gb = jnp.split(proj, splits, axis=-1)
        q = q.reshape(B, T, N_HEADS, HEAD_DIM)
        c_kv = rms_norm(ckv, kv_norm_g[l])
        q_lat = jnp.einsum('bthd,rhd->bthr', q, w_uk[l])
        q_idx = qi.reshape(B, T, IDX_HEADS, IDX_DIM)
        w_idx = wi * idx_scale
        o_lat = sparse_attention(q_lat, q_idx, w_idx, c_kv, ki, rel_bias)
        o_a = jnp.einsum('bthr,rhd->bthd', o_lat, w_uv[l]).reshape(B, T, ATTN_WIDTH)
        y_a = o_a @ w_proj_a[l]
        y_b = chunked_gmlp(u, v, ln_v_g[l], ln_v_b[l], w_spatial[l], b_spatial[l]) @ w_proj_b[l]
        merged = jax.nn.sigmoid(ga) * y_a + jax.nn.sigmoid(gb) * y_b
        x = x + merged @ w_out[l]
        h2 = rms_norm(x, norm2_g[l]).reshape(B * T, D)
        y = hier_moe(h2, router_group_w[l], router_group_b[l], router_expert_w[l], router_expert_b[l], w_gate[l], w_up[l], w_down[l])
        x = x + y.reshape(B, T, D)
    return rms_norm(x, final_norm_g)


DEPTH_2 = 2

N_HEADS_2 = 16
ATTN_WIDTH_2 = N_HEADS_2 * HEAD_DIM
DILATED_PATTERNS = ((128, 1), (512, 4), (2048, 16))
N_GROUPS_2 = len(DILATED_PATTERNS)
FOX_Q_BLOCK = 128
ROT_DIM = HEAD_DIM // 4
ROPE_THETA = 500000.0
D_FF = -(-8 * D_MODEL // (3 * 256)) * 256
RMS_EPS = 1e-6
NEG_INF = -1e30
N_MIXERS = 2
N_A_LAYERS = (DEPTH_2 + 1) // 2
N_B_LAYERS = DEPTH_2 // 2


def rmsnorm(x, g):
    xf = x.astype(jnp.float32)
    y = xf * lax.rsqrt(jnp.mean(xf * xf, axis=-1, keepdims=True) + RMS_EPS) * g.astype(jnp.float32)
    return y.astype(x.dtype)

def partial_rotary(t, pos):
    half = ROT_DIM // 2
    inv_freq = ROPE_THETA ** (-jnp.arange(half, dtype=jnp.float32) * 2.0 / ROT_DIM)
    ang = pos[:, None] * inv_freq[None, :]
    cos = jnp.cos(ang)[None, :, None, :]
    sin = jnp.sin(ang)[None, :, None, :]
    t1 = t[..., :half].astype(jnp.float32)
    t2 = t[..., half:ROT_DIM].astype(jnp.float32)
    rot = jnp.concatenate([t1 * cos - t2 * sin, t2 * cos + t1 * sin], axis=-1).astype(t.dtype)
    return jnp.concatenate([rot, t[..., ROT_DIM:]], axis=-1)

def dilated_band_attention(q, k, v, dil, steps):
    B, S, H, D = q.shape
    L = S // dil
    blk = steps
    nb = -(-L // blk)
    Lp = nb * blk

    def by_stride(t):
        t = t.reshape(B, L, dil, H, D).transpose(0, 2, 1, 3, 4)
        return jnp.pad(t, ((0, 0), (0, 0), (0, Lp - L), (0, 0), (0, 0)))

    def band(t):
        tp = jnp.pad(t, ((0, 0), (0, 0), (blk, 0), (0, 0), (0, 0))).reshape(B, dil, nb + 1, blk, H, D)
        return jnp.concatenate([tp[:, :, :-1], tp[:, :, 1:]], axis=3)

    qb = by_stride(q).reshape(B, dil, nb, blk, H, D)
    kb = band(by_stride(k))
    vb = band(by_stride(v))

    s = jnp.einsum('bcnihd,bcnjhd->bcnhij', qb, kb).astype(jnp.float32) * (D ** -0.5)
    i = jnp.arange(blk)[:, None]
    j = jnp.arange(2 * blk)[None, :]
    diff = i + blk - j
    key_step = (jnp.arange(nb)[:, None] - 1) * blk + jnp.arange(2 * blk)[None, :]
    valid = ((diff >= 0) & (diff <= steps))[None, :, :] & (key_step >= 0)[:, None, :]
    s = jnp.where(valid[None, None, :, None, :, :], s, NEG_INF)

    m = jnp.max(s, axis=-1, keepdims=True)
    p = jnp.exp(s - m)
    den = jnp.sum(p, axis=-1, keepdims=True)
    o = jnp.einsum('bcnhij,bcnjhd->bcnihd', p / den, vb.astype(jnp.float32))
    lse = (m + jnp.log(den))[..., 0]

    o = o.reshape(B, dil, Lp, H, D)[:, :, :L].transpose(0, 2, 1, 3, 4).reshape(B, S, H, D)
    lse = lse.transpose(0, 1, 2, 4, 3).reshape(B, dil, Lp, H)[:, :, :L].transpose(0, 2, 1, 3).reshape(B, S, H)
    return o, lse

def dilated_mixer(h, w_in, w_out):
    B, S, _ = h.shape
    proj = (h @ w_in).reshape(B, S, N_GROUPS_2, 3, N_HEADS_2, HEAD_DIM)
    pos = jnp.arange(S, dtype=jnp.float32)
    outs, lses = [], []
    for g, (window, dil) in enumerate(DILATED_PATTERNS):
        q = partial_rotary(proj[:, :, g, 0], pos)
        k = partial_rotary(proj[:, :, g, 1], pos)
        v = proj[:, :, g, 2]
        o, lse = dilated_band_attention(q, k, v, dil, window // dil)
        outs.append(o)
        lses.append(lse)
    wts = jax.nn.softmax(jnp.stack(lses, axis=0), axis=0)
    o = jnp.einsum('gbsh,gbshd->bshd', wts, jnp.stack(outs, axis=0))
    return o.reshape(B, S, ATTN_WIDTH_2).astype(h.dtype) @ w_out

def forgetting_mixer(h, w_in, b_f, w_out):
    B, S, _ = h.shape
    proj = h @ w_in
    qkv = proj[..., :3 * ATTN_WIDTH_2].reshape(B, S, 3, N_HEADS_2, HEAD_DIM)
    q, k, v = qkv[:, :, 0], qkv[:, :, 1], qkv[:, :, 2]
    log_f = jax.nn.log_sigmoid(proj[..., 3 * ATTN_WIDTH_2:].astype(jnp.float32) + b_f.astype(jnp.float32))
    c = lax.cumsum(log_f, axis=1)
    nq = S // FOX_Q_BLOCK
    qb = q.reshape(B, nq, FOX_Q_BLOCK, N_HEADS_2, HEAD_DIM).transpose(1, 0, 2, 3, 4)
    cqb = c.reshape(B, nq, FOX_Q_BLOCK, N_HEADS_2).transpose(1, 0, 3, 2)
    ck = c.transpose(0, 2, 1)
    key_pos = jnp.arange(S)
    vf = v.astype(jnp.float32)
    scale = HEAD_DIM ** -0.5

    def block(args):
        qi, ci, n = args
        s = jnp.einsum('bihd,bjhd->bhij', qi, k).astype(jnp.float32) * scale
        s = s + ci[..., None] - ck[:, :, None, :]
        qpos = n * FOX_Q_BLOCK + jnp.arange(FOX_Q_BLOCK)
        s = jnp.where(key_pos[None, :] <= qpos[:, None], s, NEG_INF)
        p = jax.nn.softmax(s, axis=-1)
        return jnp.einsum('bhij,bjhd->bihd', p, vf)

    o = lax.map(block, (qb, cqb, jnp.arange(nq)))
    o = o.transpose(1, 0, 2, 3, 4).reshape(B, S, ATTN_WIDTH_2).astype(h.dtype)
    return o @ w_out

def swiglu(h, w_gu, w_down):
    gu = h @ w_gu
    g, u = gu[..., :D_FF], gu[..., D_FF:]
    return (jax.nn.silu(g) * u) @ w_down

def second_inputs(seed: int = 0) -> dict:
    key = jax.random.key(seed)
    ks = jax.random.split(key, 13)
    f32 = jnp.float32
    x = jax.random.normal(ks[0], (BATCH, SEQ, D_MODEL), f32)
    a_norm = 1.0 + 0.02 * jax.random.normal(ks[1], (N_A_LAYERS, D_MODEL), f32)
    a_w_in = jax.random.normal(ks[2], (N_A_LAYERS, D_MODEL, N_GROUPS_2 * 3 * ATTN_WIDTH_2), f32) * D_MODEL ** -0.5
    a_w_out = jax.random.normal(ks[3], (N_A_LAYERS, ATTN_WIDTH_2, D_MODEL), f32) * ATTN_WIDTH_2 ** -0.5
    b_norm = 1.0 + 0.02 * jax.random.normal(ks[4], (N_B_LAYERS, D_MODEL), f32)
    b_w_in = jax.random.normal(ks[5], (N_B_LAYERS, D_MODEL, 3 * ATTN_WIDTH_2 + N_HEADS_2), f32) * D_MODEL ** -0.5
    b_f = jnp.linspace(1.0, 6.0, N_HEADS_2, dtype=f32)[None, :] + 0.1 * jax.random.normal(ks[6], (N_B_LAYERS, N_HEADS_2), f32)
    b_w_out = jax.random.normal(ks[7], (N_B_LAYERS, ATTN_WIDTH_2, D_MODEL), f32) * ATTN_WIDTH_2 ** -0.5
    ffn_norm = 1.0 + 0.02 * jax.random.normal(ks[8], (DEPTH_2, D_MODEL), f32)
    ffn_w_gu = jax.random.normal(ks[9], (DEPTH_2, D_MODEL, 2 * D_FF), f32) * D_MODEL ** -0.5
    ffn_w_down = jax.random.normal(ks[10], (DEPTH_2, D_FF, D_MODEL), f32) * D_FF ** -0.5
    final_norm = 1.0 + 0.02 * jax.random.normal(ks[11], (D_MODEL,), f32)
    return {"x": x, "a_norm": a_norm, "a_w_in": a_w_in, "a_w_out": a_w_out,
            "b_norm": b_norm, "b_w_in": b_w_in, "b_f": b_f, "b_w_out": b_w_out,
            "ffn_norm": ffn_norm, "ffn_w_gu": ffn_w_gu, "ffn_w_down": ffn_w_down,
            "final_norm": final_norm}

def second_block(x, a_norm, a_w_in, a_w_out, b_norm, b_w_in, b_f, b_w_out,
              ffn_norm, ffn_w_gu, ffn_w_down, final_norm):
    h = x
    for i in range(DEPTH_2):
        j = i // N_MIXERS
        if i % N_MIXERS == 0:
            h = h + dilated_mixer(rmsnorm(h, a_norm[j]), a_w_in[j], a_w_out[j])
        else:
            h = h + forgetting_mixer(rmsnorm(h, b_norm[j]), b_w_in[j], b_f[j], b_w_out[j])
        h = h + swiglu(rmsnorm(h, ffn_norm[i]), ffn_w_gu[i], ffn_w_down[i])
    return rmsnorm(h, final_norm)


def setup_inputs(seed=0):
    out = dict(first_inputs(seed))
    for name, value in second_inputs(seed + 1).items():
        if name != "x":
            out[name + "_2"] = value
    return out


def reference(
    x, w_in, kv_norm_g, w_uk, w_uv, rel_bias, ln_v_g, ln_v_b, w_spatial, b_spatial, w_proj_a,
    w_proj_b, w_out, norm1_g, norm2_g, router_group_w, router_group_b, router_expert_w,
    router_expert_b, w_gate, w_up, w_down, final_norm_g, a_norm_2, a_w_in_2, a_w_out_2,
    b_norm_2, b_w_in_2, b_f_2, b_w_out_2, ffn_norm_2, ffn_w_gu_2, ffn_w_down_2, final_norm_2,
):
    x = first_block(
        x, w_in, kv_norm_g, w_uk, w_uv, rel_bias, ln_v_g, ln_v_b, w_spatial, b_spatial,
        w_proj_a, w_proj_b, w_out, norm1_g, norm2_g, router_group_w, router_group_b,
        router_expert_w, router_expert_b, w_gate, w_up, w_down, final_norm_g,
    )
    return second_block(
        x, a_norm_2, a_w_in_2, a_w_out_2, b_norm_2, b_w_in_2, b_f_2, b_w_out_2, ffn_norm_2,
        ffn_w_gu_2, ffn_w_down_2, final_norm_2,
    )


_drawn_inputs = setup_inputs


def setup_inputs(seed=0):
    import zlib

    import numpy as np

    out = dict(_drawn_inputs(seed))
    spreads = {}
    factors = {'kv_norm_g': 4.367,
     'ln_v_g': 8.0,
     'ln_v_b': 5.228,
     'b_spatial': 8.0,
     'norm1_g': 3.17,
     'router_expert_b': 2.69,
     'final_norm_g': 4.301,
     'a_norm_2': 8.0,
     'b_norm_2': 6.675,
     'final_norm_2': 7.146,
     'ffn_norm_2': 5.805}
    for name, (base, spread) in spreads.items():
        noise = np.random.default_rng([zlib.crc32(name.encode()), seed]).standard_normal(out[name].shape)
        drawn = base * np.exp(spread * noise) if base else spread * noise
        out[name] = __import__('jax').numpy.asarray(drawn.astype(out[name].dtype))
    for name, factor in factors.items():
        out[name] = (out[name] * factor).astype(out[name].dtype)
    return out
```

```python
import concourse.bass as bass
from concourse import mybir
from contextlib import ExitStack

F32 = mybir.dt.float32
F32R = mybir.dt.float32r
I32 = mybir.dt.int32
ALU = mybir.AluOpType
ACT = mybir.ActivationFunctionType
AXX = mybir.AxisListType.X

P = 128
T = 512
NT = T // P
D = 1024
KD = D // P
HALF = 512
HH = 8
DH = 64
NE = 32
NG = 4
EPG = NE // NG
FE = 256
FF = 2816
EPS = 1e-6
TOPK = 128
NEG = -1.0e30
TAKEN = -3.0e38
SCALE = DH ** -0.5
IDX_SCALE = (8 ** -0.5) * (64 ** -0.5)
BAND = T + P
SLOTS = 42
OOB = 4096

C_IDENT = 0
C_CAUSAL = 128
C_PREV = 640
C_CLASS = 768
C_NONE = 896
C_TRI = 1152
C_TRIS = 1280
C_ONES = 1408
C_RANK = 1536
C_SLOT = 1544
C_COS = 1586
C_SIN = 1714
C_COLS = 1842

B_MISC, B_Q, B_QI, B_V, B_U, B_GATES = 0, 1, 3, 5, 7, 9
B_PROJ = 17
B_WOUT = 21
B_DIL = 25
B_AOUT = 61
B_FFN = [65, 115]
B_FOX = 99
B_BOUT = 111
N_BLOCKS = 149
FF_ROUNDS = [8, 8, 6]
FF_CHUNK = [0, 8, 16]
FF_BLOCK = [0, 12, 24]
NORM_IN, NORM_MOE, NORM_A, NORM_F0, NORM_B, NORM_F1 = range(6)


def two_blocks_kernel(nc, a):
    ctx = ExitStack()

    def at(name, kb, shape, dt=F32):
        return nc.alloc_sbuf_tensor_at(name, shape, dt, offset=int((kb + 16) * 1024))

    X = at("X", 1, [P, NT, D])
    cst = at("cst", 17, [P, C_COLS])
    cursor = [40 * 1024 + 512]

    def small(name, shape, dt=F32):
        size = 4
        for n in shape[1:]:
            size *= n
        t = nc.alloc_sbuf_tensor_at(name, shape, dt, offset=cursor[0])
        cursor[0] += -(-size // 32) * 32
        return t

    gcol = small("gcol", [P, 6, KD])
    ones_col = small("ones_col", [P, 1])
    ss = small("ss", [P, NT])
    msq = small("msq", [P, NT])
    rms = small("rms", [P, NT])
    rstd = small("rstd", [P, NT])
    ids = small("ids", [P, 2 * NT], I32)
    gate_w = small("gate_w", [P, 2, NT])
    slot_rows = small("slot_rows", [P, SLOTS], I32)
    slot_expert = small("slot_expert", [1, SLOTS], I32)
    trips = small("trips", [1, 1], I32)
    gather_rows = small("gather_rows", [P, 2], I32)
    scatter_rows = small("scatter_rows", [P, 2], I32)
    w_idx = small("w_idx", [P, NT, HH])
    kvg = small("kvg", [P, 1])
    mx = small("mx", [P, 32])
    nmx = small("nmx", [P, 32])
    rsum = small("rsum", [P, 32])
    rinv = small("rinv", [P, 32])
    lse = small("lse", [P, NT, HH])
    ln_mean = small("ln_mean", [P, NT])
    max8 = small("max8", [P, 8])
    lse3 = small("lse3", [P, 3, NT, 16])
    lmax = small("lmax", [P, NT, 16])
    assert cursor[0] <= 45 * 1024
    raw = at("raw", 29, [P, 2, 2048])
    w_high = at("w_high", 45, [P, 2, 2048], F32R)
    w_low = at("w_low", 61, [P, 2, 2048], F32R)
    h_high = at("h_high", 77, [P, KD, T], F32R)
    h_low = at("h_low", 93, [P, KD, T], F32R)
    AR = 109
    xn = at("xn", AR + 80, [P, NT, D])
    band = at("band", AR, [P, HH, BAND])
    qT = at("qT", AR, [P, 4, T])
    qiT = at("qiT", AR + 8, [P, 4, T])
    PT = at("PT", AR + 8, [P, 2, T])
    bs_b = at("bs_b", AR + 12, [P, 4, P])
    uT = at("uT", AR + 16, [P, 4, T])
    vtok = at("vtok", AR + 24, [P, NT, HALF])
    KT = at("KT", AR + 16, [P, 4, T])
    V = at("V", AR + 24, [P, NT, HALF])
    merged_high = at("merged_high", AR, [P, KD, T], F32R)
    merged_low = at("merged_low", AR + 16, [P, KD, T], F32R)
    gates = at("gates", AR + 32, [P, 2 * KD, T])
    toep = at("toep", AR + 64, [P, HH, T])
    lng = at("lng", AR + 64, [P, HALF])
    lnb = at("lnb", AR + 66, [P, HALF])
    ws_raw = at("ws_raw", AR + 68, [P, 4, P])
    relb = at("relb", AR + 70, [32, HH])
    relb_wide = at("relb_wide", AR + 70.25, [32, HH, P])
    onehot = at("onehot", AR + 74.5, [32, BAND])
    idx = at("idx", AR + 80, [P, NT, T])
    sc = at("sc", AR + 88, [P, 2, T])
    misc = at("misc", AR + 92, [P, NT, 256])
    pr = at("pr", AR + 92, [P, 2, T])
    ws_t = at("ws_t", AR + 96, [P, 4, P])
    o_tok = at("o_tok", 1, [P, NT, HALF])
    ckvT = at("ckvT", 9, [P, T])
    kiT = at("kiT", 11, [P, T])
    w_uk = at("w_uk_s", 13, [P, HALF])
    w_uv = at("w_uv_s", 15, [P, HALF])
    g_wide = at("g_wide", AR, [P, D])
    rt_raw = at("rt_raw", AR + 4, [P, KD, 36])
    rt_high = at("rt_high", AR + 6, [P, KD, 36], F32R)
    rt_low = at("rt_low", AR + 8, [P, KD, 36], F32R)
    rt_bias = at("rt_bias", AR + 10, [P, 36])
    logit = at("logit", AR + 10.25, [P, NT, 36])
    r1 = at("r1", AR + 11, [P, NT, NE])
    r2 = at("r2", AR + 11.5, [P, NT, NE])
    pick = at("pick", AR + 12, [P, 2, NT, NE])
    both = at("both", AR + 13, [P, NT, NE])
    goh = at("goh", AR + 13.5, [P, NT, NG])
    el = at("el", AR + 13.75, [P, NT, EPG])
    el2 = at("el2", AR + 14, [P, NT, EPG])
    oh = at("oh", AR + 14.25, [P, 2, NT, EPG])
    rv = at("rv", AR + 14.75, [P, 12, NT])
    ntile = at("ntile", AR + 15, [P, NE])
    scan = at("scan", AR + 15.25, [P, 2, NE])
    posf = at("posf", AR + 15.5, [P, 2, NT])
    pos = at("pos", AR + 15.75, [P, 2 * NT], I32)
    cum = at("cum", AR + 16, [P, NT, NE])
    slotf = at("slotf", AR + 16.5, [1, SLOTS, NE])
    slote = at("slote", AR + 22, [1, SLOTS])
    cnt = at("cnt", AR + 22.25, [P, NE])
    empty = at("empty", AR + 23, [P, SLOTS], I32)
    m_raw = at("m_raw", 29, [P, 3, 2048])
    m_high = at("m_high", 53, [P, 2, 3, 2048], F32R)
    m_low = at("m_low", 101, [P, 2, 3, 2048], F32R)
    xg = at("xg", 149, [P, 2, D])
    xt_high = at("xt_high", 157, [P, 2, KD, P], F32R)
    xt_low = at("xt_low", 165, [P, 2, KD, P], F32R)
    y_out = at("y_out", 173, [P, 2, D])
    sg = at("sg", 181, [P, FE])
    he = at("he", 182, [P, FE])
    het_high = at("het_high", 183, [P, 2, P], F32R)
    het_low = at("het_low", 184, [P, 2, P], F32R)
    y_in = at("y_in", AR, [P, 2, NT, D])
    gw1 = at("gw1", AR + 64, [P, D])
    gw2 = at("gw2", AR, [P, D])
    qk = at("qk", AR, [P, 8, HALF])
    dqT = at("dqT", AR + 16, [P, 4, T])
    dkT = at("dkT", AR + 24, [P, 4, T])
    dV = at("dV", AR + 32, [P, NT, HALF])
    rot = at("rot", AR + 40, [P, 4, 8, 8, 8])
    dsc = at("dsc", AR + 48, [P, 2, T])
    dpr = at("dpr", AR + 52, [P, 2, T])
    dPT = at("dPT", AR + 56, [P, 2, T])
    o_st = at("o_st", AR + 60, [P, 2, HALF])
    og = at("og", AR, [P, 2, 3, D])
    act_high = at("act_high", AR, [P, 8, T], F32R)
    act_low = at("act_low", AR + 16, [P, 8, T], F32R)
    silu = at("silu", AR + 32, [P, 2, T])
    gu = at("gu", AR + 36, [P, 2, T])
    fqT = at("fqT", AR, [P, 4, T])
    fkT = at("fkT", AR + 8, [P, 4, T])
    fV = at("fV", AR + 16, [P, NT, HALF])
    ncb = at("ncb", AR + 24, [P, HH, T])
    o_high = at("o_high", AR + 40, [P, KD, T], F32R)
    o_low = at("o_low", AR + 56, [P, KD, T], F32R)
    fo_tok = at("fo_tok", AR + 72, [P, NT, HALF])
    fsc = at("fsc", AR + 80, [P, 2, T])
    fpr = at("fpr", AR + 84, [P, 2, T])
    fPT = at("fPT", AR + 88, [P, 2, T])
    fw_raw = at("fw_raw", AR + 24, [P, KD, 16])
    fw_high = at("fw_high", AR + 24.5, [P, KD, 16], F32R)
    fw_low = at("fw_low", AR + 25, [P, KD, 16], F32R)
    fb = at("fb", AR + 25.5, [P, 16])
    fz = at("fz", AR + 93.75, [P, NT, 16])
    fm = at("fm", AR + 94, [P, NT, 16])
    fe = at("fe", AR + 94.25, [P, NT, 16])
    c_tok = at("c_tok", AR + 94.5, [P, NT, 16])
    cT = at("cT", AR + 94.75, [16, T])
    sel16 = at("sel16", AR + 96.75, [16, P])

    d_band = nc.dram_tensor("d_band", [HH, P * BAND], F32, kind="Internal").ap()
    d_rows = nc.dram_tensor("d_rows", [2 * T, D], F32, kind="Internal").ap()
    d_y = nc.dram_tensor("d_y", [2 * T, D], F32, kind="Internal").ap()
    d_list = nc.dram_tensor("d_list", [SLOTS * P, 1], I32, kind="Internal").ap()
    d_o = nc.dram_tensor("d_o", [3, T, D], F32, kind="Internal").ap()
    d_lse = nc.dram_tensor("d_lse", [3, T, 16], F32, kind="Internal").ap()

    bank = [ctx.enter_context(nc.psum_tensor(f"bank{i}", [P, 512], F32)) for i in range(8)]
    G = bank[0:4]
    TB = bank[4:6]
    SB = bank[6:8]

    ident = cst[:, C_IDENT:C_IDENT + P]
    ones = cst[:, C_ONES:C_ONES + P]
    def sem(name):
        return ctx.enter_context(nc.semaphore(name))

    x_loaded = sem("x_loaded")
    cst_loaded = sem("cst_loaded")
    vec_loaded = sem("vec_loaded")
    band_vec_loaded = sem("band_vec_loaded")
    raw0 = sem("raw0")
    raw1 = sem("raw1")
    high_done = sem("high_done")
    low_done = sem("low_done")
    block_used = sem("block_used")
    phase_done = sem("phase_done")
    dve_step = sem("dve_step")
    act_step = sem("act_step")
    nm_squares = sem("nm_squares")
    nm_mean = sem("nm_mean")
    nm_root = sem("nm_root")
    nm_rows = sem("nm_rows")
    turned = sem("turned")
    turn_high = sem("turn_high")
    turn_free = sem("turn_free")
    relb_wide_done = sem("relb_wide_done")
    band_psum = sem("band_psum")
    band_copied = sem("band_copied")
    band_stored = sem("band_stored")
    toep_loaded = sem("toep_loaded")
    in_out = sem("in_out")
    misc_copied = sem("misc_copied")
    in_evac = sem("in_evac")
    ln_loaded = sem("ln_loaded")
    ck_mean = sem("ck_mean")
    ck_root = sem("ck_root")
    uk_loaded = sem("uk_loaded")
    ix_scores = sem("ix_scores")
    ix_relu = sem("ix_relu")
    ix_added = sem("ix_added")
    ln_var = sem("ln_var")
    ln_root = sem("ln_root")
    ln_done = sem("ln_done")
    bs_loaded = sem("bs_loaded")
    ws_loaded = sem("ws_loaded")
    gm_out = sem("gm_out")
    gm_free = sem("gm_free")
    kv_out = sem("kv_out")
    kv_copied = sem("kv_copied")
    g_done = sem("g_done")
    at_scores = sem("at_scores")
    at_read = sem("at_read")
    at_max = sem("at_max")
    at_prob = sem("at_prob")
    at_turned = sem("at_turned")
    at_copied = sem("at_copied")
    at_out = sem("at_out")
    at_done = sem("at_done")
    x_again = sem("x_again")
    pj_out = sem("pj_out")
    pj_free = sem("pj_free")
    pj_sum = sem("pj_sum")
    pj_high = sem("pj_high")
    wo_out = sem("wo_out")
    wo_free = sem("wo_free")
    rows_stored = sem("rows_stored")
    gw_loaded = sem("gw_loaded")
    rt_loaded = sem("rt_loaded")
    rt_high_done = sem("rt_high_done")
    rt_low_done = sem("rt_low_done")
    rt_out = sem("rt_out")
    rt_exp_in = sem("rt_exp_in")
    rt_exp = sem("rt_exp")
    rt_e2_in = sem("rt_e2_in")
    rt_e2 = sem("rt_e2")
    rt_both = sem("rt_both")
    rt_cum = sem("rt_cum")
    rt_pos = sem("rt_pos")
    rt_empty = sem("rt_empty")
    empty_stored = sem("empty_stored")
    list_stored = sem("list_stored")
    list_loaded = sem("list_loaded")
    rt_tables = sem("rt_tables")
    m_raw0 = sem("m_raw0")
    m_raw1 = sem("m_raw1")
    m_raw2 = sem("m_raw2")
    m_high_done = sem("m_high_done")
    m_low01 = sem("m_low01")
    m_low2 = sem("m_low2")
    m_gath0 = sem("m_gath0")
    m_gath1 = sem("m_gath1")
    m_scat0 = sem("m_scat0")
    m_scat1 = sem("m_scat1")
    m_turned = sem("m_turned")
    m_xhigh = sem("m_xhigh")
    m_xlow = sem("m_xlow")
    m_gu = sem("m_gu")
    m_silu = sem("m_silu")
    m_he = sem("m_he")
    m_he_turned = sem("m_he_turned")
    m_hehigh = sem("m_hehigh")
    m_helow = sem("m_helow")
    m_down = sem("m_down")
    m_y = sem("m_y")
    m_idx = sem("m_idx")
    y_loaded = sem("y_loaded")
    dve_summed = sem("dve_summed")
    dl_out = sem("dl_out")
    dl_evac = sem("dl_evac")
    dl_rot = sem("dl_rot")
    dl_stored0 = sem("dl_stored0")
    dl_stored1 = sem("dl_stored1")
    dl_ln = sem("dl_ln")
    dl_lse = sem("dl_lse")
    dl_lse_stored = sem("dl_lse_stored")
    mg_lse_loaded = sem("mg_lse_loaded")
    mg_og0 = sem("mg_og0")
    mg_og1 = sem("mg_og1")
    mg_exp_in = sem("mg_exp_in")
    mg_exp = sem("mg_exp")
    mg_done = sem("mg_done")
    ao_out = sem("ao_out")
    ao_free = sem("ao_free")
    ff_out = sem("ff_out")
    ff_silu = sem("ff_silu")
    ff_mul = sem("ff_mul")
    ff_high = sem("ff_high")
    ff_low = sem("ff_low")
    ff_down_out = sem("ff_down_out")
    ff_down_free = sem("ff_down_free")
    fo_loaded = sem("fo_loaded")
    fo_high = sem("fo_high")
    fo_lowd = sem("fo_lowd")
    fo_logit = sem("fo_logit")
    fo_e_in = sem("fo_e_in")
    fo_e = sem("fo_e")
    fo_l = sem("fo_l")
    fo_f = sem("fo_f")
    fo_c = sem("fo_c")
    fo_ct = sem("fo_ct")
    fo_sel = sem("fo_sel")
    fo_nc = sem("fo_nc")
    fo_ncb = sem("fo_ncb")
    fo_out = sem("fo_out")
    fo_evac = sem("fo_evac")
    bo_out = sem("bo_out")
    bo_free = sem("bo_free")
    gw1_loaded = sem("gw1_loaded")
    gw2_loaded = sem("gw2_loaded")
    out_stored = sem("out_stored")
    raw_loaded = [raw0, raw1]
    block = ctx.enter_context(nc.Block())

    def shaped(t, slot, k):
        return t[:, slot, :].rearrange("p (k n) -> p k n", k=k)

    def first_head(q, heads):
        return q if heads == 4 else 4 * (q // 2) + q % 2

    def tokens(t, chunk, tile, order):
        if order == 0:
            return t[:, chunk, tile * P:(tile + 1) * P]
        return t[:, chunk, tile:T:NT]

    @block.sync
    def _(sp):
        def load(n, slot, pieces):
            if not isinstance(n, int) or n >= 2:
                sp.wait_ge(low_done, n - 1)
            for dst, src in pieces:
                sp.dma_start(dst, src).then_inc(raw_loaded[slot], 16)

        def by_k(w):
            return w.rearrange("(k p) n -> p k n", p=P)

        def load_wide(n, w, k0, col):
            dst = shaped(raw, n % 2, 4)
            load(n, n % 2, [(dst[:, 2 * i:2 * i + 2, :],
                             by_k(w)[:, k0 + 2 * i:k0 + 2 * i + 2, col:col + 512]) for i in range(2)])

        def load_tall(n, w, col):
            dst = shaped(raw, n % 2, 8)
            load(n, n % 2, [(dst[:, 4 * i:4 * i + 4, :],
                             by_k(w)[:, 4 * i:4 * i + 4, col:col + 256]) for i in range(2)])

        w_in = a["w_in"][0]
        sp.dma_start(X[:, :, :], a["x"][0].rearrange("(t p) d -> p t d", p=P)).then_inc(x_loaded, 16)
        sp.dma_start(cst[:, :], a["table"]).then_inc(cst_loaded, 16)
        dst = shaped(raw, 0, 8)
        load(B_MISC, 0, [(dst[:, :, 0:128], by_k(w_in)[:, :, 512:640]),
                         (dst[:, :, 128:256], by_k(w_in)[:, :, 1152:1280])])
        load_tall(B_Q, w_in, 0)
        for dst, src in ((onehot[:, :], a["buckets"]), (relb[:, :], a["rel_bias"])):
            sp.dma_start(dst, src).then_inc(band_vec_loaded, 16)
        for dst, src in ((lng[:, :], a["ln_v_g"]), (lnb[:, :], a["ln_v_b"])):
            sp.dma_start(dst, src.partition_broadcast(P)).then_inc(ln_loaded, 16)
        sp.dma_start(ws_raw[:, :, :], a["w_spatial"][0].rearrange("g i j -> i g j")).then_inc(ws_loaded, 16)
        sp.wait_ge(band_copied, 2 * HH)
        sp.dma_start(d_band.rearrange("h (p m) -> p h m", p=P), band[:, :, :]).then_inc(band_stored, 16)
        load_tall(B_Q + 1, w_in, 256)
        sp.wait_ge(nm_rows, NT)
        sp.dma_start(w_uk[:, :], a["w_uk"][0].rearrange("r h d -> r (h d)")).then_inc(uk_loaded, 16)
        sp.dma_start(w_uv[:, :], a["w_uv"][0].rearrange("r h d -> r (h d)")).then_inc(uk_loaded, 16)
        for i in range(2):
            load_tall(B_QI + i, w_in, 640 + 256 * i)
        for i in range(2):
            load_wide(B_V + i, w_in, 4 * i, 1736)
        for i in range(2):
            load_tall(B_U + i, w_in, 1224 + 256 * i)
        with sp.Fori(0, 4) as i:
            for c in range(2):
                n = B_GATES + 2 * i + c
                slot = (B_GATES + c) % 2
                dst = shaped(raw, slot, 8)
                src = by_k(w_in)
                load(n, slot, [(dst[:, 4 * k:4 * k + 4, :],
                                src[:, 4 * k:4 * k + 4, bass.ds(2248 + 256 * c + 512 * i, 256)])
                               for k in range(2)])
        load_wide(B_PROJ, a["w_proj_a"][0], 0, 0)
        load_wide(B_PROJ + 1, a["w_proj_b"][0], 0, 0)
        sp.wait_ge(ln_done, NT)
        sp.wait_ge(ix_added, 24)
        sp.dma_start(bs_b[:, :, :].rearrange("p g i -> p (g i)"),
                     a["b_spatial"][0].rearrange("g i -> (g i)").partition_broadcast(P)).then_inc(bs_loaded, 16)
        sp.wait_ge(band_stored, 16)
        for h in range(HH):
            flat = d_band[h, P - 1:P - 1 + P * (BAND - 1)].rearrange("(p m) -> p m", m=BAND - 1)
            sp.dma_start(toep[:, h, :], flat[:, 0:T]).then_inc(toep_loaded, 16)
        load_wide(B_PROJ + 2, a["w_proj_a"][0], 0, 512)
        load_wide(B_PROJ + 3, a["w_proj_b"][0], 0, 512)
        sp.wait_ge(phase_done, 3 * 2)
        sp.dma_start(X[:, :, :], a["x"][0].rearrange("(t p) d -> p t d", p=P)).then_inc(x_again, 16)
        for half in range(2):
            for i in range(2):
                load_wide(B_WOUT + 2 * half + i, a["w_out"][0], 4 * i, 512 * half)
        sp.wait_ge(phase_done, 3 * 4)
        sp.dma_start(g_wide[:, :], a["norm2_g"][0].partition_broadcast(P)).then_inc(gw_loaded, 16)
        sp.dma_start(rt_raw[:, :, 0:NG], by_k(a["router_group_w"][0])).then_inc(rt_loaded, 16)
        sp.dma_start(rt_raw[:, :, NG:36], by_k(a["router_expert_w"][0])).then_inc(rt_loaded, 16)
        sp.dma_start(rt_bias[:, 0:NG], a["router_group_b"][0].partition_broadcast(P)).then_inc(rt_loaded, 16)
        sp.dma_start(rt_bias[:, NG:36], a["router_expert_b"][0].partition_broadcast(P)).then_inc(rt_loaded, 16)
        sp.wait_ge(nm_rows, 2 * NT)
        for k in range(2):
            sp.dma_start(d_rows[k * T:(k + 1) * T, :].rearrange("(t p) d -> p t d", p=P),
                         xn[:, :, :]).then_inc(rows_stored, 16)
        sp.wait_ge(rt_empty, 1)
        sp.dma_start(d_list.rearrange("(p j) o -> p (j o)", p=P), empty[:, :]).then_inc(empty_stored, 16)
        sp.wait_ge(list_stored, 16 * 2 * NT)
        sp.dma_start(slot_rows[:, :], d_list.rearrange("(p j) o -> p (j o)", p=P)).then_inc(list_loaded, 16)
        sp.wait_ge(rt_tables, 1)
        sp.wait_ge(phase_done, 3 * 5)
        m_raws = [m_raw0, m_raw1, m_raw2]

        def expert(j, first):
            e = sp.value_load(slot_expert[0:1, bass.ds(j, 1)] if not isinstance(j, int)
                              else slot_expert[0:1, j:j + 1], min_val=0, max_val=NE - 1)
            w_g = a["w_gate"][0, bass.ds(e, 1), :, :].rearrange("o (k p) n -> p (o k) n", p=P)
            w_u = a["w_up"][0, bass.ds(e, 1), :, :].rearrange("o (k p) n -> p (o k) n", p=P)
            w_d = a["w_down"][0, bass.ds(e, 1), :, :].rearrange("o (k p) n -> p (o k) n", p=P)
            for b in range(2):
                if not first:
                    sp.wait_ge(m_low01, 2 * j + b - 1)
                dst = shaped(m_raw, b, 4)
                sp.dma_start(dst[:, :, 0:FE], w_g[:, 4 * b:4 * b + 4, :]).then_inc(m_raws[b], 16)
                sp.dma_start(dst[:, :, FE:2 * FE], w_u[:, 4 * b:4 * b + 4, :]).then_inc(m_raws[b], 16)
            if not first:
                sp.wait_ge(m_low2, j)
            sp.dma_start(shaped(m_raw, 2, 2), w_d).then_inc(m_raws[2], 16)

        n_trips = sp.value_load(trips[0:1, 0:1], min_val=4, max_val=20)
        expert(0, True)
        expert(1, False)
        expert(2, False)
        with sp.Fori(1, n_trips) as i:
            expert(2 * i + 1, False)
            expert(2 * i + 2, False)
        sp.wait_ge(phase_done, 3 * 6)
        sp.dma_start(gw1[:, :], a["final_norm_g"].partition_broadcast(P)).then_inc(gw1_loaded, 16)
        for k in range(2):
            sp.dma_start(y_in[:, k, :, :], d_y[k * T:(k + 1) * T, :].rearrange("(t p) d -> p t d", p=P))\
              .then_inc(y_loaded, 16)
        def dil_block(hf, g, kind, kh):
            load_wide(B_DIL + ((hf * 3 + g) * 3 + kind) * 2 + kh, a["a_w_in_2"][0], 4 * kh,
                      g * 3 * D + kind * D + hf * HALF)
        for v in range(6):
            for kind in range(3):
                for kh in range(2):
                    dil_block(v // 3, v % 3, kind, kh)
        load_wide(B_AOUT, a["a_w_out_2"][0], 0, 0)
        load_wide(B_AOUT + 1, a["a_w_out_2"][0], 4, 0)
        sp.wait_ge(phase_done, 3 * 9)
        sp.wait_ge(dl_lse_stored, 16 * 6)
        for g in range(3):
            sp.dma_start(lse3[:, g, :, :], d_lse[g].rearrange("(t p) h -> p t h", p=P)).then_inc(mg_lse_loaded, 16)
        sp.wait_ge(dl_stored0, 16 * 12)
        sp.wait_ge(dl_stored1, 16 * 12)
        for t in range(NT):
            if t >= 2:
                sp.wait_ge(mg_done, t - 1)
            sp.dma_start(og[:, t % 2, :, :], d_o[:, t * P:(t + 1) * P, :].rearrange("g p d -> p g d"))\
              .then_inc([mg_og0, mg_og1][t % 2], 16)
        for i in range(2):
            load_wide(B_AOUT + 2 + i, a["a_w_out_2"][0], 4 * i, 512)

        def ffn_loads(l):
            w_gu, w_dn = by_k(a["ffn_w_gu_2"][l]), a["ffn_w_down_2"][l]
            for r, chunks in enumerate(FF_ROUNDS):
                n0 = B_FFN[l] + FF_BLOCK[r]
                with sp.Fori(0, chunks // 2) as i:
                    for c in range(2):
                        slot = (n0 + c) % 2
                        dst = shaped(raw, slot, 8)
                        col = P * (FF_CHUNK[r] + c) + 2 * P * i
                        load(n0 + c + 2 * i, slot, [(dst[:, :, 0:P], w_gu[:, :, bass.ds(col, P)]),
                                                    (dst[:, :, P:2 * P], w_gu[:, :, bass.ds(col + FF, P)])])
                for half in range(2):
                    for i in range(2):
                        n = n0 + chunks + 2 * half + i
                        k0, kn = FF_CHUNK[r] + 4 * i, min(4, chunks - 4 * i)
                        dst = shaped(raw, n % 2, 4)
                        src = by_k(w_dn)
                        load(n, n % 2, [(dst[:, k:k + kn // 2, :],
                                         src[:, k0 + k:k0 + k + kn // 2, 512 * half:512 * half + 512])
                                        for k in (0, kn // 2)])

        ffn_loads(0)
        w_b = a["b_w_in_2"][0]
        for i in range(2):
            load_tall(B_FOX + i, w_b, 256 * i)
        sp.wait_ge(phase_done, 3 * 11)
        sp.dma_start(fw_raw[:, :, :], by_k(w_b)[:, :, 3 * D:3 * D + 16]).then_inc(fo_loaded, 16)
        sp.dma_start(fb[:, :], a["b_f_2"][0].partition_broadcast(P)).then_inc(fo_loaded, 16)
        for hf in range(2):
            for kind in range(0 if hf else 1, 2):
                for i in range(2):
                    load_tall(B_FOX + 6 * hf + 2 * kind + i, w_b, kind * D + hf * HALF + 256 * i)
            for i in range(2):
                load_wide(B_FOX + 6 * hf + 4 + i, w_b, 4 * i, 2 * D + hf * HALF)
        for half in range(2):
            for i in range(2):
                load_wide(B_BOUT + 2 * half + i, a["b_w_out_2"][0], 4 * i, 512 * half)
        ffn_loads(1)
        sp.wait_ge(phase_done, 3 * 14)
        sp.dma_start(gw2[:, :], a["final_norm_2"].partition_broadcast(P)).then_inc(gw2_loaded, 16)
        sp.wait_ge(nm_rows, 8 * NT)
        sp.dma_start(a["out"][0].rearrange("(t p) d -> p t d", p=P), xn[:, :, :]).then_inc(out_stored, 16)
        sp.wait_ge(out_stored, 16)

    @block.tensor
    def _(pe):
        def phase_end(k):
            pe.drain().then_inc(phase_done, 1)
            pe.wait_ge(phase_done, 3 * k)

        def pass3(out, sta, mov, start, stop):
            pe.matmul(out, sta[0], mov[0], start=start, stop=False)
            pe.matmul(out, sta[0], mov[1], start=False, stop=False)
            return pe.matmul(out, sta[1], mov[0], start=False, stop=stop)

        def weights(slot, k):
            return shaped(w_high, slot, k), shaped(w_low, slot, k)

        def block_ready(n):
            pe.wait_ge(low_done, n + 1)

        chunk = [0]

        def turn(tiles):
            m = chunk[0]
            chunk[0] += 1
            if m >= 2:
                pe.wait_ge(turn_free, m - 1)
            for t, src in enumerate(tiles):
                last = pe.transpose(TB[m % 2][:, t * P:(t + 1) * P], src, ident)
            last.then_inc(turned, 1)

        def turn_norm(r):
            pe.wait_ge(nm_rows, NT * (r + 1))
            for c in range(KD):
                turn([xn[:, t, c * P:(c + 1) * P] for t in range(NT)])

        def by_rows(n, mov_k, act, k0, kn, outs, free, done, start, stop, order=0):
            block_ready(n)
            wh, wl = weights(n % 2, mov_k)
            for t in range(NT):
                if start and free is not None:
                    free(t)
                for k in range(kn):
                    sta = (tokens(act[0], k0 + k, t, order), tokens(act[1], k0 + k, t, order))
                    last = pass3(outs[t][:, :], sta, (wh[:, k, :], wl[:, k, :]), start and k == 0, stop and k == kn - 1)
                if stop:
                    last.then_inc(done, 1)
            if not stop:
                last.then_inc(block_used, 1)

        pe.wait_ge(cst_loaded, 16)
        pe.wait_ge(band_vec_loaded, 32)
        pe.wait_ge(relb_wide_done, 1)
        for h in range(HH):
            if h:
                pe.wait_ge(band_copied, 2 * h)
            pe.matmul(SB[0][:, 0:T], relb_wide[:, h, :], onehot[:, 0:T], start=True, stop=True)
            pe.matmul(SB[1][:, 0:P], relb_wide[:, h, :], onehot[:, T:BAND], start=True, stop=True)\
              .then_inc(band_psum, 1)
        pe.wait_ge(ws_loaded, 16)
        turn([ws_raw[:, g, :] for g in range(4)])
        turn_norm(0)
        pe.wait_ge(turn_free, chunk[0])

        hh = (h_high, h_low)

        def in_free(j):
            if 4 <= j < 8:
                pe.wait_ge(misc_copied, j - 3)
            elif j >= 8:
                pe.wait_ge(in_evac, j - 7)

        def tall(n, j0):
            block_ready(n)
            wh, wl = weights(n % 2, 8)
            for m in range(2):
                in_free(j0 + m)
                for k in range(KD):
                    c = slice(m * P, (m + 1) * P)
                    last = pass3(G[(j0 + m) % 4][:, :], (wh[:, k, c], wl[:, k, c]),
                                 (h_high[:, k, :], h_low[:, k, :]), k == 0, k == KD - 1)
                if m == 0:
                    last.then_inc(in_out, 1)
            return last

        block_ready(B_MISC)
        wh, wl = weights(0, 8)
        for t in range(NT):
            for k in range(KD):
                last = pass3(G[t][:, 0:200], (tokens(h_high, k, t, 0), tokens(h_low, k, t, 0)),
                             (wh[:, k, 0:200], wl[:, k, 0:200]), k == 0, k == KD - 1)
            last.then_inc(in_out, 1)
        for i in range(2):
            tall(B_Q + i, 4 + 2 * i).then_inc(in_out, 1)
        pe.wait_ge(ck_root, 1)
        turn([misc[:, t, 0:P] for t in range(NT)])
        turn([misc[:, t, P:2 * P] for t in range(NT)])
        for i in range(2):
            tall(B_QI + i, 8 + 2 * i).then_inc(in_out, 1)
        for kh in range(2):
            by_rows(B_V + kh, 4, hh, 4 * kh, 4, G, lambda t: in_free(12 + t), in_out, kh == 0, kh == 1)
        pe.wait_ge(turn_free, chunk[0])
        pe.wait_ge(in_evac, 8)
        unit = 0
        for qt in range(1, NT):
            for h in range(HH):
                if unit >= 2:
                    pe.wait_ge(ix_relu, unit - 1)
                rows = slice(DH * (h % 2), DH * (h % 2) + DH)
                pe.matmul(SB[unit % 2][:, 0:(qt + 1) * P], qiT[rows, h // 2, qt * P:(qt + 1) * P],
                          kiT[rows, 0:(qt + 1) * P], start=True, stop=True).then_inc(ix_scores, 1)
                unit += 1
        for i in range(2):
            tall(B_U + i, 16 + 2 * i).then_inc(in_out, 1)
        with pe.Fori(0, 4) as it:
            for c in range(2):
                n = B_GATES + c
                pe.wait_ge(low_done, 2 * it + n + 1)
                wh, wl = weights(n % 2, 8)
                for m in range(2):
                    j = 20 + 2 * c + m
                    pe.wait_ge(in_evac, 4 * it + j - 7)
                    for k in range(KD):
                        cc = slice(m * P, (m + 1) * P)
                        last = pass3(G[j % 4][:, :], (wh[:, k, cc], wl[:, k, cc]),
                                     (h_high[:, k, :], h_low[:, k, :]), k == 0, k == KD - 1)
                    last.then_inc(in_out, 1)
        phase_end(1)

        pe.wait_ge(ln_done, NT)
        for g in range(4):
            for c in range(NT):
                last = pe.matmul(G[g][:, c * P:(c + 1) * P], vtok[:, c, g * P:(g + 1) * P], ws_t[:, g, :],
                                 start=True, stop=True)
            last.then_inc(gm_out, 1)
        pe.wait_ge(uk_loaded, 32)
        for m in range(4):
            pe.wait_ge(gm_free, m + 1)
            pe.matmul(G[m][:, :], w_uk[:, m * P:(m + 1) * P], ckvT[:, :], start=True, stop=True)\
              .then_inc(kv_out, 1)
        for t in range(NT):
            pe.wait_ge(kv_copied, t + 1)
            pe.matmul(G[t][:, :], ckvT[:, t * P:(t + 1) * P], w_uv[:, :], start=True, stop=True)\
              .then_inc(kv_out, 1)

        def attend(base, tile0, q_, k_, v_, pr_, pt_):
            def scores(u):
                qt, h = divmod(u, HH)
                if u >= 2:
                    pe.wait_ge(at_read, base + u - 1)
                rows = slice(DH * (h % 2), DH * (h % 2) + DH)
                pe.matmul(SB[u % 2][:, 0:(qt + 1) * P], q_[rows, h // 2, qt * P:(qt + 1) * P],
                          k_[rows, h // 2, 0:(qt + 1) * P], start=True, stop=True).then_inc(at_scores, 1)

            def turn_probs(u):
                pe.wait_ge(at_prob, base + u + 1)
                if u >= 2:
                    pe.wait_ge(at_copied, base + u - 1)
                for kt in range(u // HH + 1):
                    last = pe.transpose(TB[u % 2][:, kt * P:(kt + 1) * P],
                                        pr_[:, u % 2, kt * P:(kt + 1) * P], ident)
                last.then_inc(at_turned, 1)

            def times_values(u):
                qt, h = divmod(u, HH)
                pe.wait_ge(at_copied, base + u + 1)
                if h == 0 and qt >= 2:
                    pe.wait_ge(at_done, tile0 + qt - 1)
                for kt in range(qt + 1):
                    last = pe.matmul(G[qt % 2][:, h * DH:(h + 1) * DH], pt_[:, u % 2, kt * P:(kt + 1) * P],
                                     v_[:, kt, h * DH:(h + 1) * DH], start=(kt == 0), stop=(kt == qt))
                if h == HH - 1:
                    last.then_inc(at_out, 1)

            scores(0)
            scores(1)
            for u in range(NT * HH):
                turn_probs(u)
                if u + 2 < NT * HH:
                    scores(u + 2)
                if u >= 1:
                    times_values(u - 1)
            times_values(NT * HH - 1)

        pe.wait_ge(kv_copied, 8)
        pe.wait_ge(turn_free, chunk[0])
        attend(0, 0, qT, KT, V, pr, PT)
        pe.wait_ge(at_done, NT)
        pe.wait_ge(at_copied, 32)
        for m in range(4):
            turn([o_tok[:, t, m * P:(m + 1) * P] for t in range(NT)])
        pe.wait_ge(turn_free, chunk[0])
        pe.wait_ge(g_done, 4)
        phase_end(2)

        for b in range(4):
            block_ready(B_PROJ + b)
            wh, wl = weights((B_PROJ + b) % 2, 4)
            src0 = 0 if b % 2 == 0 else 4
            for m in range(4):
                if b:
                    pe.wait_ge(pj_free, 4 * (b - 1) + m + 1)
                for k in range(4):
                    cc = slice(m * P, (m + 1) * P)
                    last = pass3(G[m][:, :], (wh[:, k, cc], wl[:, k, cc]),
                                 (h_high[:, src0 + k, :], h_low[:, src0 + k, :]), k == 0, k == 3)
                last.then_inc(pj_out, 1)
        phase_end(3)

        def rows_out(n0, act, out, free, base):
            for half in range(2):
                for kh in range(2):
                    def wait_free(t):
                        if half:
                            pe.wait_ge(free, base + t + 1)
                    by_rows(n0 + 2 * half + kh, 4, act, 4 * kh, 4, G, wait_free, out, kh == 0, kh == 1)

        rows_out(B_WOUT, (merged_high, merged_low), wo_out, wo_free, 0)
        phase_end(4)

        turn_norm(1)
        pe.wait_ge(turn_free, chunk[0])
        pe.wait_ge(rt_low_done, 1)
        for t in range(NT):
            for k in range(KD):
                last = pass3(G[t][:, 0:36], (tokens(h_high, k, t, 0), tokens(h_low, k, t, 0)),
                             (rt_high[:, k, :], rt_low[:, k, :]), k == 0, k == KD - 1)
            last.then_inc(rt_out, 1)
        pe.wait_ge(rt_both, 1)
        for t in range(NT):
            for q in range(t + 1):
                pe.matmul(SB[0][:, t * NE:(t + 1) * NE], ones if q < t else cst[:, C_TRIS:C_TRIS + P],
                          both[:, q, :], start=(q == 0), stop=(q == t))
        for q in range(NT):
            last = pe.matmul(SB[1][:, 0:NE], ones, both[:, q, :], start=(q == 0), stop=(q == NT - 1))
        last.then_inc(rt_cum, 1)
        phase_end(5)

        m_gath = [m_gath0, m_gath1]

        def turn_rows(j, b, uses):
            pe.wait_ge(m_gath[b], 16 * uses)
            for half in range(2):
                for c in range(4):
                    k = 4 * half + c
                    last = pe.transpose(TB[half][:, c * P:(c + 1) * P], xg[:, b, k * P:(k + 1) * P], ident)
                last.then_inc(m_turned, 1)

        def slot(j, b, next_uses):
            pe.wait_ge(m_xlow, 2 * j + 2)
            for k in range(KD):
                if k % 4 == 0:
                    pe.wait_ge(m_low01, 2 * j + 1 + k // 4)
                w = [shaped(t[:, b], k // 4, 4)[:, k % 4, :] for t in (m_high, m_low)]
                last = pass3(G[b][:, :], (xt_high[:, b, k, :], xt_low[:, b, k, :]), w, k == 0, k == KD - 1)
            last.then_inc(m_gu, 1)
            turn_rows(j + 1, 1 - b, next_uses)
            pe.wait_ge(m_he, j + 1)
            for c in range(2):
                last = pe.transpose(SB[0][:, c * P:(c + 1) * P], he[:, c * P:(c + 1) * P], ident)
            last.then_inc(m_he_turned, 1)
            pe.wait_ge(m_helow, j + 1)
            pe.wait_ge(m_low2, j + 1)
            pe.wait_ge(m_y, j + 1)
            for c in range(2):
                for half in range(2):
                    w = [shaped(t[:, b], 2, 2)[:, c, 512 * half:512 * half + 512] for t in (m_high, m_low)]
                    last = pass3(G[2 + half][:, :], (het_high[:, c, :], het_low[:, c, :]), w, c == 0, c == 1)
            last.then_inc(m_down, 1)

        n_trips = pe.value_load(trips[0:1, 0:1], min_val=4, max_val=20)
        turn_rows(0, 0, 1)
        slot(0, 0, 1)
        slot(1, 1, 2)
        with pe.Fori(1, n_trips) as i:
            slot(2 * i, 0, i + 1)
            slot(2 * i + 1, 1, i + 2)
        phase_end(6)
        phase_end(7)
        turn_norm(3)
        pe.wait_ge(turn_free, chunk[0])
        phase_end(8)
        unit0 = 32
        for v in range(6):
            g = v % 3
            order = min(g, 1)
            for kind in range(3):
                for kh in range(2):
                    def wait_free(t):
                        j = v * 12 + kind * 4 + t
                        if kind:
                            pe.wait_ge(dl_evac, j - 3)
                        elif v:
                            pe.wait_ge(dl_evac, 12 * v)
                            pe.wait_ge(at_done, NT * (v + 1))
                    by_rows(B_DIL + (v * 3 + kind) * 2 + kh, 4, hh, 4 * kh, 4, G, wait_free,
                            dl_out, kh == 0, kh == 1, order=order)
            pe.wait_ge(dl_rot, v + 1)
            if v:
                pe.wait_ge(at_copied, unit0)
            for kind in range(2):
                for m in range(4):
                    turn([qk[:, 4 * kind + t, m * P:(m + 1) * P] for t in range(NT)])
            pe.wait_ge(turn_free, chunk[0])
            pe.wait_ge(dl_evac, 12 * (v + 1))
            hu = 2 if g == 0 else 4
            per_tile = HH // hu
            units = NT * per_tile

            def scores(u):
                t, q = divmod(u, per_tile)
                if u >= 2:
                    pe.wait_ge(at_read, unit0 + u - 1)
                for e in range(hu):
                    h = first_head(q, hu) + 2 * e
                    rows = slice(DH * (h % 2), DH * (h % 2) + DH)
                    q_ = dqT[rows, h // 2, t * P:(t + 1) * P]
                    keys = ([t, t - 1] if t else [0, 0]) if g == 0 else [t]
                    for z, kt in enumerate(keys):
                        o = (e * len(keys) + z) * P
                        last = pe.matmul(SB[u % 2][:, o:o + P], q_, dkT[rows, h // 2, kt * P:(kt + 1) * P],
                                         start=True, stop=True)
                last.then_inc(at_scores, 1)

            def turn_probs(u):
                pe.wait_ge(at_prob, unit0 + u + 1)
                if u >= 2:
                    pe.wait_ge(at_copied, unit0 + u - 1)
                for c in range(4):
                    last = pe.transpose(TB[u % 2][:, c * P:(c + 1) * P], dpr[:, u % 2, c * P:(c + 1) * P], ident)
                last.then_inc(at_turned, 1)

            def times_values(u):
                t, q = divmod(u, per_tile)
                pe.wait_ge(at_copied, unit0 + u + 1)
                if q == 0 and t >= 2:
                    pe.wait_ge(at_done, NT * (v + 1) + t - 1)
                for e in range(hu):
                    h = first_head(q, hu) + 2 * e
                    keys = ([t, t - 1] if t else [0, 0]) if g == 0 else [t]
                    for z, kt in enumerate(keys):
                        o = (e * len(keys) + z) * P
                        last = pe.matmul(G[t % 2][:, h * DH:(h + 1) * DH], dPT[:, u % 2, o:o + P],
                                         dV[:, kt, h * DH:(h + 1) * DH], start=(z == 0), stop=(z == len(keys) - 1))
                if q == per_tile - 1:
                    last.then_inc(at_out, 1)

            scores(0)
            scores(1)
            for u in range(units):
                turn_probs(u)
                if u + 2 < units:
                    scores(u + 2)
                if u >= 1:
                    times_values(u - 1)
            times_values(units - 1)
            unit0 += units
        phase_end(9)
        pe.wait_ge(mg_done, NT)
        for c in range(KD):
            turn([xn[:, t, c * P:(c + 1) * P] for t in range(NT)])
        pe.wait_ge(turn_free, chunk[0])
        rows_out(B_AOUT, hh, ao_out, ao_free, 0)
        phase_end(10)

        def swiglu(l):
            for r, chunks in enumerate(FF_ROUNDS):
                n0 = B_FFN[l] + FF_BLOCK[r]
                f0 = 22 * l + FF_CHUNK[r]
                down0 = (3 * l + r) * 8
                if r:
                    pe.wait_ge(ff_down_free, down0)

                def up(i, peeled):
                    for c in range(2):
                        pe.wait_ge(low_done, n0 + c + 1 + 2 * i)
                        wh, wl = weights((n0 + c) % 2, 8)
                        if not peeled:
                            pe.wait_ge(ff_mul, f0 + c - 1 + 2 * i)
                        for m in range(2):
                            cc = slice(m * P, (m + 1) * P)
                            for k in range(KD):
                                last = pass3(G[2 * c + m][:, :], (wh[:, k, cc], wl[:, k, cc]),
                                             (h_high[:, k, :], h_low[:, k, :]), k == 0, k == KD - 1)
                            if m == 1:
                                last.then_inc(ff_out, 1)

                up(0, f0 == 0)
                with pe.Fori(1, chunks // 2) as i:
                    up(i, False)
                pe.wait_ge(ff_low, f0 + chunks)
                for half in range(2):
                    outs = bank[4:8] if half == 0 else bank[0:4]
                    for i in range(2):
                        n = n0 + chunks + 2 * half + i
                        kn = min(4, chunks - 4 * i)
                        by_rows(n, 4, (act_high, act_low), 4 * i, kn, outs, None, ff_down_out, i == 0, i == 1)

        turn_norm(4)
        pe.wait_ge(turn_free, chunk[0])
        swiglu(0)
        phase_end(11)
        turn_norm(5)
        pe.wait_ge(turn_free, chunk[0])
        pe.wait_ge(fo_lowd, 1)
        for t in range(NT):
            for k in range(KD):
                last = pass3(SB[0][:, t * 16:(t + 1) * 16], (tokens(h_high, k, t, 0), tokens(h_low, k, t, 0)),
                             (fw_high[:, k, :], fw_low[:, k, :]), k == 0, k == KD - 1)
        last.then_inc(fo_logit, 1)
        pe.wait_ge(fo_f, 1)
        for t in range(NT):
            for q in range(t + 1):
                last = pe.matmul(SB[1][:, t * 16:(t + 1) * 16], ones if q < t else cst[:, C_TRI:C_TRI + P],
                                 fz[:, q, :], start=(q == 0), stop=(q == t))
        last.then_inc(fo_c, 1)
        pe.wait_ge(fo_ct, 1)
        for t in range(NT):
            last = pe.transpose(SB[0][0:16, t * P:(t + 1) * P], c_tok[:, t, :], ident)
        last.then_inc(fo_sel, 1)
        for hf in range(2):
            for kind in range(3):
                if kind < 2:
                    for i in range(2):
                        n = B_FOX + 6 * hf + 2 * kind + i
                        block_ready(n)
                        wh, wl = weights(n % 2, 8)
                        for m in range(2):
                            j = 12 * hf + 4 * kind + 2 * i + m
                            if j % 12 >= 4:
                                pe.wait_ge(fo_evac, j - 3)
                            elif hf:
                                pe.wait_ge(at_done, 28 + NT)
                            cc = slice(m * P, (m + 1) * P)
                            for k in range(KD):
                                last = pass3(G[j % 4][:, :], (wh[:, k, cc], wl[:, k, cc]),
                                             (h_high[:, k, :], h_low[:, k, :]), k == 0, k == KD - 1)
                            last.then_inc(fo_out, 1)
                else:
                    for kh in range(2):
                        by_rows(B_FOX + 6 * hf + 4 + kh, 4, hh, 4 * kh, 4, G,
                                lambda t: pe.wait_ge(fo_evac, 12 * hf + 8 + t - 3),
                                fo_out, kh == 0, kh == 1)
            for h in range(HH):
                pe.wait_ge(fo_nc, (HH + 1) * hf + h + 1)
                pe.matmul(SB[h % 2][:, :], sel16[:, :], cT[:, :], start=True, stop=True).then_inc(fo_ncb, 1)
            pe.wait_ge(fo_nc, (HH + 1) * (hf + 1))
            pe.wait_ge(fo_evac, 12 * (hf + 1))
            pe.wait_ge(turn_free, chunk[0])
            attend(96 + 32 * hf, 28 + NT * hf, fqT, fkT, fV, fpr, fPT)
            pe.wait_ge(at_done, 28 + NT * (hf + 1))
            pe.wait_ge(at_copied, 96 + 32 * (hf + 1))
            for m in range(4):
                turn([fo_tok[:, t, m * P:(m + 1) * P] for t in range(NT)])
        pe.wait_ge(turn_free, chunk[0])
        phase_end(12)
        rows_out(B_BOUT, (o_high, o_low), bo_out, bo_free, 0)
        phase_end(13)
        turn_norm(6)
        pe.wait_ge(turn_free, chunk[0])
        swiglu(1)
        phase_end(14)

    @block.scalar
    def _(act):
        def phase_end(k):
            act.drain().then_inc(phase_done, 1)
            act.wait_ge(phase_done, 3 * k)

        def split_high(n, slot, uses):
            act.wait_ge(raw_loaded[slot], 32 * uses)
            act.activation(w_high[:, slot, :], raw[:, slot, :], ACT.Copy).then_inc(high_done, 1)

        def ahead(n):
            if n + 2 < N_BLOCKS:
                split_high(n + 2, n % 2, (n + 2) // 2 + 1)

        halves = [0]

        def half_read():
            halves[0] += 1
            act.wait_ge(block_used, halves[0])

        def squares_and_root(r):
            for t in range(NT):
                act.activation(xn[:, t, :], X[:, t, :], ACT.Square, accum_out=ss[:, t:t + 1])\
                   .then_inc(nm_squares, 1)
            act.wait_ge(nm_mean, r + 1)
            act.activation(rms[:, :], msq[:, :], ACT.Sqrt).then_inc(nm_root, 1)

        chunk = [0]
        highs = [0]

        def turned_high(dst, scale=None):
            m = chunk[0]
            chunk[0] += 1
            act.wait_ge(turned, m + 1)
            kw = {} if scale is None else {"scale": scale}
            act.activation(dst, TB[m % 2][:, :], ACT.Copy, **kw).then_inc(turn_high, 1)

        def norm(r, g):
            squares_and_root(r)
            for c in range(KD):
                turned_high(h_high[:, c, :], None if g is None else gcol[:, g, c:c + 1])

        vecs = [(gcol[:, i, :], v) for i, v in enumerate([a["norm1_g"][0], a["norm2_g"][0], a["a_norm_2"][0],
                                                          a["ffn_norm_2"][0], a["b_norm_2"][0], a["ffn_norm_2"][1]])]
        for dst, v in vecs:
            act.dma_start(dst, v.rearrange("(k p) -> p k", p=P), allow_slow_non_contiguous=True).then_inc(vec_loaded, 16)
        act.dma_start(kvg[:, :], a["kv_norm_g"][0].rearrange("(p o) -> p o", o=1)).then_inc(vec_loaded, 16)
        act.dma_start(ids[:, :], a["pairs"]).then_inc(vec_loaded, 16)
        split_high(0, 0, 1)
        split_high(1, 1, 1)
        act.wait_ge(x_loaded, 16)
        squares_and_root(0)
        act.wait_ge(vec_loaded, 16 * 8)
        chunk[0] += 1
        for c in range(KD):
            turned_high(h_high[:, c, :], gcol[:, 0, c:c + 1])

        act.wait_ge(in_out, 4)
        ahead(B_MISC)
        act.wait_ge(ck_mean, 1)
        act.activation(rms[:, :], msq[:, :], ACT.Sqrt).then_inc(act_step, 1)
        act.wait_ge(band_stored, 16)

        def take(j, dst, func):
            act.wait_ge(in_out, j + 1)
            act.activation(dst, G[j % 4][:, :], func).then_inc(in_evac, 1)

        for i in range(2):
            for m in range(2):
                take(4 + 2 * i + m, qT[:, 2 * i + m, :], ACT.Copy)
            ahead(B_Q + i)
        chunk[0] += 2
        for i in range(2):
            for m in range(2):
                take(8 + 2 * i + m, qiT[:, 2 * i + m, :], ACT.Copy)
            ahead(B_QI + i)
        half_read()
        ahead(B_V)
        for t in range(NT):
            take(12 + t, vtok[:, t, :], ACT.Gelu_apprx_tanh)
        ahead(B_V + 1)
        unit = 0
        for qt in range(1, NT):
            for h in range(HH):
                act.wait_ge(ix_scores, unit + 1)
                if unit >= 2:
                    act.wait_ge(ix_added, unit - 1)
                act.activation(sc[:, unit % 2, 0:(qt + 1) * P], SB[unit % 2][:, 0:(qt + 1) * P], ACT.Relu)\
                   .then_inc(ix_relu, 1)
                unit += 1
        for i in range(2):
            for m in range(2):
                take(16 + 2 * i + m, uT[:, 2 * i + m, :], ACT.Gelu_apprx_tanh)
            ahead(B_U + i)
        with act.Fori(0, 4) as it:
            for c in range(2):
                for m in range(2):
                    j = 20 + 2 * c + m
                    act.wait_ge(in_out, 4 * it + j + 1)
                    act.activation(gates[:, bass.ds(4 * it + 2 * c + m, 1), :],
                                   G[j % 4][:, :].rearrange("p (o n) -> p o n", o=1), ACT.Sigmoid)\
                       .then_inc(in_evac, 1)
                n = B_GATES + c
                split_high(None, n % 2, (n + 2) // 2 + 1 + it)
        act.wait_ge(ln_var, 1)
        act.activation(rms[:, :], msq[:, :], ACT.Sqrt).then_inc(ln_root, 1)
        phase_end(1)

        act.wait_ge(g_done, 4)
        for m in range(4):
            act.wait_ge(kv_out, m + 1)
            act.activation(KT[:, m, :], G[m][:, :], ACT.Copy).then_inc(kv_copied, 1)
        for t in range(NT):
            act.wait_ge(kv_out, 5 + t)
            act.activation(V[:, t, :], G[t][:, :], ACT.Copy).then_inc(kv_copied, 1)

        def attend(base, sc_, pr_, pt_):
            def copy(u):
                k = (u // HH + 1) * P
                act.wait_ge(at_turned, base + u + 1)
                act.activation(pt_[:, u % 2, 0:k], TB[u % 2][:, 0:k], ACT.Copy).then_inc(at_copied, 1)

            for u in range(NT * HH):
                k = (u // HH + 1) * P
                act.wait_ge(at_max, base + u + 1)
                act.activation(pr_[:, u % 2, 0:k], sc_[:, u % 2, 0:k], ACT.Exp, bias=nmx[:, u:u + 1],
                               accum_out=rsum[:, u:u + 1]).then_inc(at_prob, 1)
                if u:
                    copy(u - 1)
            copy(NT * HH - 1)

        attend(0, sc, pr, PT)
        for m in range(4):
            turned_high(h_high[:, m, :])
        phase_end(2)

        for b in range(4):
            act.wait_ge(pj_out, 4 * (b + 1))
            ahead(B_PROJ + b)
            if b % 2:
                for m in range(4):
                    c = 4 * (b // 2) + m
                    act.wait_ge(pj_sum, c + 1)
                    act.activation(merged_high[:, c, :], gates[:, c, :], ACT.Copy).then_inc(pj_high, 1)
        phase_end(3)

        def rows_ahead(n0, out, base=0, last=4):
            for half in range(2):
                half_read()
                if 2 * half < last:
                    ahead(n0 + 2 * half)
                act.wait_ge(out, base + 4 * (half + 1))
                if 2 * half + 1 < last:
                    ahead(n0 + 2 * half + 1)

        rows_ahead(B_WOUT, wo_out, 0, 2)
        phase_end(4)

        act.wait_ge(rt_loaded, 64)
        act.activation(rt_high[:, :, :], rt_raw[:, :, :], ACT.Copy).then_inc(rt_high_done, 1)
        norm(1, None)
        act.wait_ge(rt_exp_in, 1)
        act.activation(el[:, :, 0:NG], el[:, :, 0:NG], ACT.Exp).then_inc(rt_exp, 1)
        act.wait_ge(rt_e2_in, 1)
        act.activation(rv[:, 5, :], rv[:, 5, :], ACT.Exp).then_inc(rt_e2, 1)
        phase_end(5)
        m_raws = [m_raw0, m_raw1, m_raw2]

        def m_split(j, b, q):
            act.wait_ge(m_raws[q], (32 if q < 2 else 16) * (j + 1))
            act.activation(m_high[:, b, q, :], m_raw[:, q, :], ACT.Copy).then_inc(m_high_done, 1)

        def x_high(j, b):
            for half in range(2):
                act.wait_ge(m_turned, 2 * j + half + 1)
                act.activation(xt_high[:, b, 4 * half:4 * half + 4, :],
                               TB[half][:, :].rearrange("p (c n) -> p c n", c=4), ACT.Copy).then_inc(m_xhigh, 1)

        def slot(j, b):
            m_split(j + 1, 1 - b, 0)
            m_split(j + 1, 1 - b, 1)
            act.wait_ge(m_gu, j + 1)
            act.activation(sg[:, :], G[b][:, 0:FE], ACT.Silu).then_inc(m_silu, 1)
            x_high(j + 1, 1 - b)
            act.wait_ge(m_he_turned, j + 1)
            act.activation(het_high[:, :, :], SB[0][:, 0:FE].rearrange("p (c n) -> p c n", c=2), ACT.Copy)\
               .then_inc(m_hehigh, 1)
            m_split(j + 1, 1 - b, 2)

        n_trips = act.value_load(trips[0:1, 0:1], min_val=4, max_val=20)
        for q in range(3):
            m_split(0, 0, q)
        x_high(0, 0)
        slot(0, 0)
        slot(1, 1)
        with act.Fori(1, n_trips) as i:
            slot(2 * i, 0)
            slot(2 * i + 1, 1)
        phase_end(6)
        ahead(B_DIL - 2)
        ahead(B_DIL - 1)
        act.wait_ge(dve_summed, 1)
        squares_and_root(2)
        phase_end(7)
        norm(3, 2)
        phase_end(8)
        unit0 = 32
        for v in range(6):
            g = v % 3
            for kind in range(3):
                n = B_DIL + (3 * v + kind) * 2
                half_read()
                ahead(n)
                for t in range(NT):
                    act.wait_ge(dl_out, 12 * v + 4 * kind + t + 1)
                    dst = dV[:, t, :] if kind == 2 else qk[:, 4 * kind + t, :]
                    act.activation(dst, G[t][:, :], ACT.Copy).then_inc(dl_evac, 1)
                ahead(n + 1)
            chunk[0] += 8
            hu = 2 if g == 0 else 4
            w = T // hu
            per_tile = HH // hu
            units = NT * per_tile

            def copy(u):
                act.wait_ge(at_turned, unit0 + u + 1)
                act.activation(dPT[:, u % 2, :], TB[u % 2][:, :], ACT.Copy).then_inc(at_copied, 1)

            for u in range(units):
                act.wait_ge(at_max, unit0 + u + 1)
                for e in range(hu):
                    col = HH * (u // per_tile) + first_head(u % per_tile, hu) + 2 * e
                    last = act.activation(dpr[:, u % 2, e * w:(e + 1) * w], dsc[:, u % 2, e * w:(e + 1) * w],
                                          ACT.Exp, bias=nmx[:, col:col + 1], accum_out=rsum[:, col:col + 1])
                last.then_inc(at_prob, 1)
                if u:
                    copy(u - 1)
            copy(units - 1)
            act.wait_ge(at_prob, unit0 + units)
            if v:
                act.wait_ge(dl_lse_stored, 16 * v)
            act.activation(lse[:, :, :], rsum[:, :].rearrange("p (t h) -> p t h", h=HH), ACT.Ln).then_inc(dl_ln, 1)
            unit0 += units
        phase_end(9)
        act.wait_ge(mg_exp_in, 1)
        act.activation(lse3[:, :, :, :], lse3[:, :, :, :], ACT.Exp).then_inc(mg_exp, 1)
        for c in range(KD):
            turned_high(h_high[:, c, :])
        rows_ahead(B_AOUT, ao_out)
        phase_end(10)

        def swiglu(l):
            for r, chunks in enumerate(FF_ROUNDS):
                n0 = B_FFN[l] + FF_BLOCK[r]
                f0 = 22 * l + FF_CHUNK[r]
                with act.Fori(0, chunks // 2) as i:
                    for c in range(2):
                        f = f0 + c + 2 * i
                        act.wait_ge(ff_out, f + 1)
                        act.activation(silu[:, c, :], G[2 * c][:, :], ACT.Silu).then_inc(ff_silu, 1)
                        split_high(None, (n0 + c) % 2, (n0 + c + 2) // 2 + 1 + i)
                        act.wait_ge(ff_mul, f + 1)
                        act.activation(act_high[:, bass.ds(c + 2 * i, 1), :],
                                       gu[:, c, :].rearrange("p (o n) -> p o n", o=1), ACT.Copy).then_inc(ff_high, 1)
                for half in range(2):
                    n = n0 + chunks + 2 * half
                    half_read()
                    ahead(n)
                    act.wait_ge(ff_down_out, (3 * l + r) * 8 + 4 * (half + 1))
                    ahead(n + 1)

        norm(4, 3)
        swiglu(0)
        phase_end(11)
        act.wait_ge(fo_loaded, 32)
        act.activation(fw_high[:, :, :], fw_raw[:, :, :], ACT.Copy).then_inc(fo_high, 1)
        norm(5, 4)
        act.wait_ge(fo_e_in, 1)
        act.activation(fe[:, :, :], fm[:, :, :], ACT.Exp).then_inc(fo_e, 1)
        act.wait_ge(fo_e, 1)
        act.activation(fe[:, :, :], fe[:, :, :], ACT.Ln, bias=ones_col[:, :]).then_inc(fo_l, 1)
        for hf in range(2):
            for kind in range(3):
                n = B_FOX + 6 * hf + 2 * kind
                if kind == 2:
                    half_read()
                    ahead(n)
                for t in range(4):
                    act.wait_ge(fo_out, 12 * hf + 4 * kind + t + 1)
                    dst = [fqT, fkT, fV][kind][:, t, :]
                    if kind == 0:
                        act.activation(dst, G[t][:, :], ACT.Copy, scale=SCALE).then_inc(fo_evac, 1)
                    else:
                        act.activation(dst, G[t][:, :], ACT.Copy).then_inc(fo_evac, 1)
                    if kind < 2 and t == 1:
                        ahead(n)
                ahead(n + 1)
            attend(96 + 32 * hf, fsc, fpr, fPT)
            for m in range(4):
                turned_high(o_high[:, 4 * hf + m, :])
        phase_end(12)
        rows_ahead(B_BOUT, bo_out)
        phase_end(13)
        norm(6, 5)
        swiglu(1)
        phase_end(14)
        squares_and_root(7)

    @block.vector
    def _(dve):
        def phase_end(k):
            dve.drain().then_inc(phase_done, 1)
            dve.wait_ge(phase_done, 3 * k)

        steps = [0]

        def step(ins):
            steps[0] += 1
            ins.then_inc(dve_step, 1)
            dve.wait_ge(dve_step, steps[0])

        def mul(out, x, y):
            return dve.tensor_tensor(out=out, in0=x, in1=y, op=ALU.mult)

        def add(out, x, y):
            return dve.tensor_tensor(out=out, in0=x, in1=y, op=ALU.add)

        def sub(out, x, y):
            return dve.tensor_tensor(out=out, in0=x, in1=y, op=ALU.subtract)

        chunk = [0]
        highs = [0]

        def turned_low(dst, high, scale=None):
            m = chunk[0]
            chunk[0] += 1
            highs[0] += 1
            dve.wait_ge(turn_high, highs[0])
            if scale is None:
                last = sub(dst, TB[m % 2][:, :], high.bitcast(F32))
            else:
                last = dve.scalar_tensor_tensor(out=dst, in0=TB[m % 2][:, :], scalar=scale,
                                                in1=high.bitcast(F32), op0=ALU.mult, op1=ALU.subtract)
            last.then_inc(turn_free, 1)

        def turned_chunk():
            m = chunk[0]
            chunk[0] += 1
            dve.wait_ge(turned, m + 1)
            return TB[m % 2]

        def norm_rows(r, dst, wide=None):
            dve.wait_ge(nm_squares, NT * (r + 1))
            dve.tensor_scalar(msq[:, :], ss[:, :], 1.0 / D, EPS, ALU.mult, ALU.add).then_inc(nm_mean, 1)
            dve.wait_ge(nm_root, r + 1)
            step(dve.reciprocal(rstd[:, :], rms[:, :]))
            for t in range(NT):
                if wide is None:
                    last = dve.tensor_scalar(dst[:, t, :], X[:, t, :], rstd[:, t:t + 1], None, ALU.mult)
                else:
                    last = dve.scalar_tensor_tensor(out=dst[:, t, :], in0=X[:, t, :], scalar=rstd[:, t:t + 1],
                                                    in1=wide[:, :], op0=ALU.mult, op1=ALU.mult)
                last.then_inc(nm_rows, 1)

        def norm(r, g, wide=None):
            norm_rows(r, xn, wide)
            for c in range(KD):
                turned_low(h_low[:, c, :], h_high[:, c, :], None if g is None else gcol[:, g, c:c + 1])

        dve.memset(ones_col[:, :], 1.0)
        dve.wait_ge(band_vec_loaded, 32)
        dve.tensor_copy(relb_wide[:, :, :], relb[:, :].unsqueeze(2).broadcast_to([32, HH, P]))\
           .then_inc(relb_wide_done, 1)
        for h in range(HH):
            dve.wait_ge(band_psum, h + 1)
            dve.tensor_copy(band[:, h, 0:T], SB[0][:, :]).then_inc(band_copied, 1)
            dve.tensor_copy(band[:, h, T:BAND], SB[1][:, 0:P]).then_inc(band_copied, 1)
        dve.wait_ge(x_loaded, 16)
        norm_rows(0, xn)
        dve.wait_ge(cst_loaded, 16)
        dve.wait_ge(vec_loaded, 16 * 8)
        src = turned_chunk()
        mul(ws_t[:, :, :], src[:, :].rearrange("p (g i) -> p g i", g=4),
            cst[:, C_TRI:C_TRI + P].unsqueeze(1).broadcast_to([P, 4, P])).then_inc(turn_free, 1)
        for c in range(KD):
            turned_low(h_low[:, c, :], h_high[:, c, :], gcol[:, 0, c:c + 1])

        for t in range(NT):
            dve.wait_ge(in_out, t + 1)
            dve.tensor_copy(misc[:, t, 0:192], G[t][:, 0:192])
            dve.tensor_copy(misc[:, t, 192:256], G[t][:, 128:192])
            dve.tensor_scalar(w_idx[:, t, :], G[t][:, 192:200], IDX_SCALE, None, ALU.mult).then_inc(misc_copied, 1)
        dve.wait_ge(misc_copied, NT)
        for t in range(NT):
            last = dve.tensor_tensor_reduce(sc[:, 0, t * P:(t + 1) * P], misc[:, t, 0:P], misc[:, t, 0:P],
                                            1.0, 0.0, ALU.mult, ALU.add, ss[:, t:t + 1])
        step(last)
        dve.tensor_scalar(msq[:, :], ss[:, :], 1.0 / P, EPS, ALU.mult, ALU.add).then_inc(ck_mean, 1)
        dve.wait_ge(act_step, 1)
        step(dve.reciprocal(rstd[:, :], rms[:, :]))
        for t in range(NT):
            last = dve.tensor_scalar(misc[:, t, 0:P], misc[:, t, 0:P], rstd[:, t:t + 1], None, ALU.mult)
        last.then_inc(ck_root, 1)
        src = turned_chunk()
        dve.tensor_scalar(ckvT[:, :], src[:, :], kvg[:, 0:1], None, ALU.mult).then_inc(turn_free, 1)
        src = turned_chunk()
        dve.tensor_copy(kiT[:, :], src[:, :]).then_inc(turn_free, 1)
        unit = 0
        for qt in range(1, NT):
            k = (qt + 1) * P
            for h in range(HH):
                dve.wait_ge(ix_relu, unit + 1)
                w = w_idx[:, qt, h:h + 1]
                if h == 0:
                    last = dve.tensor_scalar(idx[:, qt, 0:k], sc[:, unit % 2, 0:k], w, None, ALU.mult)
                else:
                    dve.wait_ge(ix_added, unit)
                    last = dve.scalar_tensor_tensor(out=idx[:, qt, 0:k], in0=sc[:, unit % 2, 0:k], scalar=w,
                                                    in1=idx[:, qt, 0:k], op0=ALU.mult, op1=ALU.add)
                last.then_inc(ix_added, 1)
                unit += 1
        causal = cst[:, C_CAUSAL + 3 * P:C_CAUSAL + 4 * P]
        dve.tensor_copy(idx[:, 0, 0:P], causal)
        dve.wait_ge(ix_added, unit)
        for qt in range(1, NT):
            k = (qt + 1) * P
            step(add(idx[:, qt, qt * P:k], idx[:, qt, qt * P:k], causal))
            for _ in range(TOPK // 8):
                step(dve.max(max8[:, :], idx[:, qt, 0:k]))
                step(dve.match_replace(idx[:, qt, 0:k], max8[:, :], idx[:, qt, 0:k], TAKEN))
            step(dve.tensor_scalar(idx[:, qt, 0:k], idx[:, qt, 0:k], -2.0e38, NEG, ALU.is_ge, ALU.mult))
        dve.wait_ge(in_evac, 12)
        dve.wait_ge(ln_loaded, 32)
        step(dve.tensor_reduce(out=ln_mean[:, :], in_=vtok[:, :, :], axis=AXX, op=ALU.add))
        step(dve.tensor_scalar(ln_mean[:, :], ln_mean[:, :], 1.0 / HALF, None, ALU.mult))
        step(sub(vtok[:, :, :], vtok[:, :, :], ln_mean[:, :].unsqueeze(2).broadcast_to([P, NT, HALF])))
        for t in range(NT):
            step(dve.tensor_tensor_reduce(sc[:, t % 2, :], vtok[:, t, :], vtok[:, t, :],
                                          1.0, 0.0, ALU.mult, ALU.add, ss[:, t:t + 1]))
        dve.tensor_scalar(msq[:, :], ss[:, :], 1.0 / HALF, EPS, ALU.mult, ALU.add).then_inc(ln_var, 1)
        dve.wait_ge(ln_root, 1)
        step(dve.reciprocal(rstd[:, :], rms[:, :]))
        for t in range(NT):
            last = dve.scalar_tensor_tensor(out=vtok[:, t, :], in0=vtok[:, t, :], scalar=rstd[:, t:t + 1],
                                            in1=lng[:, :], op0=ALU.mult, op1=ALU.mult)
        step(last)
        for t in range(NT):
            add(vtok[:, t, :], vtok[:, t, :], lnb[:, :]).then_inc(ln_done, 1)
        phase_end(1)

        dve.wait_ge(bs_loaded, 16)
        for g in range(4):
            dve.wait_ge(gm_out, g + 1)
            add(sc[:, 0, :].rearrange("p (c i) -> p c i", c=NT), G[g][:, :].rearrange("p (c i) -> p c i", c=NT),
                bs_b[:, g, :].unsqueeze(1).broadcast_to([P, NT, P])).then_inc(gm_free, 1)
            dve.wait_ge(gm_free, g + 1)
            step(mul(sc[:, 1, :], sc[:, 0, :], uT[:, g, :]))
            step(dve.tensor_copy(h_high[:, 4 + g, :], sc[:, 1, :]))
            sub(h_low[:, 4 + g, :], sc[:, 1, :], h_high[:, 4 + g, :].bitcast(F32)).then_inc(g_done, 1)

        def attend(base, tile0, sc_, read, mask, out):
            def tile_end(t):
                dve.wait_ge(at_out, tile0 + t + 1)
                step(dve.reciprocal(rinv[:, HH * t:HH * t + HH], rsum[:, HH * t:HH * t + HH]))
                mul(out[:, t, :].rearrange("p (h d) -> p h d", h=HH),
                    G[t % 2][:, :].rearrange("p (h d) -> p h d", h=HH),
                    rinv[:, HH * t:HH * t + HH].unsqueeze(2).broadcast_to([P, HH, DH])).then_inc(at_done, 1)

            for u in range(NT * HH):
                t, h = divmod(u, HH)
                k = (t + 1) * P
                dve.wait_ge(at_scores, base + u + 1)
                if u >= 2:
                    dve.wait_ge(at_prob, base + u - 1)
                read(sc_[:, u % 2, 0:k], SB[u % 2][:, 0:k], t, h, k).then_inc(at_read, 1)
                dve.wait_ge(at_read, base + u + 1)
                step(dve.tensor_tensor_reduce(sc_[:, u % 2, 0:k], sc_[:, u % 2, 0:k], mask(t, k), 1.0, TAKEN,
                                              ALU.add, ALU.max, mx[:, u:u + 1]))
                dve.tensor_scalar(nmx[:, u:u + 1], mx[:, u:u + 1], -1.0, None, ALU.mult).then_inc(at_max, 1)
                if h == 1 and t:
                    tile_end(t - 1)
            tile_end(NT - 1)

        def read_biased(dst, psum, t, h, k):
            return dve.scalar_tensor_tensor(out=dst, in0=psum, scalar=SCALE, in1=toep[:, h, T - k:T],
                                            op0=ALU.mult, op1=ALU.add)

        dve.wait_ge(toep_loaded, 16 * HH)
        attend(0, 0, sc, read_biased, lambda t, k: idx[:, t, 0:k], o_tok)
        for m in range(4):
            turned_low(h_low[:, m, :], h_high[:, m, :])
        phase_end(2)

        for b in range(4):
            for m in range(4):
                c = 4 * (b // 2) + m
                dve.wait_ge(pj_out, 4 * b + m + 1)
                g = gates[:, c if b % 2 == 0 else KD + c, :]
                mul(g, G[m][:, :], g).then_inc(pj_free, 1)
                if b % 2:
                    dve.wait_ge(pj_free, 4 * b + m + 1)
                    add(gates[:, c, :], gates[:, c, :], g).then_inc(pj_sum, 1)
                    dve.wait_ge(pj_high, c + 1)
                    sub(merged_low[:, c, :], gates[:, c, :], merged_high[:, c, :].bitcast(F32))
        phase_end(3)

        def onto_x(out, free):
            for half in range(2):
                for t in range(NT):
                    dve.wait_ge(out, 4 * half + t + 1)
                    x = X[:, t, 512 * half:512 * half + 512]
                    add(x, G[t][:, :], x).then_inc(free, 1)

        dve.wait_ge(x_again, 16)
        onto_x(wo_out, wo_free)
        phase_end(4)

        dve.wait_ge(rt_high_done, 1)
        sub(rt_low[:, :, :], rt_raw[:, :, :], rt_high[:, :, :].bitcast(F32)).then_inc(rt_low_done, 1)
        dve.wait_ge(gw_loaded, 16)
        norm(1, None, g_wide)
        for t in range(NT):
            dve.wait_ge(rt_out, t + 1)
            last = add(logit[:, t, :], G[t][:, 0:36], rt_bias[:, :])
        step(last)

        def row(i):
            return rv[:, i, :]

        def wide(i, n):
            return rv[:, i, :].unsqueeze(2).broadcast_to([P, NT, n])

        def reduce(out, x, op):
            return dve.tensor_reduce(out=out, in_=x, axis=AXX, op=op)

        def first_max(dst, x, n, i):
            step(reduce(row(i), x, ALU.max))
            step(dve.tensor_tensor(out=dst, in0=x, in1=wide(i, n), op=ALU.is_equal))
            step(mul(dst, dst, cst[:, C_RANK:C_RANK + n].unsqueeze(1).broadcast_to([P, NT, n])))
            step(reduce(row(11), dst, ALU.max))
            step(dve.tensor_tensor(out=dst, in0=dst, in1=wide(11, n), op=ALU.is_equal))

        groups = logit[:, :, 0:NG]
        first_max(goh[:, :, :], groups, NG, 0)
        sub(el[:, :, 0:NG], groups, wide(0, NG)).then_inc(rt_exp_in, 1)
        dve.wait_ge(rt_exp, 1)
        step(reduce(row(1), el[:, :, 0:NG], ALU.add))
        step(dve.reciprocal(row(2), row(1)))
        lg = logit[:, :, NG:36].rearrange("p t (g e) -> p t g e", g=NG)
        r1v = r1[:, :, :].rearrange("p t (g e) -> p t g e", g=NG)
        step(mul(r1v, lg, goh[:, :, :].unsqueeze(3).broadcast_to([P, NT, NG, EPG])))
        step(reduce(el[:, :, :], r1[:, :, :].rearrange("p t (g e) -> p t e g", g=NG), ALU.add))
        first_max(oh[:, 0, :, :], el[:, :, :], EPG, 3)
        step(dve.scalar_tensor_tensor(out=el2[:, :, :], in0=oh[:, 0, :, :], scalar=NEG, in1=el[:, :, :],
                                      op0=ALU.mult, op1=ALU.add))
        first_max(oh[:, 1, :, :], el2[:, :, :], EPG, 4)
        sub(row(5), row(4), row(3)).then_inc(rt_e2_in, 1)
        dve.wait_ge(rt_e2, 1)
        step(dve.tensor_scalar(row(6), row(5), 1.0, None, ALU.add))
        step(dve.reciprocal(row(7), row(6)))
        step(mul(gate_w[:, 0, :], row(7), row(2)))
        step(mul(gate_w[:, 1, :], gate_w[:, 0, :], row(5)))
        for k in range(2):
            pv = pick[:, k, :, :].rearrange("p t (g e) -> p t g e", g=NG)
            step(dve.tensor_copy(pv, goh[:, :, :].unsqueeze(3).broadcast_to([P, NT, NG, EPG])))
            step(mul(pv, pv, oh[:, k, :, :].unsqueeze(2).broadcast_to([P, NT, NG, EPG])))
        add(both[:, :, :], pick[:, 0, :, :], pick[:, 1, :, :]).then_inc(rt_both, 1)
        dve.wait_ge(rt_cum, 1)
        dve.tensor_copy(cum[:, :, :], SB[0][:, 0:NT * NE].rearrange("p (t e) -> p t e", e=NE))
        step(dve.tensor_copy(cnt[:, :], SB[1][:, 0:NE]))
        step(dve.tensor_scalar(ntile[:, :], cnt[:, :], 0.0, None, ALU.is_gt))
        for q in range(1, NT):
            step(dve.scalar_tensor_tensor(out=ntile[:, :], in0=cnt[:, :], scalar=float(q * P), in1=ntile[:, :],
                                          op0=ALU.is_gt, op1=ALU.add))
        step(dve.tensor_copy(scan[:, 0, :], ntile[:, :]))
        w, cur = 1, 0
        while w < NE:
            dve.tensor_copy(scan[:, 1 - cur, 0:w], scan[:, cur, 0:w])
            step(add(scan[:, 1 - cur, w:NE], scan[:, cur, w:NE], scan[:, cur, 0:NE - w]))
            w, cur = 2 * w, 1 - cur
        ends, starts = scan[:, cur, :], scan[:, 1 - cur, :]
        step(sub(starts, ends, ntile[:, :]))
        begin, cut = rv[:, 0:2, :], rv[:, 3:5, :]
        for k in range(2):
            step(mul(r2[:, :, :], pick[:, k, :, :], cum[:, :, :]))
            step(reduce(posf[:, k, :], r2[:, :, :], ALU.add))
            step(mul(r2[:, :, :], pick[:, k, :, :], starts.unsqueeze(1).broadcast_to([P, NT, NE])))
            step(reduce(rv[:, k, :], r2[:, :, :], ALU.add))
        step(dve.tensor_scalar(cut, posf[:, :, :], float(P), None, ALU.is_ge))
        for q in range(2, NT):
            step(dve.scalar_tensor_tensor(out=cut, in0=posf[:, :, :], scalar=float(q * P), in1=cut,
                                          op0=ALU.is_ge, op1=ALU.add))
        step(dve.scalar_tensor_tensor(out=posf[:, :, :], in0=posf[:, :, :], scalar=float(SLOTS), in1=begin,
                                      op0=ALU.mult, op1=ALU.add))
        step(dve.scalar_tensor_tensor(out=posf[:, :, :], in0=cut, scalar=float(1 - P * SLOTS), in1=posf[:, :, :],
                                      op0=ALU.mult, op1=ALU.add))
        dve.tensor_copy(pos[:, :], posf[:, :, :].rearrange("p k t -> p (k t)")).then_inc(rt_pos, 1)
        step(dve.tensor_tensor(out=slotf[:, :, :], in0=ends[0:1, :].unsqueeze(1).broadcast_to([1, SLOTS, NE]),
                               in1=cst[0:1, C_SLOT:C_SLOT + SLOTS].unsqueeze(2).broadcast_to([1, SLOTS, NE]),
                               op=ALU.is_le))
        step(reduce(slote[:, :], slotf[:, :, :], ALU.add))
        step(dve.tensor_scalar(slot_expert[:, :], slote[:, :], float(NE - 1), None, ALU.min))
        step(dve.tensor_scalar(slote[:, 0:20], cst[0:1, C_SLOT:C_SLOT + 40:2], ends[0:1, NE - 1:NE], None, ALU.is_lt))
        step(reduce(posf[0:1, 0, 0:1], slote[:, 0:20], ALU.add))
        dve.tensor_copy(trips[:, :], posf[0:1, 0, 0:1]).then_inc(rt_tables, 1)
        phase_end(5)

        m_scat = [m_scat0, m_scat1]
        m_gath = [m_gath0, m_gath1]

        def low01(j, b, q):
            dve.wait_ge(m_high_done, 3 * j + q + 1)
            sub(m_low[:, b, q, :], m_raw[:, q, :], m_high[:, b, q, :].bitcast(F32)).then_inc(m_low01, 1)

        def x_low(j, b):
            for half in range(2):
                dve.wait_ge(m_xhigh, 2 * j + half + 1)
                c = slice(4 * half, 4 * half + 4)
                sub(xt_low[:, b, c, :], TB[half][:, :].rearrange("p (c n) -> p c n", c=4),
                    xt_high[:, b, c, :].bitcast(F32)).then_inc(m_xlow, 1)

        def slot(j, b, i):
            low01(j + 1, 1 - b, 0)
            low01(j + 1, 1 - b, 1)
            dve.wait_ge(m_silu, j + 1)
            mul(he[:, :], sg[:, :], G[b][:, FE:2 * FE]).then_inc(m_he, 1)
            x_low(j + 1, 1 - b)
            dve.wait_ge(m_hehigh, j + 1)
            sub(het_low[:, :, :], SB[0][:, 0:FE].rearrange("p (c n) -> p c n", c=2),
                het_high[:, :, :].bitcast(F32)).then_inc(m_helow, 1)
            dve.wait_ge(m_down, j + 1)
            if not isinstance(i, int):
                dve.wait_ge(m_scat[b], 16 * i)
            dve.tensor_copy(y_out[:, b, 0:512], G[2][:, :])
            dve.tensor_copy(y_out[:, b, 512:1024], G[3][:, :]).then_inc(m_y, 1)

        n_trips = dve.value_load(trips[0:1, 0:1], min_val=4, max_val=20)
        dve.drain().then_inc(m_y, 1)
        low01(0, 0, 0)
        low01(0, 0, 1)
        x_low(0, 0)
        slot(0, 0, 0)
        slot(1, 1, 0)
        with dve.Fori(1, n_trips) as i:
            slot(2 * i, 0, i)
            slot(2 * i + 1, 1, i)
        for b in range(2):
            dve.wait_ge(m_scat[b], 16 * n_trips)
            dve.tensor_copy(y_out[:, b, 0:1], G[2][:, 0:1])
            dve.wait_ge(m_gath[b], 16 * n_trips + 16)
            dve.tensor_copy(xg[:, b, 0:1], G[2][:, 0:1])
        phase_end(6)
        dve.wait_ge(y_loaded, 32)
        dve.wait_ge(gw1_loaded, 16)
        for k in range(2):
            for t in range(NT):
                last = dve.scalar_tensor_tensor(out=X[:, t, :], in0=y_in[:, k, t, :], scalar=gate_w[:, k, t:t + 1],
                                                in1=X[:, t, :], op0=ALU.mult, op1=ALU.add)
            step(last)
        dve.drain().then_inc(dve_summed, 1)
        norm_rows(2, X, gw1)
        phase_end(7)
        norm(3, 2)
        phase_end(8)
        stored = [dl_stored0, dl_stored1]
        unit0 = 32
        for v in range(6):
            g = v % 3
            order = min(g, 1)
            dve.wait_ge(dl_evac, 12 * v + 8)
            qv = qk[:, :, :].rearrange("p a (h d) -> p a h d", h=HH)
            x1, x2 = qv[:, :, :, 0:8], qv[:, :, :, 8:16]
            cos = cst[:, C_COS + 64 * order:C_COS + 64 * order + 64].rearrange("p (a f) -> p a f", f=8)\
                .unsqueeze(2).broadcast_to([P, 8, 8, 8])
            sin = cst[:, C_SIN + 64 * order:C_SIN + 64 * order + 64].rearrange("p (a f) -> p a f", f=8)\
                .unsqueeze(2).broadcast_to([P, 8, 8, 8])
            mul(rot[:, 0], x1, cos)
            mul(rot[:, 1], x2, sin)
            mul(rot[:, 2], x2, cos)
            step(mul(rot[:, 3], x1, sin))
            sub(x1, rot[:, 0], rot[:, 1])
            add(x2, rot[:, 2], rot[:, 3]).then_inc(dl_rot, 1)
            for m in range(8):
                src = turned_chunk()
                dst = dqT[:, m, :] if m < 4 else dkT[:, m - 4, :]
                dve.tensor_copy(dst, src[:, :]).then_inc(turn_free, 1)
            hu = 2 if g == 0 else 4
            w = T // hu
            per_tile = HH // hu
            units = NT * per_tile

            def tile_end(t):
                dve.wait_ge(at_out, NT * (v + 1) + t + 1)
                step(dve.reciprocal(rinv[:, HH * t:HH * t + HH], rsum[:, HH * t:HH * t + HH]))
                if 2 * v + t // 2:
                    dve.wait_ge(stored[t % 2], 16 * (2 * v + t // 2))
                mul(o_st[:, t % 2, :].rearrange("p (h d) -> p h d", h=HH),
                    G[t % 2][:, :].rearrange("p (h d) -> p h d", h=HH),
                    rinv[:, HH * t:HH * t + HH].unsqueeze(2).broadcast_to([P, HH, DH])).then_inc(at_done, 1)

            for u in range(units):
                t = u // per_tile
                if g == 0:
                    m0 = C_CAUSAL + 3 * P if t else C_NONE
                else:
                    m0 = C_CAUSAL + 3 * P if g == 1 else C_CLASS
                dve.wait_ge(at_scores, unit0 + u + 1)
                if u >= 2:
                    dve.wait_ge(at_prob, unit0 + u - 1)
                view = dsc[:, u % 2, :].rearrange("p (e w) -> p e w", e=hu)
                dve.scalar_tensor_tensor(out=view, in0=SB[u % 2][:, :].rearrange("p (e w) -> p e w", e=hu),
                                         scalar=SCALE, in1=cst[:, m0:m0 + w].unsqueeze(1).broadcast_to([P, hu, w]),
                                         op0=ALU.mult, op1=ALU.add).then_inc(at_read, 1)
                dve.wait_ge(at_read, unit0 + u + 1)
                c0 = HH * t + first_head(u % per_tile, hu)
                cols = slice(c0, c0 + 2 * hu - 1, 2)
                step(dve.tensor_reduce(out=mx[:, cols], in_=view, axis=AXX, op=ALU.max))
                dve.tensor_scalar(nmx[:, cols], mx[:, cols], -1.0, None, ALU.mult)\
                   .then_inc(at_max, 1)
                if u % per_tile == 1 and t:
                    tile_end(t - 1)
            tile_end(NT - 1)
            dve.wait_ge(dl_ln, v + 1)
            add(lse[:, :, :], lse[:, :, :], mx[:, :].rearrange("p (t h) -> p t h", h=HH)).then_inc(dl_lse, 1)
            unit0 += units
        phase_end(9)
        dve.wait_ge(mg_lse_loaded, 48)
        step(dve.tensor_tensor(out=lmax[:, :, :], in0=lse3[:, 0], in1=lse3[:, 1], op=ALU.max))
        step(dve.tensor_tensor(out=lmax[:, :, :], in0=lmax[:, :, :], in1=lse3[:, 2], op=ALU.max))
        for g in range(3):
            last = sub(lse3[:, g], lse3[:, g], lmax[:, :, :])
        last.then_inc(mg_exp_in, 1)
        dve.wait_ge(mg_exp, 1)
        step(add(lmax[:, :, :], lse3[:, 0], lse3[:, 1]))
        step(add(lmax[:, :, :], lmax[:, :, :], lse3[:, 2]))
        step(dve.reciprocal(lmax[:, :, :], lmax[:, :, :]))
        for g in range(3):
            last = mul(lse3[:, g], lse3[:, g], lmax[:, :, :])
        step(last)
        for t in range(NT):
            dve.wait_ge([mg_og0, mg_og1][t % 2], 16 * (t // 2 + 1))
            for g in range(3):
                o = og[:, t % 2, g, :].rearrange("p (h d) -> p h d", h=16)
                last = mul(o, o, lse3[:, g, t, :].unsqueeze(2).broadcast_to([P, 16, DH]))
            step(last)
            step(add(xn[:, t, :], og[:, t % 2, 0, :], og[:, t % 2, 1, :]))
            add(xn[:, t, :], xn[:, t, :], og[:, t % 2, 2, :]).then_inc(mg_done, 1)
        for c in range(KD):
            turned_low(h_low[:, c, :], h_high[:, c, :])
        onto_x(ao_out, ao_free)
        phase_end(10)

        def swiglu(l):
            for r, chunks in enumerate(FF_ROUNDS):
                f0 = 22 * l + FF_CHUNK[r]
                with dve.Fori(0, chunks // 2) as i:
                    for c in range(2):
                        f = f0 + c + 2 * i
                        dve.wait_ge(ff_silu, f + 1)
                        mul(gu[:, c, :], silu[:, c, :], G[2 * c + 1][:, :]).then_inc(ff_mul, 1)
                        dve.wait_ge(ff_high, f + 1)
                        sub(act_low[:, bass.ds(c + 2 * i, 1), :], gu[:, c, :].rearrange("p (o n) -> p o n", o=1),
                            act_high[:, bass.ds(c + 2 * i, 1), :].bitcast(F32)).then_inc(ff_low, 1)
                for half in range(2):
                    outs = bank[4:8] if half == 0 else bank[0:4]
                    for t in range(NT):
                        dve.wait_ge(ff_down_out, (3 * l + r) * 8 + 4 * half + t + 1)
                        x = X[:, t, 512 * half:512 * half + 512]
                        add(x, outs[t][:, :], x).then_inc(ff_down_free, 1)

        norm(4, 3)
        swiglu(0)
        phase_end(11)
        dve.wait_ge(fo_high, 1)
        sub(fw_low[:, :, :], fw_raw[:, :, :], fw_high[:, :, :].bitcast(F32)).then_inc(fo_lowd, 1)
        norm(5, 4)
        dve.wait_ge(fo_logit, 1)
        step(add(fz[:, :, :], SB[0][:, 0:64].rearrange("p (t h) -> p t h", h=16),
                 fb[:, :].unsqueeze(1).broadcast_to([P, NT, 16])))
        dve.scalar_tensor_tensor(out=fm[:, :, :], in0=fz[:, :, :], scalar=-1.0, in1=fz[:, :, :],
                                 op0=ALU.mult, op1=ALU.min).then_inc(fo_e_in, 1)
        dve.wait_ge(fo_l, 1)
        dve.scalar_tensor_tensor(out=fz[:, :, :], in0=fz[:, :, :], scalar=0.0, in1=fe[:, :, :],
                                 op0=ALU.min, op1=ALU.subtract).then_inc(fo_f, 1)
        dve.wait_ge(fo_c, 1)
        dve.tensor_copy(c_tok[:, :, :], SB[1][:, 0:64].rearrange("p (t h) -> p t h", h=16)).then_inc(fo_ct, 1)
        dve.wait_ge(fo_sel, 1)
        step(dve.tensor_copy(cT[:, :], SB[0][0:16, :]))
        for hf in range(2):
            for h in range(HH):
                n = HH * hf + h
                if n:
                    dve.wait_ge(fo_ncb, n)
                dve.tensor_copy(sel16[:, :], cst[0:16, C_IDENT + n:C_IDENT + n + 1].broadcast_to([16, P]))\
                   .then_inc(fo_nc, 1)
                dve.wait_ge(fo_ncb, n + 1)
                last = dve.tensor_scalar(ncb[:, h, :], SB[h % 2][:, :], -1.0, None, ALU.mult)
            last.then_inc(fo_nc, 1)
            dve.wait_ge(fo_nc, (HH + 1) * (hf + 1))

            def read_decayed(dst, psum, t, h, k, hf=hf):
                n = HH * hf + h
                return dve.scalar_tensor_tensor(out=dst, in0=ncb[:, h, 0:k], scalar=c_tok[:, t, n:n + 1],
                                                in1=psum, op0=ALU.add, op1=ALU.add)

            attend(96 + 32 * hf, 28 + NT * hf, fsc, read_decayed,
                   lambda t, k: cst[:, C_CAUSAL + T - k:C_CAUSAL + T], fo_tok)
            for m in range(4):
                turned_low(o_low[:, 4 * hf + m, :], o_high[:, 4 * hf + m, :])
        phase_end(12)
        onto_x(bo_out, bo_free)
        phase_end(13)
        norm(6, 5)
        swiglu(1)
        phase_end(14)
        dve.wait_ge(gw2_loaded, 16)
        norm_rows(7, xn, gw2)

    @block.gpsimd
    def _(pool):
        def split_low(n, slot):
            pool.wait_ge(high_done, n + 1)
            pool.tensor_tensor(out=w_low[:, slot, :], in0=raw[:, slot, :], in1=w_high[:, slot, :].bitcast(F32),
                               op=ALU.subtract).then_inc(low_done, 1)

        def split_pairs(n0, pairs):
            with pool.Fori(0, pairs) as i:
                for c in range(2):
                    split_low(n0 + c + 2 * i, (n0 + c) % 2)

        split_pairs(0, 12)
        split_low(24, 0)
        pool.wait_ge(phase_done, 3 * 4)
        pool.memset(empty[:, :], OOB).then_inc(rt_empty, 1)
        pool.wait_ge(empty_stored, 16)
        pool.wait_ge(rt_pos, 1)
        pool.wait_ge(vec_loaded, 16 * 8)
        for c in range(2 * NT):
            pool.indirect_dma_start(out=d_list, out_offset=bass.IndirectOffsetOnAxis(ap=pos[:, c:c + 1], axis=0),
                                    in_=ids[:, c:c + 1], in_offset=None).then_inc(list_stored, 16)
        m_gath = [m_gath0, m_gath1]
        m_scat = [m_scat0, m_scat1]
        pool.wait_ge(phase_done, 3 * 5)
        pool.wait_ge(list_loaded, 16)
        pool.wait_ge(rows_stored, 32)
        pool.memset(xg[:, :, :], 0.0).then_inc(m_idx, 1)

        def column(j):
            return slot_rows[:, j:j + 1] if isinstance(j, int) else slot_rows[:, bass.ds(j, 1)]

        def gather(j, b, copies):
            pool.tensor_copy(gather_rows[:, b:b + 1], column(j)).then_inc(m_idx, 1)
            pool.wait_ge(m_idx, copies)
            pool.indirect_dma_start(out=xg[:, b, :], out_offset=None, in_=d_rows,
                                    in_offset=bass.IndirectOffsetOnAxis(ap=gather_rows[:, b:b + 1], axis=0),
                                    bounds_check=2 * T - 1 + j, oob_is_err=False).then_inc(m_gath[b], 16)

        def scatter(j, b, copies):
            pool.tensor_copy(scatter_rows[:, b:b + 1], column(j)).then_inc(m_idx, 1)
            pool.wait_ge(m_idx, copies)
            pool.indirect_dma_start(out=d_y, out_offset=bass.IndirectOffsetOnAxis(ap=scatter_rows[:, b:b + 1], axis=0),
                                    in_=y_out[:, b, :], in_offset=None,
                                    bounds_check=2 * T - 1 + j, oob_is_err=False).then_inc(m_scat[b], 16)

        def low2(j, b):
            pool.wait_ge(m_high_done, 3 * j + 3)
            pool.tensor_tensor(out=m_low[:, b, 2, :], in0=m_raw[:, 2, :], in1=m_high[:, b, 2, :].bitcast(F32),
                               op=ALU.subtract).then_inc(m_low2, 1)

        def slot(j, b):
            low2(j + 1, 1 - b)
            pool.wait_ge(m_y, j + 2)
            scatter(j, b, 2 * j + 4)
            pool.wait_ge(m_turned, 2 * j + 2)
            gather(j + 2, b, 2 * j + 5)

        n_trips = pool.value_load(trips[0:1, 0:1], min_val=4, max_val=20)
        gather(0, 0, 2)
        gather(1, 1, 3)
        low2(0, 0)
        slot(0, 0)
        slot(1, 1)
        with pool.Fori(1, n_trips) as i:
            slot(2 * i, 0)
            slot(2 * i + 1, 1)
        split_low(B_DIL, B_DIL % 2)
        split_low(B_DIL + 1, (B_DIL + 1) % 2)
        for v in range(6):
            hf, g = divmod(v, 3)
            split_pairs(B_DIL + 2 + 6 * v, 3)
            for t in range(NT):
                cols = slice(HALF * hf, HALF * hf + HALF)
                dst = d_o[g, t * P:(t + 1) * P, cols] if g == 0 else d_o[g, t:T:NT, cols]
                pool.wait_ge(at_done, NT * (v + 1) + t + 1)
                pool.dma_start(dst, o_st[:, t % 2, :]).then_inc([dl_stored0, dl_stored1][t % 2], 16)
            heads = slice(HH * hf, HH * hf + HH)
            pool.wait_ge(dl_lse, v + 1)
            dst = d_lse[g].rearrange("(t p) h -> p t h" if g == 0 else "(p t) h -> p t h", t=NT)
            pool.dma_start(dst[:, :, heads], lse[:, :, :]).then_inc(dl_lse_stored, 16)
        split_pairs(B_AOUT + 2, (N_BLOCKS - B_AOUT - 2) // 2)

    ctx.close()


_INPUTS = """x w_in kv_norm_g w_uk w_uv rel_bias ln_v_g ln_v_b w_spatial b_spatial w_proj_a w_proj_b w_out
    norm1_g norm2_g router_group_w router_group_b router_expert_w router_expert_b w_gate w_up w_down
    final_norm_g a_norm_2 a_w_in_2 a_w_out_2 b_norm_2 b_w_in_2 b_f_2 b_w_out_2 ffn_norm_2 ffn_w_gu_2
    ffn_w_down_2 final_norm_2""".split()


def _tables():
    import numpy as np

    f = np.float32
    p, q = np.arange(P)[:, None], np.arange(P)[None, :]
    neg = f(NEG)
    tab = np.zeros((P, C_COLS), f)
    tab[:, C_IDENT:C_IDENT + P] = np.eye(P, dtype=f)
    causal = np.where(q <= p, f(0), neg)
    tab[:, C_CAUSAL + 3 * P:C_CAUSAL + 4 * P] = causal
    tab[:, C_PREV:C_PREV + P] = np.where(q >= p, f(0), neg)
    tab[:, C_CLASS:C_CLASS + P] = np.where((q <= p) & (q % 4 == p % 4), f(0), neg)
    tab[:, C_NONE:C_NONE + P] = neg
    tab[:, C_NONE + P:C_NONE + 2 * P] = causal
    tab[:, C_TRI:C_TRI + P] = p <= q
    tab[:, C_TRIS:C_TRIS + P] = p < q
    tab[:, C_ONES:C_ONES + P] = 1
    tab[:, C_RANK:C_RANK + 8] = 8 - np.arange(8)
    tab[:, C_SLOT:C_SLOT + SLOTS] = np.arange(SLOTS)
    freq = f(500000.0) ** (-np.arange(8, dtype=f) * f(2.0) / f(16))
    for order in range(2):
        for tile in range(NT):
            pos = np.arange(P) + P * tile if order == 0 else tile + NT * np.arange(P)
            ang = pos.astype(f)[:, None] * freq[None, :]
            for kind in range(2):
                c = 64 * order + 8 * (NT * kind + tile)
                tab[:, C_COS + c:C_COS + c + 8] = np.cos(ang)
                tab[:, C_SIN + c:C_SIN + c + 8] = np.sin(ang)
    n = np.maximum(T - 1 - np.arange(BAND), 0)
    large = 16 + (np.log(np.maximum(n, 1).astype(f) / 16) / f(np.log(128 / 16)) * 16).astype(np.int32)
    bucket = np.where(n < 16, n, np.minimum(large, 31))
    buckets = (np.arange(32)[:, None] == bucket[None, :]).astype(f)
    pairs = (np.arange(2 * T).reshape(2 * NT, P).T).astype(np.int32)
    return {"table": tab, "buckets": buckets, "pairs": np.ascontiguousarray(pairs)}


def kernel(**inputs):
    import numpy as np
    import concourse.bacc as bacc
    from concourse.bass_utils import run_bass_kernel_spmd

    nc = bacc.Bacc("TRN2", target_bir_lowering=False, num_devices=1)
    arrays, a = {}, {}
    for name, value in [(n, inputs[n]) for n in _INPUTS] + list(_tables().items()):
        value = np.ascontiguousarray(value)
        arrays["in_" + name] = value
        a[name] = nc.dram_tensor("in_" + name, value.shape, mybir.dt.from_np(value.dtype),
                                          kind="ExternalInput").ap()
    a["out"] = nc.dram_tensor("out", (1, T, D), F32, kind="ExternalOutput").ap()
    two_blocks_kernel(nc, a)
    r = run_bass_kernel_spmd(nc, [arrays], core_ids=[0])
    return r.results[0]["out"]
```

```python
import concourse.bass as bass
from concourse import mybir
from contextlib import ExitStack

F32 = mybir.dt.float32
F32R = mybir.dt.float32r
I32 = mybir.dt.int32
ALU = mybir.AluOpType
ACT = mybir.ActivationFunctionType
AXX = mybir.AxisListType.X

P = 128
T = 512
NT = T // P
D = 1024
KD = D // P
HALF = 512
HH = 8
DH = 64
NE = 32
NG = 4
EPG = NE // NG
FE = 256
FF = 2816
EPS = 1e-6
TOPK = 128
NEG = -1.0e30
TAKEN = -3.0e38
SCALE = DH ** -0.5
IDX_SCALE = (8 ** -0.5) * (64 ** -0.5)
BAND = T + P
R = 64
SLOTS = 50
TRIPS = SLOTS // 2 - 1
OOB = 4096

C_IDENT = 0
C_CAUSAL = 128
C_PREV = 640
C_CLASS = 768
C_NONE = 896
C_TRI = 1152
C_TRIS = 1280
C_ONES = 1408
C_RANK = 1536
C_SLOT = 1544
C_COS = C_SLOT + SLOTS
C_SIN = C_COS + 128
C_COLS = C_SIN + 128

B_MISC, B_Q, B_QI, B_V, B_U, B_GATES = 0, 1, 3, 5, 7, 9
B_PROJ = 17
B_WOUT = 21
B_DIL = 25
B_AOUT = 61
B_FFN = [65, 115]
B_FOX = 99
B_BOUT = 111
N_BLOCKS = 149
FF_ROUNDS = [8, 8, 6]
FF_CHUNK = [0, 8, 16]
FF_BLOCK = [0, 12, 24]
NORM_IN, NORM_MOE, NORM_A, NORM_F0, NORM_B, NORM_F1 = range(6)


def two_blocks_kernel(nc, a):
    ctx = ExitStack()

    def at(name, kb, shape, dt=F32):
        return nc.alloc_sbuf_tensor_at(name, shape, dt, offset=int((kb + 16) * 1024))

    X = at("X", 1, [P, NT, D])
    cst = at("cst", 17, [P, C_COLS])
    cursor = [40 * 1024 + 512]

    def small(name, shape, dt=F32):
        size = 4
        for n in shape[1:]:
            size *= n
        t = nc.alloc_sbuf_tensor_at(name, shape, dt, offset=cursor[0])
        cursor[0] += -(-size // 32) * 32
        return t

    gcol = small("gcol", [P, 6, KD])
    ones_col = small("ones_col", [P, 1])
    ss = small("ss", [P, NT])
    msq = small("msq", [P, NT])
    rms = small("rms", [P, NT])
    rstd = small("rstd", [P, NT])
    ids = small("ids", [P, 2 * NT], I32)
    gate_w = small("gate_w", [P, 2, NT])
    slot_rows = small("slot_rows", [R, SLOTS], I32)
    slot_expert = small("slot_expert", [1, SLOTS], I32)
    trips = small("trips", [1, 2], I32)
    gather_rows = small("gather_rows", [R, 2], I32)
    scatter_rows = small("scatter_rows", [R, 2], I32)
    w_idx = small("w_idx", [P, NT, HH])
    kvg = small("kvg", [P, 1])
    mx = small("mx", [P, 32])
    nmx = small("nmx", [P, 32])
    rsum = small("rsum", [P, 32])
    rinv = small("rinv", [P, 32])
    lse = small("lse", [P, NT, HH])
    ln_mean = small("ln_mean", [P, NT])
    ln_sum = small("ln_sum", [P, NT])
    max8 = small("max8", [P, 8])
    lse3 = small("lse3", [P, 3, NT, 16])
    lmax = small("lmax", [P, NT, 16])
    assert cursor[0] <= 45 * 1024
    raw = at("raw", 29, [P, 2, 2048])
    w_high = at("w_high", 45, [P, 2, 2048], F32R)
    w_low = at("w_low", 61, [P, 2, 2048], F32R)
    h_high = at("h_high", 77, [P, KD, T], F32R)
    h_low = at("h_low", 93, [P, KD, T], F32R)
    AR = 109
    xn = at("xn", AR + 80, [P, NT, D])
    band = at("band", AR + 16, [P, HH, BAND])
    qT = at("qT", AR, [P, 4, T])
    qiT = at("qiT", AR + 8, [P, 4, T])
    PT = at("PT", AR + 94, [P, 2, T])
    bs_b = at("bs_b", AR + 61, [P, 4, P])
    uT = at("uT", AR + 16, [P, 4, T])
    vtok = at("vtok", AR + 24, [P, NT, HALF])
    KT = at("KT", AR + 8, [P, 4, T])
    V = at("V", AR + 24, [P, NT, HALF])
    merged_high = at("merged_high", AR, [P, KD, T], F32R)
    merged_low = at("merged_low", AR + 16, [P, KD, T], F32R)
    gates = at("gates", AR + 32, [P, 2 * KD, T])
    toep = at("toep", AR + 64, [P, HH, T])
    lng = at("lng", AR + 48, [P, HALF])
    lnb = at("lnb", AR + 50, [P, HALF])
    ws_raw = at("ws_raw", AR + 52, [P, 4, P])
    relb = at("relb", AR + 54, [32, HH])
    relb_wide = at("relb_wide", AR + 54.25, [32, HH, P])
    onehot = at("onehot", AR + 58.5, [32, BAND])
    idx = at("idx", AR + 80, [P, NT, T])
    sc = at("sc", AR + 88, [P, 3, T])
    misc = at("misc", AR + 92, [P, NT, 256])
    ws_t = at("ws_t", AR + 96, [P, 4, P])
    o_tok = at("o_tok", 1, [P, NT, HALF])
    ckvT = at("ckvT", 9, [P, T])
    kiT = at("kiT", 11, [P, T])
    w_uk = at("w_uk_s", 13, [P, HALF])
    w_uv = at("w_uv_s", 15, [P, HALF])
    g_wide = at("g_wide", AR + 64, [P, D])
    rt_raw = at("rt_raw", AR + 68, [P, KD, 36])
    rt_split = at("rt_split", AR + 70, [P, KD, 72], F32R)
    rt_bias = at("rt_bias", AR + 74, [P, 36])
    logit = at("logit", AR + 10.25, [P, NT, 36])
    r1 = at("r1", AR + 11, [P, NT, NE])
    r2 = at("r2", AR + 11.5, [P, NT, NE])
    pick = at("pick", AR + 12, [P, 2, NT, NE])
    both = at("both", AR + 13, [P, NT, NE])
    goh = at("goh", AR + 13.5, [P, NT, NG])
    el = at("el", AR + 13.75, [P, NT, EPG])
    el2 = at("el2", AR + 14, [P, NT, EPG])
    oh = at("oh", AR + 14.25, [P, 2, NT, EPG])
    rv = at("rv", AR + 14.75, [P, 12, NT])
    ntile = at("ntile", AR + 15, [P, NE])
    scan = at("scan", AR + 15.25, [P, 2, NE])
    posf = at("posf", AR + 15.5, [P, 2, NT])
    pos = at("pos", AR + 15.75, [P, 2 * NT], I32)
    cum = at("cum", AR + 16, [P, NT, NE])
    slotf = at("slotf", AR + 16.5, [1, SLOTS, NE])
    slote = at("slote", AR + 23, [1, SLOTS])
    cnt = at("cnt", AR + 23.25, [P, NE])
    empty = at("empty", AR + 23.5, [R, SLOTS], I32)
    m_w = at("m_w", 77, [P, 2, 3, 2048])
    xg = at("xg", 149, [R, 2, D])
    xt = at("xt", 157, [P, 2, KD, R])
    y_out = at("y_out", 161, [R, 2, D])
    sg = at("sg", 169, [R, FE])
    he = at("he", 170, [R, FE])
    het = at("het", 171, [P, 2, R])
    y_in = at("y_in", AR, [P, 2, NT, D])
    gw1 = at("gw1", AR + 64, [P, D])
    gw2 = at("gw2", AR + 64, [P, D])
    qk = at("qk", AR, [P, 8, HALF])
    dqT = at("dqT", AR + 16, [P, 4, T])
    dkT = at("dkT", AR + 24, [P, 4, T])
    o_st = at("o_st", AR + 32, [P, NT, HALF])
    dV = at("dV", AR + 64, [P, 2, NT, HALF])
    rot = at("rot", AR + 40, [P, 4, 8, 8, 8])
    dsc = at("dsc", AR + 48, [P, 3, T])
    dPT = at("dPT", AR + 54, [P, 3, T])
    og = at("og", AR, [P, NT, 2, D])
    act_high = at("act_high", AR, [P, 8, T], F32R)
    act_low = at("act_low", AR + 16, [P, 8, T], F32R)
    silu = at("silu", AR + 32, [P, 2, T])
    gu = at("gu", AR + 36, [P, 2, T])
    fqT = [at("fqT0", AR, [P, 4, T]), at("fqT1", AR + 40, [P, 4, T])]
    fkT = [at("fkT0", AR + 8, [P, 4, T]), at("fkT1", AR + 48, [P, 4, T])]
    fV = [at("fV0", AR + 16, [P, NT, HALF]), at("fV1", AR + 56, [P, NT, HALF])]
    ncb = at("ncb", AR + 24, [P, HH, T])
    o_high, o_low = h_high, h_low
    fo_tok = at("fo_tok", AR + 72, [P, NT, HALF])
    fsc = at("fsc", AR + 80, [P, 3, T])
    fPT = at("fPT", AR + 86, [P, 2, T])
    fw_raw = at("fw_raw", AR + 24, [P, KD, 16])
    fw_split = at("fw_split", AR + 24.5, [P, KD, 32], F32R)
    fb = at("fb", AR + 25.5, [P, 16])
    fz = at("fz", AR + 93.75, [P, NT, 16])
    fm = at("fm", AR + 94, [P, NT, 16])
    fe = at("fe", AR + 94.25, [P, NT, 16])
    c_tok = at("c_tok", AR + 94.5, [P, NT, 16])
    cT = at("cT", AR + 94.75, [16, T])
    sel16 = at("sel16", AR + 96.75, [16, 2, P])

    d_band = nc.dram_tensor("d_band", [HH, P * BAND], F32, kind="Internal").ap()
    d_rows = nc.dram_tensor("d_rows", [2 * T, D], F32, kind="Internal").ap()
    d_y = nc.dram_tensor("d_y", [2 * T, D], F32, kind="Internal").ap()
    d_list = nc.dram_tensor("d_list", [SLOTS * R, 1], I32, kind="Internal").ap()
    d_o = nc.dram_tensor("d_o", [2, T, D], F32, kind="Internal").ap()
    d_lse = nc.dram_tensor("d_lse", [3, T, 16], F32, kind="Internal").ap()

    bank = [ctx.enter_context(nc.psum_tensor(f"bank{i}", [P, 512], F32)) for i in range(8)]
    G = bank[0:4]
    TB = bank[4:6]
    SB = bank[6:8]
    S3 = [bank[6], bank[7], bank[2]]
    T3 = [bank[4], bank[5], bank[3]]

    ident = cst[:, C_IDENT:C_IDENT + P]
    ones = cst[:, C_ONES:C_ONES + P]
    def sem(name):
        return ctx.enter_context(nc.semaphore(name))

    tile0_loaded = sem("tile0_loaded")
    tile1_loaded = sem("tile1_loaded")
    tile2_loaded = sem("tile2_loaded")
    tile3_loaded = sem("tile3_loaded")
    cst_loaded = sem("cst_loaded")
    vec_loaded = sem("vec_loaded")
    band_vec_loaded = sem("band_vec_loaded")
    raw0 = sem("raw0")
    raw1 = sem("raw1")
    high_done = sem("high_done")
    low_done = sem("low_done")
    block_used = sem("block_used")
    phase_done = sem("phase_done")
    dve_step = sem("dve_step")
    act_step = sem("act_step")
    nm_squares = sem("nm_squares")
    nm_mean = sem("nm_mean")
    nm_root = sem("nm_root")
    nm_rows = sem("nm_rows")
    turned = sem("turned")
    turn_high = sem("turn_high")
    turn_free = sem("turn_free")
    relb_wide_done = sem("relb_wide_done")
    band_psum = sem("band_psum")
    band_copied = sem("band_copied")
    band_stored = sem("band_stored")
    toep_loaded = sem("toep_loaded")
    in_out = sem("in_out")
    misc_copied = sem("misc_copied")
    in_evac = sem("in_evac")
    ln_loaded = sem("ln_loaded")
    ck_mean = sem("ck_mean")
    ck_root = sem("ck_root")
    uk_loaded = sem("uk_loaded")
    ix_scores = sem("ix_scores")
    ix_relu = sem("ix_relu")
    ix_added = sem("ix_added")
    ln_var = sem("ln_var")
    ln_root = sem("ln_root")
    ln_done = sem("ln_done")
    bs_loaded = sem("bs_loaded")
    ws_loaded = sem("ws_loaded")
    gm_out = sem("gm_out")
    gm_free = sem("gm_free")
    kv_out = sem("kv_out")
    kv_copied = sem("kv_copied")
    g_done = sem("g_done")
    at_scores = sem("at_scores")
    at_read = sem("at_read")
    at_max = sem("at_max")
    at_prob = sem("at_prob")
    at_turned = sem("at_turned")
    at_copied = sem("at_copied")
    at_out = sem("at_out")
    at_done = sem("at_done")
    x_again = sem("x_again")
    pj_out = sem("pj_out")
    pj_free = sem("pj_free")
    pj_sum = sem("pj_sum")
    pj_high = sem("pj_high")
    pj_low = sem("pj_low")
    wo_out = sem("wo_out")
    wo_free = sem("wo_free")
    rows_stored = sem("rows_stored")
    gw_loaded = sem("gw_loaded")
    rt_loaded = sem("rt_loaded")
    rt_high_done = sem("rt_high_done")
    rt_low_done = sem("rt_low_done")
    rt_out = sem("rt_out")
    rt_exp_in = sem("rt_exp_in")
    rt_exp = sem("rt_exp")
    rt_e2_in = sem("rt_e2_in")
    rt_e2 = sem("rt_e2")
    rt_both = sem("rt_both")
    rt_cum = sem("rt_cum")
    rt_pos = sem("rt_pos")
    rt_empty = sem("rt_empty")
    empty_stored = sem("empty_stored")
    list_stored = sem("list_stored")
    list_loaded = sem("list_loaded")
    rt_tables = sem("rt_tables")
    m_up00 = sem("m_up00")
    m_up01 = sem("m_up01")
    m_up10 = sem("m_up10")
    m_up11 = sem("m_up11")
    m_dn0 = sem("m_dn0")
    m_dn1 = sem("m_dn1")
    m_gath0 = sem("m_gath0")
    m_gath1 = sem("m_gath1")
    m_scat0 = sem("m_scat0")
    m_scat1 = sem("m_scat1")
    m_turned = sem("m_turned")
    m_xt = sem("m_xt")
    m_het = sem("m_het")
    m_gu = sem("m_gu")
    m_silu = sem("m_silu")
    m_he = sem("m_he")
    m_he_turned = sem("m_he_turned")
    m_down = sem("m_down")
    m_y = sem("m_y")
    m_idx = sem("m_idx")
    y_summed = sem("y_summed")
    dl_out = sem("dl_out")
    dl_evac = sem("dl_evac")
    dl_rot = sem("dl_rot")
    dl_stored0 = sem("dl_stored0")
    dl_stored1 = sem("dl_stored1")
    dl_ln = sem("dl_ln")
    dl_lse = sem("dl_lse")
    dl_lse_stored = sem("dl_lse_stored")
    mg_lse_loaded = sem("mg_lse_loaded")
    mg_exp_in = sem("mg_exp_in")
    mg_exp = sem("mg_exp")
    mg_weights = sem("mg_weights")
    mg_third = sem("mg_third")
    mg_done = sem("mg_done")
    ao_out = sem("ao_out")
    ao_free = sem("ao_free")
    ff_out = sem("ff_out")
    ff_silu = sem("ff_silu")
    ff_mul = sem("ff_mul")
    ff_high = sem("ff_high")
    ff_low = sem("ff_low")
    ff_down_out = sem("ff_down_out")
    ff_down_free = sem("ff_down_free")
    fo_loaded = sem("fo_loaded")
    fo_high = sem("fo_high")
    fo_lowd = sem("fo_lowd")
    fo_logit = sem("fo_logit")
    fo_e_in = sem("fo_e_in")
    fo_e = sem("fo_e")
    fo_l = sem("fo_l")
    fo_f = sem("fo_f")
    fo_c = sem("fo_c")
    fo_ct = sem("fo_ct")
    fo_sel = sem("fo_sel")
    fo_nc = sem("fo_nc")
    fo_ncb = sem("fo_ncb")
    fo_out = sem("fo_out")
    fo_evac = sem("fo_evac")
    bo_out = sem("bo_out")
    bo_free = sem("bo_free")
    gw1_loaded = sem("gw1_loaded")
    gw2_loaded = sem("gw2_loaded")
    out_stored = sem("out_stored")
    raw_loaded = [raw0, raw1]
    tile_loaded = [tile0_loaded, tile1_loaded, tile2_loaded, tile3_loaded]
    m_up = [[m_up00, m_up01], [m_up10, m_up11]]
    m_dn = [m_dn0, m_dn1]
    block = ctx.enter_context(nc.Block())

    def shaped(t, slot, k):
        return t[:, slot, :].rearrange("p (k n) -> p k n", k=k)

    TWO_NORMS = [(0, 0), (0, 1), (1, 0), (0, 2), (1, 1), (0, 3), (1, 2), (1, 3)]

    def first_head(q, heads):
        return q if heads == 4 else 4 * (q // 2) + q % 2

    def units_after(v):
        return [1, 1, 1, 2, 1, 1, 1, 2, 1, 1, 1, 3] if v % 3 == 0 else [1, 0, 0, 2, 0, 0, 1, 2, 0, 0, 0, 2]

    GATE_UNITS = [3] * 8

    FOX_UNITS = [[2, 3, 2, 4, 2, 3, 2, 4, 2, 3, 2, 3], [3, 3, 3, 5] * 2]

    def tokens(t, chunk, tile, order):
        if order == 0:
            return t[:, chunk, tile * P:(tile + 1) * P]
        return t[:, chunk, tile:T:NT]

    @block.sync
    def _(sp):
        def load(n, slot, pieces):
            if not isinstance(n, int) or n >= 2:
                sp.wait_ge(low_done, n - 1)
            for dst, src in pieces:
                sp.dma_start(dst, src).then_inc(raw_loaded[slot], 16)

        def by_k(w):
            return w.rearrange("(k p) n -> p k n", p=P)

        def load_wide(n, w, k0, col):
            dst = shaped(raw, n % 2, 4)
            load(n, n % 2, [(dst[:, 2 * i:2 * i + 2, :],
                             by_k(w)[:, k0 + 2 * i:k0 + 2 * i + 2, col:col + 512]) for i in range(2)])

        def load_tall(n, w, col):
            dst = shaped(raw, n % 2, 8)
            load(n, n % 2, [(dst[:, 4 * i:4 * i + 4, :],
                             by_k(w)[:, 4 * i:4 * i + 4, col:col + 256]) for i in range(2)])

        w_in = a["w_in"][0]
        for t in range(NT):
            sp.dma_start(X[:, t, :], a["x"][0, t * P:(t + 1) * P, :]).then_inc(tile_loaded[t], 16)
        sp.dma_start(cst[:, :], a["table"]).then_inc(cst_loaded, 16)
        sp.dma_start(ws_raw[:, :, :], a["w_spatial"][0].rearrange("g i j -> i g j")).then_inc(ws_loaded, 16)
        dst = shaped(raw, 0, 8)
        load(B_MISC, 0, [(dst[:, :, 0:128], by_k(w_in)[:, :, 512:640]),
                         (dst[:, :, 128:256], by_k(w_in)[:, :, 1152:1280])])
        load_tall(B_Q, w_in, 0)
        for dst, src in ((onehot[:, :], a["buckets"]), (relb[:, :], a["rel_bias"])):
            sp.dma_start(dst, src).then_inc(band_vec_loaded, 16)
        for dst, src in ((lng[:, :], a["ln_v_g"]), (lnb[:, :], a["ln_v_b"])):
            sp.dma_start(dst, src.partition_broadcast(P)).then_inc(ln_loaded, 16)
        load_tall(B_Q + 1, w_in, 256)
        sp.wait_ge(nm_rows, NT)
        sp.dma_start(w_uk[:, :], a["w_uk"][0].rearrange("r h d -> r (h d)")).then_inc(uk_loaded, 16)
        sp.dma_start(w_uv[:, :], a["w_uv"][0].rearrange("r h d -> r (h d)")).then_inc(uk_loaded, 16)
        for i in range(2):
            load_tall(B_QI + i, w_in, 640 + 256 * i)
        for i in range(2):
            load_wide(B_V + i, w_in, 4 * i, 1736)
        sp.wait_ge(band_copied, 2 * HH)
        sp.dma_start(d_band.rearrange("h (p m) -> p h m", p=P), band[:, :, :]).then_inc(band_stored, 16)
        for i in range(2):
            load_tall(B_U + i, w_in, 1224 + 256 * i)
        sp.dma_start(bs_b[:, :, :].rearrange("p g i -> p (g i)"),
                     a["b_spatial"][0].rearrange("g i -> (g i)").partition_broadcast(P)).then_inc(bs_loaded, 16)
        sp.wait_ge(band_stored, 16)
        for h in range(HH):
            flat = d_band[h, P - 1:P - 1 + P * (BAND - 1)].rearrange("(p m) -> p m", m=BAND - 1)
            sp.dma_start(toep[:, h, :], flat[:, 0:T]).then_inc(toep_loaded, 16)
        with sp.Fori(0, 4) as i:
            for c in range(2):
                n = B_GATES + 2 * i + c
                slot = (B_GATES + c) % 2
                dst = shaped(raw, slot, 8)
                src = by_k(w_in)
                load(n, slot, [(dst[:, 4 * k:4 * k + 4, :],
                                src[:, 4 * k:4 * k + 4, bass.ds(2248 + 256 * c + 512 * i, 256)])
                               for k in range(2)])
        load_wide(B_PROJ, a["w_proj_a"][0], 0, 0)
        load_wide(B_PROJ + 1, a["w_proj_b"][0], 0, 0)
        load_wide(B_PROJ + 2, a["w_proj_a"][0], 0, 512)
        load_wide(B_PROJ + 3, a["w_proj_b"][0], 0, 512)
        sp.wait_ge(phase_done, 3 * 2)
        sp.dma_start(X[:, :, :], a["x"][0].rearrange("(t p) d -> p t d", p=P)).then_inc(x_again, 16)
        for half in range(2):
            for i in range(2):
                load_wide(B_WOUT + 2 * half + i, a["w_out"][0], 4 * i, 512 * half)
        sp.dma_start(g_wide[:, :], a["norm2_g"][0].partition_broadcast(P)).then_inc(gw_loaded, 16)
        sp.dma_start(rt_raw[:, :, 0:NG], by_k(a["router_group_w"][0])).then_inc(rt_loaded, 16)
        sp.dma_start(rt_raw[:, :, NG:36], by_k(a["router_expert_w"][0])).then_inc(rt_loaded, 16)
        sp.dma_start(rt_bias[:, 0:NG], a["router_group_b"][0].partition_broadcast(P)).then_inc(rt_loaded, 16)
        sp.dma_start(rt_bias[:, NG:36], a["router_expert_b"][0].partition_broadcast(P)).then_inc(rt_loaded, 16)
        for i in range(2):
            load_wide(B_DIL + i, a["a_w_in_2"][0], 4 * i, 0)
        sp.wait_ge(nm_rows, 2 * NT)
        for k in range(2):
            sp.dma_start(d_rows[k * T:(k + 1) * T, :].rearrange("(t p) d -> p t d", p=P),
                         xn[:, :, :]).then_inc(rows_stored, 16)
        sp.wait_ge(rt_empty, 1)
        sp.dma_start(d_list.rearrange("(p j) o -> p (j o)", p=P), empty[:, :]).then_inc(empty_stored, 16)
        sp.wait_ge(list_stored, 16 * 2 * NT)
        sp.dma_start(slot_rows[:, :], d_list.rearrange("(p j) o -> p (j o)", p=P)).then_inc(list_loaded, 16)
        sp.wait_ge(rt_tables, 1)
        sp.wait_ge(phase_done, 3 * 5)

        def expert(w, j):
            e = sp.value_load(slot_expert[0:1, bass.ds(j, 1)] if not isinstance(j, int)
                              else slot_expert[0:1, j:j + 1], min_val=0, max_val=NE - 1)
            return a[w][0, bass.ds(e, 1), :, :].rearrange("o (k p) n -> p (o k) n", p=P)

        def up(j, b):
            w_g, w_u = expert("w_gate", j), expert("w_up", j)
            if not isinstance(j, int) or j >= 2:
                sp.wait_ge(m_gu, j - 1)
            for q in range(2):
                dst = m_w[:, b, q, :].rearrange("p (k n) -> p k n", k=4)
                sp.dma_start(dst[:, :, 0:FE], w_g[:, 4 * q:4 * q + 4, :]).then_inc(m_up[b][q], 16)
                sp.dma_start(dst[:, :, FE:2 * FE], w_u[:, 4 * q:4 * q + 4, :]).then_inc(m_up[b][q], 16)

        def down(j, b):
            w_d = expert("w_down", j)
            if not isinstance(j, int) or j >= 2:
                sp.wait_ge(m_down, j - 1)
            sp.dma_start(m_w[:, b, 2, :].rearrange("p (k n) -> p k n", k=2), w_d).then_inc(m_dn[b], 16)

        sp.dma_start(gw1[:, :], a["final_norm_g"].partition_broadcast(P)).then_inc(gw1_loaded, 16)
        n_trips = sp.value_load(trips[0:1, 0:1], min_val=8, max_val=TRIPS)
        up(0, 0)
        down(0, 0)
        up(1, 1)
        down(1, 1)
        up(2, 0)
        with sp.Fori(1, n_trips) as i:
            up(2 * i + 1, 1)
            down(2 * i, 0)
            up(2 * i + 2, 0)
            down(2 * i + 1, 1)
        sp.wait_ge(phase_done, 3 * 6)
        for t in range(NT):
            for k in range(2):
                r = k * T + t * P
                sp.dma_start(y_in[:, k, t, :], d_y[r:r + P, :]).then_inc(tile_loaded[t], 16)
        def dil_block(hf, g, kind, kh):
            load_wide(B_DIL + ((hf * 3 + g) * 3 + kind) * 2 + kh, a["a_w_in_2"][0], 4 * kh,
                      g * 3 * D + kind * D + hf * HALF)
        for v in range(6):
            for kind in range(3):
                for kh in range(2):
                    if v or kind:
                        dil_block(v // 3, v % 3, kind, kh)
        load_wide(B_AOUT, a["a_w_out_2"][0], 0, 0)
        load_wide(B_AOUT + 1, a["a_w_out_2"][0], 4, 0)
        sp.wait_ge(phase_done, 3 * 9)
        sp.wait_ge(dl_lse_stored, 16 * 6)
        for g in range(3):
            sp.dma_start(lse3[:, g, :, :], d_lse[g].rearrange("(t p) h -> p t h", p=P)).then_inc(mg_lse_loaded, 16)
        sp.wait_ge(dl_stored0, 16 * 8)
        sp.wait_ge(dl_stored1, 16 * 8)
        for t in range(NT):
            sp.dma_start(og[:, t, :, :], d_o[:, t * P:(t + 1) * P, :].rearrange("g p d -> p g d"))\
              .then_inc(tile_loaded[t], 16)
        for i in range(2):
            load_wide(B_AOUT + 2 + i, a["a_w_out_2"][0], 4 * i, 512)

        def ffn_loads(l):
            w_gu, w_dn = by_k(a["ffn_w_gu_2"][l]), a["ffn_w_down_2"][l]
            for r, chunks in enumerate(FF_ROUNDS):
                n0 = B_FFN[l] + FF_BLOCK[r]
                with sp.Fori(0, chunks // 2) as i:
                    for c in range(2):
                        slot = (n0 + c) % 2
                        dst = shaped(raw, slot, 8)
                        col = P * (FF_CHUNK[r] + c) + 2 * P * i
                        load(n0 + c + 2 * i, slot, [(dst[:, :, 0:P], w_gu[:, :, bass.ds(col, P)]),
                                                    (dst[:, :, P:2 * P], w_gu[:, :, bass.ds(col + FF, P)])])
                for half in range(2):
                    for i in range(2):
                        n = n0 + chunks + 2 * half + i
                        k0, kn = FF_CHUNK[r] + 4 * i, min(4, chunks - 4 * i)
                        dst = shaped(raw, n % 2, 4)
                        src = by_k(w_dn)
                        load(n, n % 2, [(dst[:, k:k + kn // 2, :],
                                         src[:, k0 + k:k0 + k + kn // 2, 512 * half:512 * half + 512])
                                        for k in (0, kn // 2)])

        ffn_loads(0)
        w_b = a["b_w_in_2"][0]
        for i in range(2):
            load_tall(B_FOX + i, w_b, 256 * i)
        sp.wait_ge(phase_done, 3 * 11)
        sp.dma_start(fw_raw[:, :, :], by_k(w_b)[:, :, 3 * D:3 * D + 16]).then_inc(fo_loaded, 16)
        sp.dma_start(gw2[:, :], a["final_norm_2"].partition_broadcast(P)).then_inc(gw2_loaded, 16)
        sp.dma_start(fb[:, :], a["b_f_2"][0].partition_broadcast(P)).then_inc(fo_loaded, 16)
        for hf in range(2):
            for kind in range(0 if hf else 1, 2):
                for i in range(2):
                    load_tall(B_FOX + 6 * hf + 2 * kind + i, w_b, kind * D + hf * HALF + 256 * i)
            for i in range(2):
                load_wide(B_FOX + 6 * hf + 4 + i, w_b, 4 * i, 2 * D + hf * HALF)
        for kh in range(2):
            for half in range(2):
                load_wide(B_BOUT + 2 * kh + half, a["b_w_out_2"][0], 4 * kh, 512 * half)
        ffn_loads(1)
        for t in range(NT):
            sp.wait_ge(nm_rows, 7 * NT + t + 1)
            sp.dma_start(a["out"][0, t * P:(t + 1) * P, :], xn[:, t, :]).then_inc(out_stored, 16)
        sp.wait_ge(out_stored, 16 * NT)
    @block.tensor
    def _(pe):
        def phase_mark():
            pe.drain().then_inc(phase_done, 1)

        def phase_end(k):
            phase_mark()
            pe.wait_ge(phase_done, 3 * k)

        def pass3(out, sta, mov, start, stop):
            pe.matmul(out, sta[0], mov[0], start=start, stop=False)
            pe.matmul(out, sta[0], mov[1], start=False, stop=False)
            return pe.matmul(out, sta[1], mov[0], start=False, stop=stop)

        def narrow(out, sta, split, n, k):
            def high_part():
                return pe.matmul(out, sta[0], split[:, k, :], start=(k == 0), stop=(k == KD - 1))

            def low_part():
                return pe.matmul(out[:, 0:n], sta[1], split[:, k, 0:n], start=False, stop=False)

            if k == 0:
                high_part()
                return low_part()
            low_part()
            return high_part()

        def weights(slot, k):
            return shaped(w_high, slot, k), shaped(w_low, slot, k)

        def block_ready(n):
            pe.wait_ge(low_done, n + 1)

        chunk = [0]

        def turn(tiles):
            m = chunk[0]
            chunk[0] += 1
            if m >= 2:
                pe.wait_ge(turn_free, m - 1)
            for t, src in enumerate(tiles):
                last = pe.transpose(TB[m % 2][:, t * P:(t + 1) * P], src, ident)
            last.then_inc(turned, 1)

        def turn_norm(r, product):
            pe.wait_ge(nm_rows, NT * (r + 1))
            first = chunk[0]
            for c in range(KD + 2):
                if c >= 2:
                    pe.wait_ge(turn_free, first + c - 1)
                    product(c - 2)
                if c < KD:
                    turn([xn[:, t, c * P:(c + 1) * P] for t in range(NT)])

        def by_rows(n, mov_k, act, k0, kn, outs, free, done, start, stop, order=0):
            block_ready(n)
            wh, wl = weights(n % 2, mov_k)
            for t in range(NT):
                if start and free is not None:
                    free(t)
                for k in range(kn):
                    sta = (tokens(act[0], k0 + k, t, order), tokens(act[1], k0 + k, t, order))
                    last = pass3(outs[t][:, :], sta, (wh[:, k, :], wl[:, k, :]), start and k == 0, stop and k == kn - 1)
                if stop:
                    last.then_inc(done, 1)
            if not stop:
                last.then_inc(block_used, 1)

        pe.wait_ge(cst_loaded, 16)
        pe.wait_ge(ws_loaded, 16)
        turn([ws_raw[:, g, :] for g in range(4)])

        hh = (h_high, h_low)

        def in_free(j):
            if 4 <= j < 8:
                pe.wait_ge(misc_copied, j - 3)
            elif j >= 8:
                pe.wait_ge(in_evac, j - 7)

        def tall(n, j0, before=None):
            block_ready(n)
            wh, wl = weights(n % 2, 8)
            for m in range(2):
                if before:
                    before(m)
                in_free(j0 + m)
                for k in range(KD):
                    c = slice(m * P, (m + 1) * P)
                    last = pass3(G[(j0 + m) % 4][:, :], (wh[:, k, c], wl[:, k, c]),
                                 (h_high[:, k, :], h_low[:, k, :]), k == 0, k == KD - 1)
                if m == 0:
                    last.then_inc(in_out, 1)
            return last

        wh, wl = weights(0, 8)

        def misc_product(k):
            if k == 0:
                block_ready(B_MISC)
            for t in range(NT):
                last = pass3(G[t][:, 0:200], (tokens(h_high, k, t, 0), tokens(h_low, k, t, 0)),
                             (wh[:, k, 0:200], wl[:, k, 0:200]), k == 0, k == KD - 1)
                if k == KD - 1:
                    last.then_inc(in_out, 1)

        turn_norm(0, misc_product)

        def bias_row(h):
            if h:
                pe.wait_ge(band_copied, 2 * h)
            pe.matmul(SB[0][:, 0:T], relb_wide[:, h, :], onehot[:, 0:T], start=True, stop=True)
            pe.matmul(SB[1][:, 0:P], relb_wide[:, h, :], onehot[:, T:BAND], start=True, stop=True)\
              .then_inc(band_psum, 1)

        pe.wait_ge(band_vec_loaded, 32)
        pe.wait_ge(relb_wide_done, 1)
        for i in range(2):
            tall(B_Q + i, 4 + 2 * i, lambda m: bias_row(2 * i + m)).then_inc(in_out, 1)
        pe.wait_ge(ck_root, 1)
        turn([misc[:, t, 0:P] for t in range(NT)])
        turn([misc[:, t, P:2 * P] for t in range(NT)])
        for i in range(2):
            tall(B_QI + i, 8 + 2 * i, lambda m: bias_row(4 + 2 * i + m)).then_inc(in_out, 1)
        for kh in range(2):
            by_rows(B_V + kh, 4, hh, 4 * kh, 4, G, lambda t: in_free(12 + t), in_out, kh == 0, kh == 1)
        pe.wait_ge(turn_free, chunk[0])
        pe.wait_ge(in_evac, 8)
        pe.wait_ge(band_copied, 2 * HH)
        unit = 0
        for qt in range(1, NT):
            for h in range(HH):
                if unit >= 2:
                    pe.wait_ge(ix_relu, unit - 1)
                rows = slice(DH * (h % 2), DH * (h % 2) + DH)
                pe.matmul(SB[unit % 2][:, 0:(qt + 1) * P], qiT[rows, h // 2, qt * P:(qt + 1) * P],
                          kiT[rows, 0:(qt + 1) * P], start=True, stop=True).then_inc(ix_scores, 1)
                unit += 1
        for i in range(2):
            tall(B_U + i, 16 + 2 * i).then_inc(in_out, 1)
        with pe.Fori(0, 2) as it:
            for c in range(2):
                n = B_GATES + c
                pe.wait_ge(low_done, 2 * it + n + 1)
                wh, wl = weights(n % 2, 8)
                for m in range(2):
                    j = 20 + 2 * c + m
                    pe.wait_ge(in_evac, 4 * it + j - 7)
                    for k in range(KD):
                        cc = slice(m * P, (m + 1) * P)
                        last = pass3(G[j % 4][:, :], (wh[:, k, cc], wl[:, k, cc]),
                                     (h_high[:, k, :], h_low[:, k, :]), k == 0, k == KD - 1)
                    last.then_inc(in_out, 1)
        phase_mark()

        pe.wait_ge(uk_loaded, 32)
        for m in range(4):
            pe.wait_ge(in_evac, 21 + m)
            pe.matmul(G[m][:, :], w_uk[:, m * P:(m + 1) * P], ckvT[:, :], start=True, stop=True)\
              .then_inc(kv_out, 1)
        pe.wait_ge(phase_done, 3)
        pe.wait_ge(ln_done, NT)
        for g in range(4):
            pe.wait_ge(kv_copied, g + 1)
            for c in range(NT):
                last = pe.matmul(G[g][:, c * P:(c + 1) * P], vtok[:, c, g * P:(g + 1) * P], ws_t[:, g, :],
                                 start=True, stop=True)
            last.then_inc(gm_out, 1)
        for t in range(NT):
            pe.wait_ge(gm_free, t + 1)
            pe.matmul(G[t][:, :], ckvT[:, t * P:(t + 1) * P], w_uv[:, :], start=True, stop=True)\
              .then_inc(kv_out, 1)

        def attend(base, tile0, q_, k_, v_, sc_, pt_, deep=2, between=None, plan=()):
            units = NT * HH

            def scores(u):
                qt, h = divmod(u, HH)
                if u >= deep:
                    pe.wait_ge(at_read, base + u - deep + 1)
                rows = slice(DH * (h % 2), DH * (h % 2) + DH)
                pe.matmul(S3[u % deep][:, 0:(qt + 1) * P], q_[rows, h // 2, qt * P:(qt + 1) * P],
                          k_[rows, h // 2, 0:(qt + 1) * P], start=True, stop=True).then_inc(at_scores, 1)

            def turn_probs(u):
                pe.wait_ge(at_prob, base + u + 1)
                if u >= deep:
                    pe.wait_ge(at_copied, base + u - deep + 1)
                for kt in range(u // HH + 1):
                    last = pe.transpose(T3[u % deep][:, kt * P:(kt + 1) * P],
                                        sc_[:, u % 3, kt * P:(kt + 1) * P], ident)
                last.then_inc(at_turned, 1)

            def times_values(u):
                qt, h = divmod(u, HH)
                pe.wait_ge(at_copied, base + u + 1)
                if h == 0 and qt >= 2:
                    pe.wait_ge(at_done, tile0 + qt - 1)
                for kt in range(qt + 1):
                    last = pe.matmul(G[qt % 2][:, h * DH:(h + 1) * DH], pt_[:, u % deep, kt * P:(kt + 1) * P],
                                     v_[:, kt, h * DH:(h + 1) * DH], start=(kt == 0), stop=(kt == qt))
                if h == HH - 1:
                    last.then_inc(at_out, 1)

            def unit(u):
                turn_probs(u)
                if u + deep < units:
                    scores(u + deep)
                if u >= 1:
                    times_values(u - 1)

            for u in range(deep):
                scores(u)
            u = 0
            for i, after in enumerate(plan):
                between(i)
                for _ in range(after):
                    unit(u)
                    u += 1
            while u < units:
                unit(u)
                u += 1
            times_values(units - 1)

        pe.wait_ge(kv_copied, 8)
        pe.wait_ge(turn_free, chunk[0])

        def late_gate(i):
            j, n = 28 + i, B_GATES + 4 + i // 2
            if i % 2 == 0:
                block_ready(n)
            if i >= 2:
                pe.wait_ge(in_evac, j - 5)
            wh, wl = weights(n % 2, 8)
            cc = slice((i % 2) * P, (i % 2 + 1) * P)
            for k in range(KD):
                last = pass3(G[2 + i % 2][:, :], (wh[:, k, cc], wl[:, k, cc]),
                             (h_high[:, k, :], h_low[:, k, :]), k == 0, k == KD - 1)
            last.then_inc(in_out, 1)

        attend(0, 0, qT, KT, V, sc, PT, 2, late_gate, GATE_UNITS)
        pe.wait_ge(at_done, NT)
        pe.wait_ge(at_copied, 32)
        for m in range(4):
            turn([o_tok[:, t, m * P:(m + 1) * P] for t in range(NT)])
        pe.wait_ge(turn_free, chunk[0])
        pe.wait_ge(g_done, 1)
        phase_end(2)

        for b in range(4):
            block_ready(B_PROJ + b)
            wh, wl = weights((B_PROJ + b) % 2, 4)
            src0 = 0 if b % 2 == 0 else 4
            for m in range(4):
                if b:
                    pe.wait_ge(pj_free, 4 * (b - 1) + m + 1)
                for k in range(4):
                    cc = slice(m * P, (m + 1) * P)
                    last = pass3(G[m][:, :], (wh[:, k, cc], wl[:, k, cc]),
                                 (h_high[:, src0 + k, :], h_low[:, src0 + k, :]), k == 0, k == 3)
                last.then_inc(pj_out, 1)
        phase_mark()

        def rows_out(n0, act, out, free, before=None):
            for half in range(2):
                for kh in range(2):
                    if before and half == 0:
                        before(kh)

                    def wait_free(t):
                        if half:
                            pe.wait_ge(free, t + 1)
                        elif before:
                            pe.wait_ge(pj_free, 13 + t)
                    by_rows(n0 + 2 * half + kh, 4, act, 4 * kh, 4, G, wait_free, out, kh == 0, kh == 1)

        rows_out(B_WOUT, (merged_high, merged_low), wo_out, wo_free, lambda kh: pe.wait_ge(pj_low, 4 * kh + 4))
        phase_end(4)

        pe.wait_ge(rt_low_done, 1)

        def router(k):
            for t in range(NT):
                last = narrow(G[t][:, 0:72], [tokens(x, k, t, 0) for x in hh], rt_split, 36, k)
                if k == KD - 1:
                    last.then_inc(rt_out, 1)

        turn_norm(1, router)
        pe.wait_ge(rt_both, 1)
        for t in range(NT):
            for q in range(t + 1):
                pe.matmul(SB[0][:, t * NE:(t + 1) * NE], ones if q < t else cst[:, C_TRIS:C_TRIS + P],
                          both[:, q, :], start=(q == 0), stop=(q == t))
        for q in range(NT):
            last = pe.matmul(SB[1][:, 0:NE], ones, both[:, q, :], start=(q == 0), stop=(q == NT - 1))
        last.then_inc(rt_cum, 1)
        phase_end(5)

        m_gath = [m_gath0, m_gath1]

        def rows_come(b, uses):
            pe.wait_ge(m_gath[b], 16 * uses)

        def turn_rows(j, b):
            for k in range(KD):
                last = pe.transpose(TB[b][:, k * R:(k + 1) * R], xg[:, b, k * P:(k + 1) * P], ident[0:R, 0:R])
            last.then_inc(m_turned, 1)

        def turn_he():
            for c in range(2):
                last = pe.transpose(SB[0][:, c * R:(c + 1) * R], he[:, c * P:(c + 1) * P], ident[0:R, 0:R])
            last.then_inc(m_he_turned, 1)

        def up(j, b, uses, before):
            pe.wait_ge(m_xt, j + 1)
            for q in range(2):
                if q and before is not None:
                    turn_he()
                pe.wait_ge(m_up[b][q], 32 * uses)
                w = m_w[:, b, q, :].rearrange("p (k n) -> p k n", k=4)
                for k in range(4):
                    if q == 0 and k == 3 and before is not None:
                        pe.wait_ge(m_he, before + 1)
                    last = pe.matmul(G[b][0:R, :], xt[:, b, 4 * q + k, :], w[:, k, :],
                                     start=(q + k == 0), stop=(q == 1 and k == 3))
            last.then_inc(m_gu, 1)

        def down(j, b, uses, come=None):
            pe.wait_ge(m_het, j + 1)
            pe.wait_ge(m_dn[b], 16 * uses)
            pe.wait_ge(m_y, j + 1)
            w = m_w[:, b, 2, :].rearrange("p (k n) -> p k n", k=2)
            for c in range(2):
                for half in range(2):
                    if come and c + half == 2:
                        come()
                    last = pe.matmul(G[2 + half][0:R, :], het[:, c, :], w[:, c, 512 * half:512 * half + 512],
                                     start=(c == 0), stop=(c == 1))
            last.then_inc(m_down, 1)

        n_trips = pe.value_load(trips[0:1, 0:1], min_val=8, max_val=TRIPS)
        for b in range(2):
            rows_come(b, 1)
            turn_rows(b, b)
        up(0, 0, 1, None)
        rows_come(0, 2)
        turn_rows(2, 0)
        up(1, 1, 1, 0)
        down(0, 0, 1, lambda: rows_come(1, 2))
        with pe.Fori(1, n_trips) as i:
            turn_rows(2 * i + 1, 1)
            up(2 * i, 0, i + 1, 2 * i - 1)
            down(2 * i - 1, 1, i, lambda: rows_come(0, i + 2))
            turn_rows(2 * i + 2, 0)
            up(2 * i + 1, 1, i + 1, 2 * i)
            down(2 * i, 0, i + 1, lambda: rows_come(1, i + 2))
        pe.wait_ge(m_he, 2 * n_trips)
        pe.matmul(SB[1][0:R, 0:R], ident[:, 0:R], ident[:, 0:R], start=True, stop=True)
        turn_he()
        down(2 * n_trips - 1, 1, n_trips)
        for q in range(2):
            pe.wait_ge(m_up[0][q], 32 * n_trips + 32)
            last = pe.matmul(SB[1][0:R, 0:R], ident[:, 0:R], m_w[:, 0, q, 0:R], start=True, stop=True)
        phase_end(6)
        phase_end(7)
        phase_mark()
        def project(v, i):
            kind, t = divmod(i, NT)
            n, m = B_DIL + (v * 3 + kind) * 2, 12 * v + i
            if m >= 2:
                pe.wait_ge(dl_evac, m - 1)
            for kh in range(2):
                if t == 0:
                    block_ready(n + kh)
                wh, wl = weights((n + kh) % 2, 4)
                for k in range(4):
                    sta = [tokens(x, 4 * kh + k, t, min(v % 3, 1)) for x in hh]
                    last = pass3(G[2 + m % 2][:, :], sta, (wh[:, k, :], wl[:, k, :]),
                                 kh + k == 0, kh == 1 and k == 3)
                if kh == 0 and t == NT - 1:
                    last.then_inc(block_used, 1)
            last.then_inc(dl_out, 1)

        def first_two(c):
            if c % 4 == 0:
                block_ready(B_DIL + c // 4)
            wh, wl = weights((B_DIL + c // 4) % 2, 4)
            for t in range(2):
                last = pass3(G[2 + t][:, :], [tokens(x, c, t, 0) for x in hh],
                             (wh[:, c % 4, :], wl[:, c % 4, :]), c == 0, c == KD - 1)
                if c == KD - 1:
                    last.then_inc(dl_out, 1)

        turn_norm(3, first_two)
        for i in range(2, 12):
            project(0, i)
        unit0 = 32
        for v in range(6):
            g = v % 3
            pe.wait_ge(dl_rot, v + 1)
            if v:
                pe.wait_ge(at_copied, unit0)
            for kind in range(2):
                for m in range(4):
                    turn([qk[:, 4 * kind + t, m * P:(m + 1) * P] for t in range(NT)])
            pe.wait_ge(turn_free, chunk[0])
            pe.wait_ge(dl_evac, 12 * (v + 1))
            hu = 2 if g == 0 else 4
            per_tile = HH // hu
            units = NT * per_tile

            def scores(u):
                t, q = divmod(u, per_tile)
                if u >= 2:
                    pe.wait_ge(at_read, unit0 + u - 1)
                for e in range(hu):
                    h = first_head(q, hu) + 2 * e
                    rows = slice(DH * (h % 2), DH * (h % 2) + DH)
                    q_ = dqT[rows, h // 2, t * P:(t + 1) * P]
                    keys = ([t, t - 1] if t else [0, 0]) if g == 0 else [t]
                    for z, kt in enumerate(keys):
                        o = (e * len(keys) + z) * P
                        last = pe.matmul(SB[u % 2][:, o:o + P], q_, dkT[rows, h // 2, kt * P:(kt + 1) * P],
                                         start=True, stop=True)
                last.then_inc(at_scores, 1)

            def turn_probs(u):
                pe.wait_ge(at_prob, unit0 + u + 1)
                if u >= 2:
                    pe.wait_ge(at_copied, unit0 + u - 1)
                for c in range(4):
                    last = pe.transpose(TB[u % 2][:, c * P:(c + 1) * P], dsc[:, u % 3, c * P:(c + 1) * P], ident)
                last.then_inc(at_turned, 1)

            def times_values(u):
                t, q = divmod(u, per_tile)
                pe.wait_ge(at_copied, unit0 + u + 1)
                if q == 0:
                    pe.wait_ge(at_done, NT * (v + 1) + t - 1)
                for e in range(hu):
                    h = first_head(q, hu) + 2 * e
                    keys = ([t, t - 1] if t else [0, 0]) if g == 0 else [t]
                    for z, kt in enumerate(keys):
                        o = (e * len(keys) + z) * P
                        last = pe.matmul(G[t % 2][:, h * DH:(h + 1) * DH], dPT[:, u % 3, o:o + P],
                                         dV[:, v % 2, kt, h * DH:(h + 1) * DH], start=(z == 0), stop=(z == len(keys) - 1))
                if q == per_tile - 1:
                    last.then_inc(at_out, 1)

            def unit(u):
                turn_probs(u)
                if u + 2 < units:
                    scores(u + 2)
                if u >= 1:
                    times_values(u - 1)

            scores(0)
            scores(1)
            u = 0
            if v < 5:
                for i in range(12):
                    project(v + 1, i)
                    for _ in range(units_after(v)[i]):
                        unit(u)
                        u += 1
            while u < units:
                unit(u)
                u += 1
            times_values(units - 1)
            unit0 += units
        phase_end(9)
        pe.wait_ge(mg_done, NT)
        for c in range(KD):
            turn([xn[:, t, c * P:(c + 1) * P] for t in range(NT)])
        pe.wait_ge(turn_free, chunk[0])
        rows_out(B_AOUT, hh, ao_out, ao_free)
        phase_end(10)

        def swiglu(l):
            for r, chunks in enumerate(FF_ROUNDS):
                n0 = B_FFN[l] + FF_BLOCK[r]
                f0 = 22 * l + FF_CHUNK[r]
                down0 = (3 * l + r) * 8
                if r:
                    pe.wait_ge(ff_down_free, down0)

                def first_block(k):
                    if k == 0:
                        pe.wait_ge(low_done, n0 + 1)
                        if f0:
                            pe.wait_ge(ff_mul, f0 - 1)
                    wh, wl = weights(n0 % 2, 8)
                    for m in range(2):
                        cc = slice(m * P, (m + 1) * P)
                        last = pass3(G[m][:, :], (wh[:, k, cc], wl[:, k, cc]), (h_high[:, k, :], h_low[:, k, :]),
                                     k == 0, k == KD - 1)
                    if k == KD - 1:
                        last.then_inc(ff_out, 1)

                def up(i, peeled):
                    for c in range(1 if peeled else 0, 2):
                        pe.wait_ge(low_done, n0 + c + 1 + 2 * i)
                        wh, wl = weights((n0 + c) % 2, 8)
                        if not peeled or f0:
                            pe.wait_ge(ff_mul, f0 + c - 1 + 2 * i)
                        for m in range(2):
                            cc = slice(m * P, (m + 1) * P)
                            for k in range(KD):
                                last = pass3(G[2 * c + m][:, :], (wh[:, k, cc], wl[:, k, cc]),
                                             (h_high[:, k, :], h_low[:, k, :]), k == 0, k == KD - 1)
                            if m == 1:
                                last.then_inc(ff_out, 1)

                if r == 0:
                    turn_norm(4 + 2 * l, first_block)
                else:
                    for k in range(KD):
                        first_block(k)
                up(0, True)
                with pe.Fori(1, chunks // 2) as i:
                    up(i, False)
                for half in range(2):
                    outs = bank[4:8] if half == 0 else bank[0:4]
                    for i in range(2):
                        n = n0 + chunks + 2 * half + i
                        kn = min(4, chunks - 4 * i)
                        if half == 0:
                            pe.wait_ge(ff_low, f0 + 4 * i + kn)
                        by_rows(n, 4, (act_high, act_low), 4 * i, kn, outs, None, ff_down_out, i == 0, i == 1)

        swiglu(0)
        phase_end(11)
        def first_fox(k):
            if k == 0:
                block_ready(B_FOX)
            wh, wl = weights(B_FOX % 2, 8)
            for m in range(2):
                cc = slice(m * P, (m + 1) * P)
                last = pass3(G[2 + m][:, :], (wh[:, k, cc], wl[:, k, cc]), (h_high[:, k, :], h_low[:, k, :]),
                             k == 0, k == KD - 1)
                if k == KD - 1:
                    last.then_inc(fo_out, 1)

        turn_norm(5, first_fox)
        pe.wait_ge(fo_lowd, 1)
        for t in range(NT):
            for k in range(KD):
                last = narrow(SB[0][:, t * 32:(t + 1) * 32], [tokens(x, k, t, 0) for x in hh], fw_split, 16, k)
        last.then_inc(fo_logit, 1)
        pe.wait_ge(fo_f, 1)
        for t in range(NT):
            for q in range(t + 1):
                last = pe.matmul(SB[1][:, t * 16:(t + 1) * 16], ones if q < t else cst[:, C_TRI:C_TRI + P],
                                 fz[:, q, :], start=(q == 0), stop=(q == t))
        last.then_inc(fo_c, 1)
        pe.wait_ge(fo_ct, 1)
        for t in range(NT):
            last = pe.transpose(SB[0][0:16, t * P:(t + 1) * P], c_tok[:, t, :], ident)
        last.then_inc(fo_sel, 1)
        def project_fox(hf, i):
            kind, m = divmod(i, 4)
            j, n = 12 * hf + i, B_FOX + 6 * hf + 2 * kind
            out = G[2 + j % 2]
            if j >= 2:
                pe.wait_ge(fo_evac, j - 1)
            if kind < 2:
                if m % 2 == 0:
                    block_ready(n + m // 2)
                wh, wl = weights((n + m // 2) % 2, 8)
                cc = slice((m % 2) * P, (m % 2 + 1) * P)
                for k in range(KD):
                    last = pass3(out[:, :], (wh[:, k, cc], wl[:, k, cc]),
                                 (h_high[:, k, :], h_low[:, k, :]), k == 0, k == KD - 1)
            else:
                for kh in range(2):
                    if m == 0:
                        block_ready(n + kh)
                    wh, wl = weights((n + kh) % 2, 4)
                    for k in range(4):
                        last = pass3(out[:, :], [tokens(x, 4 * kh + k, m, 0) for x in hh],
                                     (wh[:, k, :], wl[:, k, :]), kh + k == 0, kh == 1 and k == 3)
                    if kh == 0 and m == NT - 1:
                        last.then_inc(block_used, 1)
            last.then_inc(fo_out, 1)

        def out_fox(i):
            b, t = divmod(i, NT)
            n, kh = B_BOUT + b, b // 2
            if t == 0:
                block_ready(n)
            if i >= 2:
                pe.wait_ge(bo_free, i - 1)
            wh, wl = weights(n % 2, 4)
            for k in range(4):
                last = pass3(G[2 + i % 2][:, :], [tokens(x, 4 * kh + k, t, 0) for x in (o_high, o_low)],
                             (wh[:, k, :], wl[:, k, :]), k == 0, k == 3)
            last.then_inc(bo_out, 1)

        for i in range(2, 12):
            project_fox(0, i)
        for hf in range(2):
            for h in range(HH):
                pe.wait_ge(fo_nc, 2 * HH * hf + (h + 1 if h < 2 else 2 * h))
                pe.matmul(SB[h % 2][:, :], sel16[:, h % 2, :], cT[:, :], start=True, stop=True).then_inc(fo_ncb, 1)
            pe.wait_ge(fo_nc, 2 * HH * (hf + 1))
            pe.wait_ge(fo_evac, 12 * (hf + 1))
            pe.wait_ge(turn_free, chunk[0])
            attend(96 + 32 * hf, 28 + NT * hf, fqT[hf], fkT[hf], fV[hf], fsc, fPT, 2,
                   out_fox if hf else lambda i: project_fox(1, i), FOX_UNITS[hf])
            pe.wait_ge(at_done, 28 + NT * (hf + 1))
            pe.wait_ge(at_copied, 96 + 32 * (hf + 1))
            for m in range(4):
                turn([fo_tok[:, t, m * P:(m + 1) * P] for t in range(NT)])
        pe.wait_ge(turn_free, chunk[0])
        phase_end(12)
        for i in range(8, 16):
            out_fox(i)
        phase_end(13)
        swiglu(1)
        phase_end(14)

    @block.scalar
    def _(act):
        def phase_mark():
            act.drain().then_inc(phase_done, 1)

        def phase_end(k):
            phase_mark()
            act.wait_ge(phase_done, 3 * k)

        def split_high(n, slot, uses):
            act.wait_ge(raw_loaded[slot], 32 * uses)
            act.activation(w_high[:, slot, :], raw[:, slot, :], ACT.Copy).then_inc(high_done, 1)

        def ahead(n):
            if n + 2 < N_BLOCKS:
                split_high(n + 2, n % 2, (n + 2) // 2 + 1)

        halves = [0]

        def half_read():
            halves[0] += 1
            act.wait_ge(block_used, halves[0])

        def norm_tile(q, t, ready, count):
            act.wait_ge(ready, count)
            act.activation(xn[:, t, :], X[:, t, :], ACT.Square, accum_out=ss[:, t:t + 1]).then_inc(nm_squares, 1)
            act.wait_ge(nm_mean, q + 1)
            act.activation(rms[:, t:t + 1], msq[:, t:t + 1], ACT.Sqrt).then_inc(nm_root, 1)

        chunk = [0]

        def turned_high(dst, scale=None):
            m = chunk[0]
            chunk[0] += 1
            act.wait_ge(turned, m + 1)
            kw = {} if scale is None else {"scale": scale}
            act.activation(dst, TB[m % 2][:, :], ACT.Copy, **kw).then_inc(turn_high, 1)

        def turned_norm(g):
            for c in range(KD):
                turned_high(h_high[:, c, :], None if g is None else gcol[:, g, c:c + 1])

        vecs = [(gcol[:, i, :], v) for i, v in enumerate([a["norm1_g"][0], a["norm2_g"][0], a["a_norm_2"][0],
                                                          a["ffn_norm_2"][0], a["b_norm_2"][0], a["ffn_norm_2"][1]])]
        for dst, v in vecs:
            act.dma_start(dst, v.rearrange("(k p) -> p k", p=P), allow_slow_non_contiguous=True).then_inc(vec_loaded, 16)
        act.dma_start(kvg[:, :], a["kv_norm_g"][0].rearrange("(p o) -> p o", o=1)).then_inc(vec_loaded, 16)
        act.dma_start(ids[:, :], a["pairs"]).then_inc(vec_loaded, 16)
        for t in range(NT):
            norm_tile(t, t, tile_loaded[t], 16)
        split_high(0, 0, 1)
        act.wait_ge(vec_loaded, 16 * 8)
        chunk[0] += 1
        for c in range(KD):
            turned_high(h_high[:, c, :], gcol[:, 0, c:c + 1])
            if c == 1:
                split_high(1, 1, 1)

        act.wait_ge(in_out, 4)
        ahead(B_MISC)
        act.wait_ge(ck_mean, 1)
        act.activation(rms[:, :], msq[:, :], ACT.Sqrt).then_inc(act_step, 1)

        def take(j, dst, func, **kw):
            act.wait_ge(in_out, j + 1)
            act.activation(dst, G[j % 4][:, :], func, **kw).then_inc(in_evac, 1)

        for i in range(2):
            for m in range(2):
                take(4 + 2 * i + m, qT[:, 2 * i + m, :], ACT.Copy)
            ahead(B_Q + i)
        chunk[0] += 2
        for i in range(2):
            for m in range(2):
                take(8 + 2 * i + m, qiT[:, 2 * i + m, :], ACT.Copy)
            ahead(B_QI + i)
        half_read()
        ahead(B_V)
        act.wait_ge(band_stored, 16)
        for t in range(NT):
            take(12 + t, vtok[:, t, :], ACT.Gelu_apprx_tanh, accum_out=ln_sum[:, t:t + 1])
        ahead(B_V + 1)
        unit = 0
        for qt in range(1, NT):
            for h in range(HH):
                act.wait_ge(ix_scores, unit + 1)
                if unit >= 2:
                    act.wait_ge(ix_added, unit - 1)
                act.activation(sc[:, unit % 2, 0:(qt + 1) * P], SB[unit % 2][:, 0:(qt + 1) * P], ACT.Relu)\
                   .then_inc(ix_relu, 1)
                unit += 1
        for i in range(2):
            for m in range(2):
                take(16 + 2 * i + m, uT[:, 2 * i + m, :], ACT.Gelu_apprx_tanh)
            ahead(B_U + i)
        with act.Fori(0, 2) as it:
            for c in range(2):
                for m in range(2):
                    j = 20 + 2 * c + m
                    act.wait_ge(in_out, 4 * it + j + 1)
                    act.activation(gates[:, bass.ds(4 * it + 2 * c + m, 1), :],
                                   G[j % 4][:, :].rearrange("p (o n) -> p o n", o=1), ACT.Sigmoid)\
                       .then_inc(in_evac, 1)
                n = B_GATES + c
                split_high(None, n % 2, (n + 2) // 2 + 1 + it)

        act.wait_ge(ln_var, 1)
        act.activation(rms[:, :], msq[:, :], ACT.Sqrt).then_inc(ln_root, 1)
        for m in range(4):
            act.wait_ge(kv_out, m + 1)
            act.activation(KT[:, m, :], G[m][:, :], ACT.Copy).then_inc(kv_copied, 1)
        phase_end(1)
        for t in range(NT):
            act.wait_ge(kv_out, 5 + t)
            act.activation(V[:, t, :], G[t][:, :], ACT.Copy).then_inc(kv_copied, 1)

        def attend(base, sc_, pt_, deep, empty, plan, blocks):
            def copy(u):
                k = (u // HH + 1) * P
                act.wait_ge(at_turned, base + u + 1)
                act.activation(pt_[:, u % deep, 0:k], T3[u % deep][:, 0:k], ACT.Copy).then_inc(at_copied, 1)

            def unit(u):
                k = (u // HH + 1) * P
                act.wait_ge(at_max, base + u + 1)
                act.activation(sc_[:, u % 3, 0:k], sc_[:, u % 3, 0:k], ACT.Exp, bias=nmx[:, u:u + 1],
                               accum_out=rsum[:, u:u + 1]).then_inc(at_prob, 1)
                if u:
                    copy(u - 1)

            u = 0
            for i, after in enumerate(plan):
                unit(u)
                empty(i)
                unit(u + 1)
                blocks(i)
                for u in range(u + 2, u + after):
                    unit(u)
                u = sum(plan[:i + 1])
            while u < NT * HH:
                unit(u)
                u += 1
            copy(NT * HH - 1)


        def take_gate(i):
            act.wait_ge(in_out, 28 + i + 1)
            act.activation(gates[:, 8 + i, :], G[2 + i % 2][:, :], ACT.Copy).then_inc(in_evac, 1)

        def gate_blocks(i):
            if i % 2:
                ahead(B_GATES + 4 + i // 2)

        attend(0, sc, PT, 2, take_gate, GATE_UNITS, gate_blocks)
        act.wait_ge(in_evac, 32)
        for i in range(0, 8, 4):
            act.activation(gates[:, 8 + i:12 + i, :], gates[:, 8 + i:12 + i, :], ACT.Sigmoid)
        for m in range(4):
            turned_high(h_high[:, m, :])
        phase_end(2)

        for b in range(4):
            act.wait_ge(pj_out, 4 * (b + 1))
            ahead(B_PROJ + b)
            if b % 2:
                for m in range(4):
                    c = 4 * (b // 2) + m
                    act.wait_ge(pj_sum, c + 1)
                    act.activation(merged_high[:, c, :], gates[:, c, :], ACT.Copy).then_inc(pj_high, 1)
        phase_mark()

        def rows_ahead(n0, out, free, r):
            for half in range(2):
                half_read()
                ahead(n0 + 2 * half)
                if half == 0:
                    act.wait_ge(out, 4)
                    ahead(n0 + 1)
            for t in range(NT):
                norm_tile(NT * r + t, t, free, NT + t + 1)
            act.wait_ge(out, 8)
            ahead(n0 + 3)

        rows_ahead(B_WOUT, wo_out, wo_free, 1)
        phase_end(4)

        act.wait_ge(rt_loaded, 64)
        act.activation(rt_split[:, :, 0:36], rt_raw[:, :, :], ACT.Copy).then_inc(rt_high_done, 1)
        turned_norm(None)
        act.wait_ge(rt_exp_in, 1)
        act.activation(el[:, :, 0:NG], el[:, :, 0:NG], ACT.Exp).then_inc(rt_exp, 1)
        act.wait_ge(rt_e2_in, 1)
        act.activation(rv[:, 5, :], rv[:, 5, :], ACT.Exp).then_inc(rt_e2, 1)
        phase_end(5)
        def turned_he(j):
            act.wait_ge(m_he_turned, j + 1)
            act.activation(het[:, :, :], SB[0][:, 0:2 * R].rearrange("p (c n) -> p c n", c=2), ACT.Copy)\
               .then_inc(m_het, 1)

        def gate(j, b):
            act.wait_ge(m_gu, j + 1)
            act.activation(sg[:, :], G[b][0:R, 0:FE], ACT.Silu).then_inc(m_silu, 1)

        n_trips = act.value_load(trips[0:1, 0:1], min_val=8, max_val=TRIPS)
        gate(0, 0)
        turned_he(0)
        gate(1, 1)
        with act.Fori(1, n_trips) as i:
            turned_he(2 * i - 1)
            gate(2 * i, 0)
            turned_he(2 * i)
            gate(2 * i + 1, 1)
        turned_he(2 * n_trips - 1)
        phase_end(6)
        for i, (second, t) in enumerate(TWO_NORMS):
            if second:
                norm_tile(2 * NT + i, t, nm_rows, 2 * NT + TWO_NORMS.index((0, t)) + 1)
            else:
                norm_tile(2 * NT + i, t, y_summed, t + 1)
        phase_end(7)
        turned_norm(2)
        phase_mark()
        def empty_group(v, i):
            kind, t = divmod(i, NT)
            n, m = B_DIL + (3 * v + kind) * 2, 12 * v + i
            if t == NT - 1:
                half_read()
                ahead(n)
            act.wait_ge(dl_out, m + 1)
            dst = dV[:, v % 2, t, :] if kind == 2 else qk[:, 4 * kind + t, :]
            act.activation(dst, G[2 + m % 2][:, :], ACT.Copy).then_inc(dl_evac, 1)

        def next_block(v, i):
            if i % NT == NT - 1:
                ahead(B_DIL + (3 * v + i // NT) * 2 + 1)

        for i in range(12):
            empty_group(0, i)
            next_block(0, i)
        unit0 = 32
        for v in range(6):
            g = v % 3
            chunk[0] += 8
            hu = 2 if g == 0 else 4
            w = T // hu
            per_tile = HH // hu
            units = NT * per_tile

            def copy(u):
                act.wait_ge(at_turned, unit0 + u + 1)
                act.activation(dPT[:, u % 3, :], TB[u % 2][:, :], ACT.Copy).then_inc(at_copied, 1)

            def unit(u):
                act.wait_ge(at_max, unit0 + u + 1)
                for e in range(hu):
                    col = HH * (u // per_tile) + first_head(u % per_tile, hu) + 2 * e
                    last = act.activation(dsc[:, u % 3, e * w:(e + 1) * w], dsc[:, u % 3, e * w:(e + 1) * w],
                                          ACT.Exp, bias=nmx[:, col:col + 1], accum_out=rsum[:, col:col + 1])
                last.then_inc(at_prob, 1)
                if u:
                    copy(u - 1)

            u = 0
            if v < 5:
                for i in range(12):
                    for c in range(max(units_after(v)[i], 1)):
                        if units_after(v)[i]:
                            unit(u)
                            u += 1
                        if c == 0:
                            empty_group(v + 1, i)
                        if c == min(1, units_after(v)[i] - 1) or units_after(v)[i] == 0:
                            next_block(v + 1, i)
            while u < units:
                unit(u)
                u += 1
            copy(units - 1)
            act.wait_ge(at_prob, unit0 + units)
            if v:
                act.wait_ge(dl_lse_stored, 16 * v)
            act.activation(lse[:, :, :], rsum[:, :].rearrange("p (t h) -> p t h", h=HH), ACT.Ln).then_inc(dl_ln, 1)
            unit0 += units
        phase_end(9)
        act.wait_ge(mg_exp_in, 1)
        act.activation(lse3[:, :, :, :], lse3[:, :, :, :], ACT.Exp).then_inc(mg_exp, 1)
        for c in range(KD):
            turned_high(h_high[:, c, :])
        rows_ahead(B_AOUT, ao_out, ao_free, 4)
        phase_end(10)

        def swiglu(l):
            for r, chunks in enumerate(FF_ROUNDS):
                n0 = B_FFN[l] + FF_BLOCK[r]
                f0 = 22 * l + FF_CHUNK[r]
                with act.Fori(0, chunks // 2) as i:
                    for c in range(2):
                        f = f0 + c + 2 * i
                        act.wait_ge(ff_out, f + 1)
                        act.activation(silu[:, c, :], G[2 * c][:, :], ACT.Silu).then_inc(ff_silu, 1)
                        split_high(None, (n0 + c) % 2, (n0 + c + 2) // 2 + 1 + i)
                        act.wait_ge(ff_mul, f + 1)
                        act.activation(act_high[:, bass.ds(c + 2 * i, 1), :],
                                       gu[:, c, :].rearrange("p (o n) -> p o n", o=1), ACT.Copy).then_inc(ff_high, 1)
                for half in range(2):
                    n = n0 + chunks + 2 * half
                    half_read()
                    ahead(n)
                    if r == 2 and half:
                        for t in range(NT):
                            norm_tile(NT * (5 + 2 * l) + t, t, ff_down_free, (3 * l + r) * 8 + 4 + t + 1)
                    act.wait_ge(ff_down_out, (3 * l + r) * 8 + 4 * (half + 1))
                    ahead(n + 1)

        turned_norm(3)
        swiglu(0)
        phase_end(11)
        act.wait_ge(fo_loaded, 32)
        act.activation(fw_split[:, :, 0:16], fw_raw[:, :, :], ACT.Copy).then_inc(fo_high, 1)
        turned_norm(4)
        act.wait_ge(fo_e_in, 1)
        act.activation(fe[:, :, :], fm[:, :, :], ACT.Exp).then_inc(fo_e, 1)
        act.wait_ge(fo_e, 1)
        act.activation(fe[:, :, :], fe[:, :, :], ACT.Ln, bias=ones_col[:, :]).then_inc(fo_l, 1)
        def empty_fox(hf, i):
            kind, m = divmod(i, 4)
            j, n = 12 * hf + i, B_FOX + 6 * hf + 2 * kind
            if kind == 2 and m == NT - 1:
                half_read()
                ahead(n)
            act.wait_ge(fo_out, j + 1)
            dst = [fqT, fkT, fV][kind][hf][:, m, :]
            if kind == 0:
                act.activation(dst, G[2 + j % 2][:, :], ACT.Copy, scale=SCALE).then_inc(fo_evac, 1)
            else:
                act.activation(dst, G[2 + j % 2][:, :], ACT.Copy).then_inc(fo_evac, 1)

        def fox_blocks(hf, i):
            kind, m = divmod(i, 4)
            n = B_FOX + 6 * hf + 2 * kind
            if kind < 2 and m == 1:
                ahead(n)
            if m == 3:
                ahead(n + 1)

        def out_ahead(i):
            if i % NT == NT - 1:
                act.wait_ge(bo_out, i + 1)
                ahead(B_BOUT + i // NT)

        for i in range(12):
            empty_fox(0, i)
            fox_blocks(0, i)
        for hf in range(2):
            attend(96 + 32 * hf, fsc, fPT, 2, (lambda i: None) if hf else (lambda i: empty_fox(1, i)),
                   FOX_UNITS[hf], out_ahead if hf else (lambda i: fox_blocks(1, i)))
            for m in range(4):
                turned_high(o_high[:, 4 * hf + m, :])
        phase_end(12)
        for i in range(8, 15):
            out_ahead(i)
        for t in range(NT):
            norm_tile(6 * NT + t, t, bo_free, 12 + t + 1)
        out_ahead(15)
        phase_end(13)
        turned_norm(5)
        swiglu(1)
        phase_end(14)

    @block.vector
    def _(dve):
        def phase_mark():
            dve.drain().then_inc(phase_done, 1)

        def phase_end(k):
            phase_mark()
            dve.wait_ge(phase_done, 3 * k)

        steps = [0]

        def step(ins):
            steps[0] += 1
            ins.then_inc(dve_step, 1)
            dve.wait_ge(dve_step, steps[0])

        def mul(out, x, y):
            return dve.tensor_tensor(out=out, in0=x, in1=y, op=ALU.mult)

        def add(out, x, y):
            return dve.tensor_tensor(out=out, in0=x, in1=y, op=ALU.add)

        def sub(out, x, y):
            return dve.tensor_tensor(out=out, in0=x, in1=y, op=ALU.subtract)

        chunk = [0]
        highs = [0]

        def turned_low(dst, high, scale=None):
            m = chunk[0]
            chunk[0] += 1
            highs[0] += 1
            dve.wait_ge(turn_high, highs[0])
            if scale is None:
                last = sub(dst, TB[m % 2][:, :], high.bitcast(F32))
            else:
                last = dve.scalar_tensor_tensor(out=dst, in0=TB[m % 2][:, :], scalar=scale,
                                                in1=high.bitcast(F32), op0=ALU.mult, op1=ALU.subtract)
            last.then_inc(turn_free, 1)

        def turned_chunk():
            m = chunk[0]
            chunk[0] += 1
            dve.wait_ge(turned, m + 1)
            return TB[m % 2]

        def norm_tile(q, t, dst, wide=None):
            dve.wait_ge(nm_squares, q + 1)
            dve.tensor_scalar(msq[:, t:t + 1], ss[:, t:t + 1], 1.0 / D, EPS, ALU.mult, ALU.add).then_inc(nm_mean, 1)
            dve.wait_ge(nm_root, q + 1)
            step(dve.reciprocal(rstd[:, t:t + 1], rms[:, t:t + 1]))
            if wide is None:
                last = dve.tensor_scalar(dst[:, t, :], X[:, t, :], rstd[:, t:t + 1], None, ALU.mult)
            else:
                last = dve.scalar_tensor_tensor(out=dst[:, t, :], in0=X[:, t, :], scalar=rstd[:, t:t + 1],
                                                in1=wide[:, :], op0=ALU.mult, op1=ALU.mult)
            last.then_inc(nm_rows, 1)

        def turned_norm(g):
            for c in range(KD):
                turned_low(h_low[:, c, :], h_high[:, c, :], None if g is None else gcol[:, g, c:c + 1])

        dve.memset(ones_col[:, :], 1.0)

        def bias_row(h):
            dve.wait_ge(band_psum, h + 1)
            dve.tensor_copy(band[:, h, 0:T], SB[0][:, :]).then_inc(band_copied, 1)
            dve.tensor_copy(band[:, h, T:BAND], SB[1][:, 0:P]).then_inc(band_copied, 1)

        for t in range(NT):
            dve.wait_ge(tile_loaded[t], 16)
            norm_tile(t, t, xn)
        dve.wait_ge(cst_loaded, 16)
        dve.wait_ge(vec_loaded, 16 * 8)
        src = turned_chunk()
        mul(ws_t[:, :, :], src[:, :].rearrange("p (g i) -> p g i", g=4),
            cst[:, C_TRI:C_TRI + P].unsqueeze(1).broadcast_to([P, 4, P])).then_inc(turn_free, 1)
        for c in range(KD):
            turned_low(h_low[:, c, :], h_high[:, c, :], gcol[:, 0, c:c + 1])
        dve.wait_ge(band_vec_loaded, 32)
        dve.tensor_copy(relb_wide[:, :, :], relb[:, :].unsqueeze(2).broadcast_to([32, HH, P]))\
           .then_inc(relb_wide_done, 1)

        for t in range(NT):
            dve.wait_ge(in_out, t + 1)
            dve.tensor_copy(misc[:, t, 0:192], G[t][:, 0:192])
            dve.tensor_copy(misc[:, t, 192:256], G[t][:, 128:192])
            dve.tensor_scalar(w_idx[:, t, :], G[t][:, 192:200], IDX_SCALE, None, ALU.mult).then_inc(misc_copied, 1)
        dve.wait_ge(misc_copied, NT)
        for t in range(NT):
            last = dve.tensor_tensor_reduce(sc[:, 0, t * P:(t + 1) * P], misc[:, t, 0:P], misc[:, t, 0:P],
                                            1.0, 0.0, ALU.mult, ALU.add, ss[:, t:t + 1])
        step(last)
        dve.tensor_scalar(msq[:, :], ss[:, :], 1.0 / P, EPS, ALU.mult, ALU.add).then_inc(ck_mean, 1)
        dve.wait_ge(act_step, 1)
        step(dve.reciprocal(rstd[:, :], rms[:, :]))
        for t in range(NT):
            last = dve.tensor_scalar(misc[:, t, 0:P], misc[:, t, 0:P], rstd[:, t:t + 1], None, ALU.mult)
        last.then_inc(ck_root, 1)
        for h in range(4):
            bias_row(h)
        src = turned_chunk()
        dve.tensor_scalar(ckvT[:, :], src[:, :], kvg[:, 0:1], None, ALU.mult).then_inc(turn_free, 1)
        src = turned_chunk()
        dve.tensor_copy(kiT[:, :], src[:, :]).then_inc(turn_free, 1)
        for h in range(4, HH):
            bias_row(h)
        unit = 0
        for qt in range(1, NT):
            k = (qt + 1) * P
            for h in range(HH):
                dve.wait_ge(ix_relu, unit + 1)
                w = w_idx[:, qt, h:h + 1]
                if h == 0:
                    last = dve.tensor_scalar(idx[:, qt, 0:k], sc[:, unit % 2, 0:k], w, None, ALU.mult)
                else:
                    dve.wait_ge(ix_added, unit)
                    last = dve.scalar_tensor_tensor(out=idx[:, qt, 0:k], in0=sc[:, unit % 2, 0:k], scalar=w,
                                                    in1=idx[:, qt, 0:k], op0=ALU.mult, op1=ALU.add)
                last.then_inc(ix_added, 1)
                unit += 1
        causal = cst[:, C_CAUSAL + 3 * P:C_CAUSAL + 4 * P]
        dve.tensor_copy(idx[:, 0, 0:P], causal)
        dve.wait_ge(ix_added, unit)
        for qt in range(1, NT):
            k = (qt + 1) * P
            step(add(idx[:, qt, qt * P:k], idx[:, qt, qt * P:k], causal))
            for _ in range(TOPK // 8):
                step(dve.max(max8[:, :], idx[:, qt, 0:k]))
                step(dve.match_replace(idx[:, qt, 0:k], max8[:, :], idx[:, qt, 0:k], TAKEN))
            step(dve.tensor_scalar(idx[:, qt, 0:k], idx[:, qt, 0:k], -2.0e38, NEG, ALU.is_ge, ALU.mult))
        dve.wait_ge(in_evac, 12)
        dve.wait_ge(ln_loaded, 32)
        step(dve.tensor_scalar(ln_mean[:, :], ln_sum[:, :], 1.0 / HALF, None, ALU.mult))
        step(sub(vtok[:, :, :], vtok[:, :, :], ln_mean[:, :].unsqueeze(2).broadcast_to([P, NT, HALF])))
        for t in range(NT):
            step(dve.tensor_tensor_reduce(sc[:, t % 2, :], vtok[:, t, :], vtok[:, t, :],
                                          1.0, 0.0, ALU.mult, ALU.add, ss[:, t:t + 1]))
        dve.tensor_scalar(msq[:, :], ss[:, :], 1.0 / HALF, EPS, ALU.mult, ALU.add).then_inc(ln_var, 1)
        dve.wait_ge(ln_root, 1)
        step(dve.reciprocal(rstd[:, :], rms[:, :]))
        for t in range(NT):
            last = dve.scalar_tensor_tensor(out=vtok[:, t, :], in0=vtok[:, t, :], scalar=rstd[:, t:t + 1],
                                            in1=lng[:, :], op0=ALU.mult, op1=ALU.mult)
        step(last)
        for t in range(NT):
            add(vtok[:, t, :], vtok[:, t, :], lnb[:, :]).then_inc(ln_done, 1)
        phase_end(1)

        dve.wait_ge(bs_loaded, 16)
        for g in range(4):
            dve.wait_ge(gm_out, g + 1)
            add(sc[:, 0, :].rearrange("p (c i) -> p c i", c=NT), G[g][:, :].rearrange("p (c i) -> p c i", c=NT),
                bs_b[:, g, :].unsqueeze(1).broadcast_to([P, NT, P])).then_inc(gm_free, 1)
            dve.wait_ge(gm_free, g + 1)
            step(mul(uT[:, g, :], sc[:, 0, :], uT[:, g, :]))

        def attend(base, tile0, sc_, read, mask, out, deep=2, between=None, plan=()):
            def tile_end(t):
                dve.wait_ge(at_out, tile0 + t + 1)
                step(dve.reciprocal(rinv[:, HH * t:HH * t + HH], rsum[:, HH * t:HH * t + HH]))
                mul(out[:, t, :].rearrange("p (h d) -> p h d", h=HH),
                    G[t % 2][:, :].rearrange("p (h d) -> p h d", h=HH),
                    rinv[:, HH * t:HH * t + HH].unsqueeze(2).broadcast_to([P, HH, DH])).then_inc(at_done, 1)

            def unit(u):
                t, h = divmod(u, HH)
                k = (t + 1) * P
                dve.wait_ge(at_scores, base + u + 1)
                if u >= 3:
                    dve.wait_ge(at_turned, base + u - 2)
                read(sc_[:, u % 3, 0:k], S3[u % deep][:, 0:k], t, h, k).then_inc(at_read, 1)
                dve.wait_ge(at_read, base + u + 1)
                step(dve.tensor_tensor_reduce(sc_[:, u % 3, 0:k], sc_[:, u % 3, 0:k], mask(t, k), 1.0, TAKEN,
                                              ALU.add, ALU.max, mx[:, u:u + 1]))
                dve.tensor_scalar(nmx[:, u:u + 1], mx[:, u:u + 1], -1.0, None, ALU.mult).then_inc(at_max, 1)
                if h == 1 and t:
                    tile_end(t - 1)

            u = 0
            for i, after in enumerate(plan):
                for _ in range(after):
                    unit(u)
                    u += 1
                between(i)
            while u < NT * HH:
                unit(u)
                u += 1
            tile_end(NT - 1)

        def read_biased(dst, psum, t, h, k):
            return dve.scalar_tensor_tensor(out=dst, in0=psum, scalar=SCALE, in1=toep[:, h, T - k:T],
                                            op0=ALU.mult, op1=ALU.add)

        dve.wait_ge(toep_loaded, 16 * HH)
        attend(0, 0, sc, read_biased, lambda t, k: idx[:, t, 0:k], o_tok, 2)
        dve.wait_ge(in_out, 36)
        step(dve.tensor_copy(h_high[:, 4:8, :], uT[:, :, :]))
        sub(h_low[:, 4:8, :], uT[:, :, :], h_high[:, 4:8, :].bitcast(F32)).then_inc(g_done, 1)
        for m in range(4):
            turned_low(h_low[:, m, :], h_high[:, m, :])
        phase_end(2)

        for b in range(4):
            for m in range(4):
                c = 4 * (b // 2) + m
                dve.wait_ge(pj_out, 4 * b + m + 1)
                g = gates[:, c if b % 2 == 0 else KD + c, :]
                mul(g, G[m][:, :], g).then_inc(pj_free, 1)
                if b % 2:
                    dve.wait_ge(pj_free, 4 * b + m + 1)
                    add(gates[:, c, :], gates[:, c, :], g).then_inc(pj_sum, 1)
                    dve.wait_ge(pj_high, c + 1)
                    sub(merged_low[:, c, :], gates[:, c, :], merged_high[:, c, :].bitcast(F32)).then_inc(pj_low, 1)
        phase_mark()

        def onto_x(out, free, r, wide=None):
            for half in range(2):
                for t in range(NT):
                    dve.wait_ge(out, 4 * half + t + 1)
                    x = X[:, t, 512 * half:512 * half + 512]
                    add(x, G[t][:, :], x).then_inc(free, 1)
                    if half:
                        norm_tile(NT * r + t, t, xn, wide)

        dve.wait_ge(x_again, 16)
        dve.wait_ge(gw_loaded, 16)
        onto_x(wo_out, wo_free, 1, g_wide)
        phase_end(4)

        dve.wait_ge(rt_high_done, 1)
        sub(rt_split[:, :, 36:72], rt_raw[:, :, :], rt_split[:, :, 0:36].bitcast(F32)).then_inc(rt_low_done, 1)
        turned_norm(None)
        for t in range(NT):
            dve.wait_ge(rt_out, t + 1)
            last = add(logit[:, t, :], G[t][:, 0:36], rt_bias[:, :])
        step(last)
        for t in range(NT):
            last = add(logit[:, t, :], G[t][:, 36:72], logit[:, t, :])
        step(last)

        def row(i):
            return rv[:, i, :]

        def wide(i, n):
            return rv[:, i, :].unsqueeze(2).broadcast_to([P, NT, n])

        def reduce(out, x, op):
            return dve.tensor_reduce(out=out, in_=x, axis=AXX, op=op)

        def first_max(dst, x, n, i):
            step(reduce(row(i), x, ALU.max))
            step(dve.tensor_tensor(out=dst, in0=x, in1=wide(i, n), op=ALU.is_equal))
            step(mul(dst, dst, cst[:, C_RANK:C_RANK + n].unsqueeze(1).broadcast_to([P, NT, n])))
            step(reduce(row(11), dst, ALU.max))
            step(dve.tensor_tensor(out=dst, in0=dst, in1=wide(11, n), op=ALU.is_equal))

        groups = logit[:, :, 0:NG]
        first_max(goh[:, :, :], groups, NG, 0)
        sub(el[:, :, 0:NG], groups, wide(0, NG)).then_inc(rt_exp_in, 1)
        dve.wait_ge(rt_exp, 1)
        step(reduce(row(1), el[:, :, 0:NG], ALU.add))
        step(dve.reciprocal(row(2), row(1)))
        lg = logit[:, :, NG:36].rearrange("p t (g e) -> p t g e", g=NG)
        r1v = r1[:, :, :].rearrange("p t (g e) -> p t g e", g=NG)
        step(mul(r1v, lg, goh[:, :, :].unsqueeze(3).broadcast_to([P, NT, NG, EPG])))
        step(reduce(el[:, :, :], r1[:, :, :].rearrange("p t (g e) -> p t e g", g=NG), ALU.add))
        first_max(oh[:, 0, :, :], el[:, :, :], EPG, 3)
        step(dve.scalar_tensor_tensor(out=el2[:, :, :], in0=oh[:, 0, :, :], scalar=NEG, in1=el[:, :, :],
                                      op0=ALU.mult, op1=ALU.add))
        first_max(oh[:, 1, :, :], el2[:, :, :], EPG, 4)
        sub(row(5), row(4), row(3)).then_inc(rt_e2_in, 1)
        dve.wait_ge(rt_e2, 1)
        step(dve.tensor_scalar(row(6), row(5), 1.0, None, ALU.add))
        step(dve.reciprocal(row(7), row(6)))
        step(mul(gate_w[:, 0, :], row(7), row(2)))
        step(mul(gate_w[:, 1, :], gate_w[:, 0, :], row(5)))
        for k in range(2):
            pv = pick[:, k, :, :].rearrange("p t (g e) -> p t g e", g=NG)
            step(dve.tensor_copy(pv, goh[:, :, :].unsqueeze(3).broadcast_to([P, NT, NG, EPG])))
            step(mul(pv, pv, oh[:, k, :, :].unsqueeze(2).broadcast_to([P, NT, NG, EPG])))
        add(both[:, :, :], pick[:, 0, :, :], pick[:, 1, :, :]).then_inc(rt_both, 1)
        dve.wait_ge(rt_cum, 1)
        dve.tensor_copy(cum[:, :, :], SB[0][:, 0:NT * NE].rearrange("p (t e) -> p t e", e=NE))
        step(dve.tensor_copy(cnt[:, :], SB[1][:, 0:NE]))
        step(dve.tensor_scalar(ntile[:, :], cnt[:, :], 0.0, None, ALU.is_gt))
        for q in range(1, T // R):
            step(dve.scalar_tensor_tensor(out=ntile[:, :], in0=cnt[:, :], scalar=float(q * R), in1=ntile[:, :],
                                          op0=ALU.is_gt, op1=ALU.add))
        step(dve.tensor_copy(scan[:, 0, :], ntile[:, :]))
        w, cur = 1, 0
        while w < NE:
            dve.tensor_copy(scan[:, 1 - cur, 0:w], scan[:, cur, 0:w])
            step(add(scan[:, 1 - cur, w:NE], scan[:, cur, w:NE], scan[:, cur, 0:NE - w]))
            w, cur = 2 * w, 1 - cur
        ends, starts = scan[:, cur, :], scan[:, 1 - cur, :]
        step(sub(starts, ends, ntile[:, :]))
        begin, cut = rv[:, 0:2, :], rv[:, 3:5, :]
        for k in range(2):
            step(mul(r2[:, :, :], pick[:, k, :, :], cum[:, :, :]))
            step(reduce(posf[:, k, :], r2[:, :, :], ALU.add))
            step(mul(r2[:, :, :], pick[:, k, :, :], starts.unsqueeze(1).broadcast_to([P, NT, NE])))
            step(reduce(rv[:, k, :], r2[:, :, :], ALU.add))
        step(dve.tensor_scalar(cut, posf[:, :, :], float(R), None, ALU.is_ge))
        for q in range(2, T // R):
            step(dve.scalar_tensor_tensor(out=cut, in0=posf[:, :, :], scalar=float(q * R), in1=cut,
                                          op0=ALU.is_ge, op1=ALU.add))
        step(dve.scalar_tensor_tensor(out=posf[:, :, :], in0=posf[:, :, :], scalar=float(SLOTS), in1=begin,
                                      op0=ALU.mult, op1=ALU.add))
        step(dve.scalar_tensor_tensor(out=posf[:, :, :], in0=cut, scalar=float(1 - R * SLOTS), in1=posf[:, :, :],
                                      op0=ALU.mult, op1=ALU.add))
        dve.tensor_copy(pos[:, :], posf[:, :, :].rearrange("p k t -> p (k t)")).then_inc(rt_pos, 1)
        step(dve.tensor_tensor(out=slotf[:, :, :], in0=ends[0:1, :].unsqueeze(1).broadcast_to([1, SLOTS, NE]),
                               in1=cst[0:1, C_SLOT:C_SLOT + SLOTS].unsqueeze(2).broadcast_to([1, SLOTS, NE]),
                               op=ALU.is_le))
        step(reduce(slote[:, :], slotf[:, :, :], ALU.add))
        step(dve.tensor_scalar(slot_expert[:, :], slote[:, :], float(NE - 1), None, ALU.min))
        step(dve.tensor_scalar(slote[:, 0:TRIPS], cst[0:1, C_SLOT:C_SLOT + 2 * TRIPS:2], ends[0:1, NE - 1:NE], None,
                               ALU.is_lt))
        step(reduce(posf[0:1, 0, 0:1], slote[:, 0:TRIPS], ALU.add))
        step(dve.tensor_scalar(posf[0:1, 0, 1:2], posf[0:1, 0, 0:1], -1.0, None, ALU.add))
        dve.tensor_copy(trips[:, :], posf[0:1, 0, 0:2]).then_inc(rt_tables, 1)
        phase_end(5)

        m_scat = [m_scat0, m_scat1]
        m_gath = [m_gath0, m_gath1]

        def rows(j, b):
            dve.wait_ge(m_turned, j + 1)
            dve.tensor_copy(xt[:, b, :, :], TB[b][:, :].rearrange("p (k n) -> p k n", k=KD)).then_inc(m_xt, 1)

        def inner(j, b):
            dve.wait_ge(m_silu, j + 1)
            mul(he[:, :], sg[:, :], G[b][0:R, FE:2 * FE]).then_inc(m_he, 1)

        def out(j, b, i):
            dve.wait_ge(m_down, j + 1)
            if not isinstance(i, int) or i:
                dve.wait_ge(m_scat[b], 16 * i)
            dve.tensor_copy(y_out[:, b, 0:512], G[2][0:R, :])
            dve.tensor_copy(y_out[:, b, 512:1024], G[3][0:R, :]).then_inc(m_y, 1)

        n_trips = dve.value_load(trips[0:1, 0:1], min_val=8, max_val=TRIPS)
        dve.drain().then_inc(m_y, 1)
        rows(0, 0)
        rows(1, 1)
        inner(0, 0)
        rows(2, 0)
        inner(1, 1)
        out(0, 0, 0)
        rows(3, 1)
        inner(2, 0)
        out(1, 1, 0)
        rows(4, 0)
        inner(3, 1)
        out(2, 0, 1)
        with dve.Fori(2, n_trips) as i:
            rows(2 * i + 1, 1)
            inner(2 * i, 0)
            out(2 * i - 1, 1, i - 1)
            rows(2 * i + 2, 0)
            inner(2 * i + 1, 1)
            out(2 * i, 0, i)
        n_less = dve.value_load(trips[0:1, 1:2], min_val=7, max_val=TRIPS - 1)
        out(2 * n_trips - 1, 1, n_less)
        for b in range(2):
            dve.wait_ge(m_scat[b], 16 * n_trips)
            dve.tensor_copy(y_out[:, b, 0:1], G[2][0:R, 0:1])
            dve.wait_ge(m_gath[b], 16 * n_trips + 16)
            dve.tensor_copy(xg[:, b, 0:1], G[2][0:R, 0:1])
        phase_end(6)
        dve.wait_ge(gw1_loaded, 16)

        def combine(t):
            dve.wait_ge(tile_loaded[t], 48)
            step(dve.scalar_tensor_tensor(out=X[:, t, :], in0=y_in[:, 0, t, :], scalar=gate_w[:, 0, t:t + 1],
                                          in1=X[:, t, :], op0=ALU.mult, op1=ALU.add))
            dve.scalar_tensor_tensor(out=X[:, t, :], in0=y_in[:, 1, t, :], scalar=gate_w[:, 1, t:t + 1],
                                     in1=X[:, t, :], op0=ALU.mult, op1=ALU.add).then_inc(y_summed, 1)

        combine(0)
        for i, (second, t) in enumerate(TWO_NORMS):
            if second:
                norm_tile(2 * NT + i, t, xn)
            else:
                if t + 1 < NT:
                    combine(t + 1)
                dve.wait_ge(y_summed, t + 1)
                norm_tile(2 * NT + i, t, X, gw1)
        phase_end(7)
        turned_norm(2)
        phase_mark()
        stored = [dl_stored0, dl_stored1]
        def rotate(v):
            order = min(v % 3, 1)
            dve.wait_ge(dl_evac, 12 * v + 8)
            qv = qk[:, :, :].rearrange("p a (h d) -> p a h d", h=HH)
            x1, x2 = qv[:, :, :, 0:8], qv[:, :, :, 8:16]
            cos = cst[:, C_COS + 64 * order:C_COS + 64 * order + 64].rearrange("p (a f) -> p a f", f=8)\
                .unsqueeze(2).broadcast_to([P, 8, 8, 8])
            sin = cst[:, C_SIN + 64 * order:C_SIN + 64 * order + 64].rearrange("p (a f) -> p a f", f=8)\
                .unsqueeze(2).broadcast_to([P, 8, 8, 8])
            mul(rot[:, 0], x1, cos)
            mul(rot[:, 1], x2, sin)
            mul(rot[:, 2], x2, cos)
            step(mul(rot[:, 3], x1, sin))
            sub(x1, rot[:, 0], rot[:, 1])
            add(x2, rot[:, 2], rot[:, 3]).then_inc(dl_rot, 1)

        rotate(0)
        unit0 = 32
        for v in range(6):
            g = v % 3
            for m in range(8):
                src = turned_chunk()
                dst = dqT[:, m, :] if m < 4 else dkT[:, m - 4, :]
                dve.tensor_copy(dst, src[:, :]).then_inc(turn_free, 1)
            hu = 2 if g == 0 else 4
            w = T // hu
            per_tile = HH // hu
            units = NT * per_tile

            def tile_end(t):
                dve.wait_ge(at_out, NT * (v + 1) + t + 1)
                step(dve.reciprocal(rinv[:, HH * t:HH * t + HH], rsum[:, HH * t:HH * t + HH]))
                if g and v > 1:
                    dve.wait_ge(stored[t % 2], 32 * (v - (v + 2) // 3))
                out = o_st[:, t, :] if g else xn[:, t, HALF * (v // 3):HALF * (v // 3) + HALF]
                mul(out.rearrange("p (h d) -> p h d", h=HH),
                    G[t % 2][:, :].rearrange("p (h d) -> p h d", h=HH),
                    rinv[:, HH * t:HH * t + HH].unsqueeze(2).broadcast_to([P, HH, DH])).then_inc(at_done, 1)

            for u in range(units):
                t = u // per_tile
                if g == 0:
                    m0 = C_CAUSAL + 3 * P if t else C_NONE
                else:
                    m0 = C_CAUSAL + 3 * P if g == 1 else C_CLASS
                dve.wait_ge(at_scores, unit0 + u + 1)
                if u >= 3:
                    dve.wait_ge(at_turned, unit0 + u - 2)
                view = dsc[:, u % 3, :].rearrange("p (e w) -> p e w", e=hu)
                dve.scalar_tensor_tensor(out=view, in0=SB[u % 2][:, :].rearrange("p (e w) -> p e w", e=hu),
                                         scalar=SCALE, in1=cst[:, m0:m0 + w].unsqueeze(1).broadcast_to([P, hu, w]),
                                         op0=ALU.mult, op1=ALU.add).then_inc(at_read, 1)
                dve.wait_ge(at_read, unit0 + u + 1)
                c0 = HH * t + first_head(u % per_tile, hu)
                cols = slice(c0, c0 + 2 * hu - 1, 2)
                step(dve.tensor_reduce(out=mx[:, cols], in_=view, axis=AXX, op=ALU.max))
                dve.tensor_scalar(nmx[:, cols], mx[:, cols], -1.0, None, ALU.mult)\
                   .then_inc(at_max, 1)
                if u % per_tile == 1 and t:
                    tile_end(t - 1)
                if u == units - 3 and v < 5:
                    rotate(v + 1)
            tile_end(NT - 1)
            dve.wait_ge(dl_ln, v + 1)
            add(lse[:, :, :], lse[:, :, :], mx[:, :].rearrange("p (t h) -> p t h", h=HH)).then_inc(dl_lse, 1)
            unit0 += units
        phase_end(9)
        dve.wait_ge(mg_lse_loaded, 48)
        step(dve.tensor_tensor(out=lmax[:, :, :], in0=lse3[:, 0], in1=lse3[:, 1], op=ALU.max))
        step(dve.tensor_tensor(out=lmax[:, :, :], in0=lmax[:, :, :], in1=lse3[:, 2], op=ALU.max))
        for g in range(3):
            last = sub(lse3[:, g], lse3[:, g], lmax[:, :, :])
        last.then_inc(mg_exp_in, 1)
        dve.wait_ge(mg_exp, 1)
        step(add(lmax[:, :, :], lse3[:, 0], lse3[:, 1]))
        step(add(lmax[:, :, :], lmax[:, :, :], lse3[:, 2]))
        step(dve.reciprocal(lmax[:, :, :], lmax[:, :, :]))
        for g in range(3):
            last = mul(lse3[:, g], lse3[:, g], lmax[:, :, :])
        last.then_inc(mg_weights, 1)
        dve.wait_ge(mg_weights, 1)
        for t in range(NT):
            dve.wait_ge(tile_loaded[t], 64)
            parts = [xn[:, t, :], og[:, t, 0, :], og[:, t, 1, :]]
            for g in range(2):
                o = parts[g].rearrange("p (h d) -> p h d", h=16)
                last = mul(o, o, lse3[:, g, t, :].unsqueeze(2).broadcast_to([P, 16, DH]))
            step(last)
            step(add(parts[0], parts[0], parts[1]))
            dve.wait_ge(mg_third, t + 1)
            add(parts[0], parts[0], parts[2]).then_inc(mg_done, 1)
        for c in range(KD):
            turned_low(h_low[:, c, :], h_high[:, c, :])
        onto_x(ao_out, ao_free, 4)
        phase_end(10)

        def swiglu(l):
            for r, chunks in enumerate(FF_ROUNDS):
                f0 = 22 * l + FF_CHUNK[r]
                with dve.Fori(0, chunks // 2) as i:
                    for c in range(2):
                        f = f0 + c + 2 * i
                        dve.wait_ge(ff_silu, f + 1)
                        mul(gu[:, c, :], silu[:, c, :], G[2 * c + 1][:, :]).then_inc(ff_mul, 1)
                        dve.wait_ge(ff_high, f + 1)
                        sub(act_low[:, bass.ds(c + 2 * i, 1), :], gu[:, c, :].rearrange("p (o n) -> p o n", o=1),
                            act_high[:, bass.ds(c + 2 * i, 1), :].bitcast(F32)).then_inc(ff_low, 1)
                for half in range(2):
                    outs = bank[4:8] if half == 0 else bank[0:4]
                    for t in range(NT):
                        dve.wait_ge(ff_down_out, (3 * l + r) * 8 + 4 * half + t + 1)
                        x = X[:, t, 512 * half:512 * half + 512]
                        add(x, outs[t][:, :], x).then_inc(ff_down_free, 1)
                        if r == 2 and half:
                            if l:
                                dve.wait_ge(gw2_loaded, 16)
                            norm_tile(NT * (5 + 2 * l) + t, t, xn, gw2 if l else None)

        turned_norm(3)
        swiglu(0)
        phase_end(11)
        dve.wait_ge(fo_high, 1)
        sub(fw_split[:, :, 16:32], fw_raw[:, :, :], fw_split[:, :, 0:16].bitcast(F32)).then_inc(fo_lowd, 1)
        turned_norm(4)
        dve.wait_ge(fo_logit, 1)
        z = SB[0][:, 0:128].rearrange("p (t h) -> p t h", h=32)
        step(add(fz[:, :, :], z[:, :, 0:16], fb[:, :].unsqueeze(1).broadcast_to([P, NT, 16])))
        step(add(fz[:, :, :], z[:, :, 16:32], fz[:, :, :]))
        dve.scalar_tensor_tensor(out=fm[:, :, :], in0=fz[:, :, :], scalar=-1.0, in1=fz[:, :, :],
                                 op0=ALU.mult, op1=ALU.min).then_inc(fo_e_in, 1)
        dve.wait_ge(fo_l, 1)
        dve.scalar_tensor_tensor(out=fz[:, :, :], in0=fz[:, :, :], scalar=0.0, in1=fe[:, :, :],
                                 op0=ALU.min, op1=ALU.subtract).then_inc(fo_f, 1)
        dve.wait_ge(fo_c, 1)
        dve.tensor_copy(c_tok[:, :, :], SB[1][:, 0:64].rearrange("p (t h) -> p t h", h=16)).then_inc(fo_ct, 1)
        dve.wait_ge(fo_sel, 1)
        step(dve.tensor_copy(cT[:, :], SB[0][0:16, :]))
        def add_fox(i):
            b, t = divmod(i, NT)
            dve.wait_ge(bo_out, i + 1)
            x = X[:, t, 512 * (b % 2):512 * (b % 2) + 512]
            if i >= 8:
                dve.wait_ge(bo_free, i - 7)
            add(x, G[2 + i % 2][:, :], x).then_inc(bo_free, 1)

        for hf in range(2):
            def select(h):
                n = HH * hf + h
                if n >= 2:
                    dve.wait_ge(fo_ncb, n - 1)
                dve.tensor_copy(sel16[:, h % 2, :], cst[0:16, C_IDENT + n:C_IDENT + n + 1].broadcast_to([16, P]))\
                   .then_inc(fo_nc, 1)

            select(0)
            select(1)
            for h in range(HH):
                dve.wait_ge(fo_ncb, HH * hf + h + 1)
                dve.tensor_scalar(ncb[:, h, :], SB[h % 2][:, :], -1.0, None, ALU.mult).then_inc(fo_nc, 1)
                if h + 2 < HH:
                    select(h + 2)
            dve.wait_ge(fo_nc, 2 * HH * (hf + 1))

            def read_decayed(dst, psum, t, h, k, hf=hf):
                n = HH * hf + h
                return dve.scalar_tensor_tensor(out=dst, in0=ncb[:, h, 0:k], scalar=c_tok[:, t, n:n + 1],
                                                in1=psum, op0=ALU.add, op1=ALU.add)

            attend(96 + 32 * hf, 28 + NT * hf, fsc, read_decayed,
                   lambda t, k: cst[:, C_CAUSAL + T - k:C_CAUSAL + T], fo_tok, 2,
                   add_fox, FOX_UNITS[1] if hf else ())
            for m in range(4):
                turned_low(o_low[:, 4 * hf + m, :], o_high[:, 4 * hf + m, :])
        phase_end(12)
        for i in range(8, 16):
            add_fox(i)
            if i >= 12:
                norm_tile(6 * NT + i - 12, i - 12, xn)
        phase_end(13)
        turned_norm(5)
        swiglu(1)
        phase_end(14)

    @block.gpsimd
    def _(pool):
        def split_low(n, slot):
            pool.wait_ge(high_done, n + 1)
            pool.tensor_tensor(out=w_low[:, slot, :], in0=raw[:, slot, :], in1=w_high[:, slot, :].bitcast(F32),
                               op=ALU.subtract).then_inc(low_done, 1)

        def split_pairs(n0, pairs):
            with pool.Fori(0, pairs) as i:
                for c in range(2):
                    split_low(n0 + c + 2 * i, (n0 + c) % 2)

        split_pairs(0, 13)
        split_low(B_DIL + 1, (B_DIL + 1) % 2)
        pool.wait_ge(phase_done, 3 * 4)
        pool.memset(xg[:, :, :], 0.0).then_inc(m_idx, 1)
        pool.memset(empty[:, :], OOB).then_inc(rt_empty, 1)
        pool.wait_ge(empty_stored, 16)
        pool.wait_ge(rt_pos, 1)
        pool.wait_ge(vec_loaded, 16 * 8)
        for c in range(2 * NT):
            pool.indirect_dma_start(out=d_list, out_offset=bass.IndirectOffsetOnAxis(ap=pos[:, c:c + 1], axis=0),
                                    in_=ids[:, c:c + 1], in_offset=None).then_inc(list_stored, 16)
        m_gath = [m_gath0, m_gath1]
        m_scat = [m_scat0, m_scat1]
        pool.wait_ge(phase_done, 3 * 5)
        pool.wait_ge(list_loaded, 16)
        pool.wait_ge(rows_stored, 32)

        def column(j):
            return slot_rows[:, j:j + 1] if isinstance(j, int) else slot_rows[:, bass.ds(j, 1)]

        def gather(j, b, copies):
            pool.tensor_copy(gather_rows[:, b:b + 1], column(j)).then_inc(m_idx, 1)
            pool.wait_ge(m_idx, copies)
            pool.indirect_dma_start(out=xg[:, b, :], out_offset=None, in_=d_rows,
                                    in_offset=bass.IndirectOffsetOnAxis(ap=gather_rows[:, b:b + 1], axis=0),
                                    bounds_check=2 * T - 1 + j, oob_is_err=False).then_inc(m_gath[b], 16)

        def scatter(j, b, copies):
            pool.tensor_copy(scatter_rows[:, b:b + 1], column(j)).then_inc(m_idx, 1)
            pool.wait_ge(m_idx, copies)
            pool.indirect_dma_start(out=d_y, out_offset=bass.IndirectOffsetOnAxis(ap=scatter_rows[:, b:b + 1], axis=0),
                                    in_=y_out[:, b, :], in_offset=None,
                                    bounds_check=2 * T - 1 + j, oob_is_err=False).then_inc(m_scat[b], 16)

        n_trips = pool.value_load(trips[0:1, 0:1], min_val=8, max_val=TRIPS)
        def step(j, b, first=False):
            pool.wait_ge(m_turned, j + 1)
            gather(j + 2, b, 2 * j + (4 if first else 3))
            if not first:
                pool.wait_ge(m_y, j + 1)
                scatter(j - 1, 1 - b, 2 * j + 4)

        gather(0, 0, 2)
        gather(1, 1, 3)
        step(0, 0, True)
        step(1, 1)
        with pool.Fori(1, n_trips) as i:
            step(2 * i, 0)
            step(2 * i + 1, 1)
        pool.wait_ge(m_y, 2 * n_trips + 1)
        scatter(2 * n_trips - 1, 1, 4 * n_trips + 3)
        split_pairs(B_DIL + 2, 3)
        for v in range(6):
            hf, g = divmod(v, 3)
            if v < 5:
                split_pairs(B_DIL + 8 + 6 * v, 3)
            for t in range(NT if g else 0):
                pool.wait_ge(at_done, NT * (v + 1) + t + 1)
                pool.dma_start(d_o[g - 1, t:T:NT, HALF * hf:HALF * hf + HALF], o_st[:, t, :])\
                    .then_inc([dl_stored0, dl_stored1][t % 2], 16)
            heads = slice(HH * hf, HH * hf + HH)
            pool.wait_ge(dl_lse, v + 1)
            dst = d_lse[g].rearrange("(t p) h -> p t h" if g == 0 else "(p t) h -> p t h", t=NT)
            pool.dma_start(dst[:, :, heads], lse[:, :, :]).then_inc(dl_lse_stored, 16)
        pool.wait_ge(mg_weights, 1)
        for t in range(NT):
            pool.wait_ge(tile_loaded[t], 64)
            o = og[:, t, 1, :].rearrange("p (h d) -> p h d", h=16)
            pool.tensor_tensor(out=o, in0=o, in1=lse3[:, 2, t, :].unsqueeze(2).broadcast_to([P, 16, DH]),
                               op=ALU.mult).then_inc(mg_third, 1)
        split_pairs(B_AOUT + 2, (N_BLOCKS - B_AOUT - 2) // 2)

    ctx.close()


_INPUTS = """x w_in kv_norm_g w_uk w_uv rel_bias ln_v_g ln_v_b w_spatial b_spatial w_proj_a w_proj_b w_out
    norm1_g norm2_g router_group_w router_group_b router_expert_w router_expert_b w_gate w_up w_down
    final_norm_g a_norm_2 a_w_in_2 a_w_out_2 b_norm_2 b_w_in_2 b_f_2 b_w_out_2 ffn_norm_2 ffn_w_gu_2
    ffn_w_down_2 final_norm_2""".split()


def _tables():
    import numpy as np

    f = np.float32
    p, q = np.arange(P)[:, None], np.arange(P)[None, :]
    neg = f(NEG)
    tab = np.zeros((P, C_COLS), f)
    tab[:, C_IDENT:C_IDENT + P] = np.eye(P, dtype=f)
    causal = np.where(q <= p, f(0), neg)
    tab[:, C_CAUSAL + 3 * P:C_CAUSAL + 4 * P] = causal
    tab[:, C_PREV:C_PREV + P] = np.where(q >= p, f(0), neg)
    tab[:, C_CLASS:C_CLASS + P] = np.where((q <= p) & (q % 4 == p % 4), f(0), neg)
    tab[:, C_NONE:C_NONE + P] = neg
    tab[:, C_NONE + P:C_NONE + 2 * P] = causal
    tab[:, C_TRI:C_TRI + P] = p <= q
    tab[:, C_TRIS:C_TRIS + P] = p < q
    tab[:, C_ONES:C_ONES + P] = 1
    tab[:, C_RANK:C_RANK + 8] = 8 - np.arange(8)
    tab[:, C_SLOT:C_SLOT + SLOTS] = np.arange(SLOTS)
    freq = f(500000.0) ** (-np.arange(8, dtype=f) * f(2.0) / f(16))
    for order in range(2):
        for tile in range(NT):
            pos = np.arange(P) + P * tile if order == 0 else tile + NT * np.arange(P)
            ang = pos.astype(f)[:, None] * freq[None, :]
            for kind in range(2):
                c = 64 * order + 8 * (NT * kind + tile)
                tab[:, C_COS + c:C_COS + c + 8] = np.cos(ang)
                tab[:, C_SIN + c:C_SIN + c + 8] = np.sin(ang)
    n = np.maximum(T - 1 - np.arange(BAND), 0)
    large = 16 + (np.log(np.maximum(n, 1).astype(f) / 16) / f(np.log(128 / 16)) * 16).astype(np.int32)
    bucket = np.where(n < 16, n, np.minimum(large, 31))
    buckets = (np.arange(32)[:, None] == bucket[None, :]).astype(f)
    pairs = (np.arange(2 * T).reshape(2 * NT, P).T).astype(np.int32)
    return {"table": tab, "buckets": buckets, "pairs": np.ascontiguousarray(pairs)}


def kernel(**inputs):
    import numpy as np
    import concourse.bacc as bacc
    from concourse.bass_utils import run_bass_kernel_spmd

    nc = bacc.Bacc("TRN2", target_bir_lowering=False, num_devices=1)
    arrays, a = {}, {}
    for name, value in [(n, inputs[n]) for n in _INPUTS] + list(_tables().items()):
        value = np.ascontiguousarray(value)
        arrays["in_" + name] = value
        a[name] = nc.dram_tensor("in_" + name, value.shape, mybir.dt.from_np(value.dtype),
                                          kind="ExternalInput").ap()
    a["out"] = nc.dram_tensor("out", (1, T, D), F32, kind="ExternalOutput").ap()
    two_blocks_kernel(nc, a)
    r = run_bass_kernel_spmd(nc, [arrays], core_ids=[0])
    return r.results[0]["out"]
```
